# Optimizing a Trainium2 kernel written in Bass

```python
import jax, jax.numpy as jnp
from jax import lax
import numpy as np

'''Hybrid streaming-encoder trunk, YOCO-style dual path.
Layers 0 .. DEPTH//2-1 (mixer A): pre-RMSNorm -> gated linear attention (GLA, chunked, low-rank
forget gate) -> residual; pre-RMSNorm -> SwiGLU FFN -> residual.
After the last A layer (including its FFN) one shared MLA key/value set (compressed latent,
decoupled rotary key, per-head K and V) is built from the residual stream.
Layers DEPTH//2 .. DEPTH-1 (mixer B): pre-RMSNorm -> multi-head latent attention with its own
low-rank queries attending to the shared K/V under the block-causal chunk mask -> residual;
pre-RMSNorm -> SwiGLU FFN -> residual.
Inputs: x (BATCH, SEQ, D_MODEL) float32, positions (BATCH, SEQ) int32 (absolute stream positions).
Output: (BATCH, SEQ, D_MODEL).
'''

D_MODEL = 1024
BATCH = 1
SEQ = 512
DEPTH = 2

CHUNK = 64
N_A_LAYERS = DEPTH // 2
N_B_LAYERS = DEPTH - N_A_LAYERS
EPS = 1e-6

GLA_HEADS = 4
GLA_DK = D_MODEL // 2
GLA_DV = D_MODEL
GLA_HK = GLA_DK // GLA_HEADS
GLA_HV = GLA_DV // GLA_HEADS
GLA_GATE_RANK = 16
GLA_TAU = 16.0
GLA_IN = 2 * GLA_DK + 2 * GLA_DV + GLA_GATE_RANK

MLA_HEADS = 16
MLA_NOPE = 64
MLA_ROPE = 32
MLA_QK = MLA_NOPE + MLA_ROPE
MLA_V = 64
MLA_Q_RANK = 384
MLA_KV_RANK = 256
ROPE_THETA = 10000.0
Q_BLOCK = 128

FFN_HIDDEN = -(-8 * D_MODEL // (3 * 256)) * 256

kernel_name = 'yoco_gla_mla_hybrid'

def rms_norm(x, g):
    xf = x.astype(jnp.float32)
    y = xf * lax.rsqrt(jnp.mean(xf * xf, axis=-1, keepdims=True) + EPS)
    return (y * g.astype(jnp.float32)).astype(x.dtype)

def rope(x, positions):
    half = x.shape[-1] // 2
    inv_freq = ROPE_THETA ** (-jnp.arange(half, dtype=jnp.float32) / half)
    ang = positions.astype(jnp.float32)[:, None, :, None] * inv_freq
    cos, sin = jnp.cos(ang), jnp.sin(ang)
    xf = x.astype(jnp.float32)
    x1, x2 = xf[..., :half], xf[..., half:]
    return jnp.concatenate([x1 * cos - x2 * sin, x1 * sin + x2 * cos], axis=-1).astype(x.dtype)

def gla_mixer(h, w_in, w_gate_up, b_gate, out_norm, w_out):
    B, S, _ = h.shape
    N = S // CHUNK
    f32 = jnp.float32
    proj = h @ w_in
    q = proj[..., :GLA_DK]
    k = proj[..., GLA_DK:2 * GLA_DK]
    v = proj[..., 2 * GLA_DK:2 * GLA_DK + GLA_DV]
    r = proj[..., 2 * GLA_DK + GLA_DV:2 * GLA_DK + 2 * GLA_DV]
    gl = proj[..., 2 * GLA_DK + 2 * GLA_DV:]
    log_a = jax.nn.log_sigmoid((gl @ w_gate_up + b_gate).astype(f32)) / GLA_TAU

    def chunks(t, d):
        return t.astype(f32).reshape(B, N, CHUNK, GLA_HEADS, d).transpose(0, 3, 1, 2, 4)

    qc = chunks(q, GLA_HK) * (GLA_HK ** -0.5)
    kc = chunks(k, GLA_HK)
    vc = chunks(v, GLA_HV)
    b = jnp.cumsum(chunks(log_a, GLA_HK), axis=3)
    b_last = b[:, :, :, -1:, :]
    q_dec = qc * jnp.exp(b)
    k_inv = kc * jnp.exp(-b)
    k_end = kc * jnp.exp(b_last - b)
    causal = jnp.tril(jnp.ones((CHUNK, CHUNK), dtype=bool))
    attn = jnp.where(causal, jnp.einsum('bhnik,bhnjk->bhnij', q_dec, k_inv), 0.0)
    o_intra = jnp.einsum('bhnij,bhnjv->bhniv', attn, vc)
    kv_chunk = jnp.einsum('bhnjk,bhnjv->nbhkv', k_end, vc)
    decay = jnp.exp(b_last[:, :, :, 0, :]).transpose(2, 0, 1, 3)

    def step(state, inp):
        dec, kv = inp
        return dec[..., None] * state + kv, state

    _, s_prev = lax.scan(step, jnp.zeros((B, GLA_HEADS, GLA_HK, GLA_HV), f32), (decay, kv_chunk))
    o_inter = jnp.einsum('bhnik,nbhkv->bhniv', q_dec, s_prev)
    o = (o_intra + o_inter).transpose(0, 2, 3, 1, 4).reshape(B, S, GLA_HEADS, GLA_HV)
    o = rms_norm(o, out_norm).reshape(B, S, GLA_DV) * jax.nn.silu(r.astype(f32))
    return o.astype(h.dtype) @ w_out

def mla_shared_kv(h, positions, kv_norm, w_down, latent_norm, w_up, k_norm):
    B, S, _ = h.shape
    d = rms_norm(h, kv_norm) @ w_down
    c_kv = rms_norm(d[..., :MLA_KV_RANK], latent_norm)
    k_rope = d[..., MLA_KV_RANK:]
    kv = (c_kv @ w_up).reshape(B, S, MLA_HEADS, MLA_NOPE + MLA_V)
    k_nope, v = kv[..., :MLA_NOPE], kv[..., MLA_NOPE:]
    k = jnp.concatenate([k_nope, jnp.broadcast_to(k_rope[:, :, None, :], (B, S, MLA_HEADS, MLA_ROPE))], axis=-1)
    k = rms_norm(k, k_norm).transpose(0, 2, 1, 3)
    k = jnp.concatenate([k[..., :MLA_NOPE], rope(k[..., MLA_NOPE:], positions)], axis=-1)
    return k, v.transpose(0, 2, 1, 3)

def mla_mixer(h, positions, k, v, w_dq, q_latent_norm, w_uq, q_norm, w_out):
    B, S, _ = h.shape
    f32 = jnp.float32
    c_q = rms_norm(h @ w_dq, q_latent_norm)
    q = (c_q @ w_uq).reshape(B, S, MLA_HEADS, MLA_QK)
    q = rms_norm(q, q_norm).transpose(0, 2, 1, 3)
    q = jnp.concatenate([q[..., :MLA_NOPE], rope(q[..., MLA_NOPE:], positions)], axis=-1)
    nb = S // Q_BLOCK
    q_blocks = q.astype(f32).reshape(B, MLA_HEADS, nb, Q_BLOCK, MLA_QK).transpose(2, 0, 1, 3, 4)
    kf, vf = k.astype(f32), v.astype(f32)
    key_chunk = jnp.arange(S) // CHUNK
    scale = MLA_QK ** -0.5

    def attend(args):
        qb, blk = args
        q_chunk = (blk * Q_BLOCK + jnp.arange(Q_BLOCK)) // CHUNK
        s = jnp.einsum('bhqd,bhkd->bhqk', qb, kf) * scale
        s = jnp.where(key_chunk[None, :] <= q_chunk[:, None], s, -jnp.inf)
        p = jax.nn.softmax(s, axis=-1)
        return jnp.einsum('bhqk,bhkv->bhqv', p, vf)

    o = lax.map(attend, (q_blocks, jnp.arange(nb)))
    o = o.transpose(1, 0, 3, 2, 4).reshape(B, S, MLA_HEADS * MLA_V)
    return o.astype(h.dtype) @ w_out

def swiglu(h, w_in, w_out):
    gu = h @ w_in
    return (jax.nn.silu(gu[..., :FFN_HIDDEN]) * gu[..., FFN_HIDDEN:]) @ w_out

def setup_inputs(seed: int = 0) -> dict:
    key = jax.random.key(seed)
    ks = jax.random.split(key, 24)
    f32 = jnp.float32
    na, nb = N_A_LAYERS, N_B_LAYERS
    out_scale = (2.0 * DEPTH) ** -0.5

    def w(k, shape, fan_in, scale=1.0):
        return jax.random.normal(k, shape, f32) * (scale * fan_in ** -0.5)

    def gain(k, shape):
        return 1.0 + 0.02 * jax.random.normal(k, shape, f32)

    x = jax.random.normal(ks[0], (BATCH, SEQ, D_MODEL), f32)
    start = jax.random.randint(ks[1], (BATCH, 1), 0, 4096, dtype=jnp.int32)
    positions = start + jnp.arange(SEQ, dtype=jnp.int32)[None, :]
    return {
        'x': x,
        'positions': positions,
        'a_norm': gain(ks[2], (na, D_MODEL)),
        'a_w_in': w(ks[3], (na, D_MODEL, GLA_IN), D_MODEL),
        'a_w_gate_up': w(ks[4], (na, GLA_GATE_RANK, GLA_DK), GLA_GATE_RANK),
        'a_b_gate': 0.1 * jax.random.normal(ks[5], (na, GLA_DK), f32),
        'a_out_norm': gain(ks[6], (na, GLA_HV)),
        'a_w_out': w(ks[7], (na, GLA_DV, D_MODEL), GLA_DV, out_scale),
        'b_norm': gain(ks[8], (nb, D_MODEL)),
        'b_w_dq': w(ks[9], (nb, D_MODEL, MLA_Q_RANK), D_MODEL),
        'b_q_latent_norm': gain(ks[10], (nb, MLA_Q_RANK)),
        'b_w_uq': w(ks[11], (nb, MLA_Q_RANK, MLA_HEADS * MLA_QK), MLA_Q_RANK),
        'b_q_norm': gain(ks[12], (nb, MLA_QK)),
        'b_w_out': w(ks[13], (nb, MLA_HEADS * MLA_V, D_MODEL), MLA_HEADS * MLA_V, out_scale),
        'kv_norm': gain(ks[14], (D_MODEL,)),
        'kv_w_down': w(ks[15], (D_MODEL, MLA_KV_RANK + MLA_ROPE), D_MODEL),
        'kv_latent_norm': gain(ks[16], (MLA_KV_RANK,)),
        'kv_w_up': w(ks[17], (MLA_KV_RANK, MLA_HEADS * (MLA_NOPE + MLA_V)), MLA_KV_RANK),
        'k_norm': gain(ks[18], (MLA_QK,)),
        'f_norm': gain(ks[19], (DEPTH, D_MODEL)),
        'f_w_in': w(ks[20], (DEPTH, D_MODEL, 2 * FFN_HIDDEN), D_MODEL),
        'f_w_out': w(ks[21], (DEPTH, FFN_HIDDEN, D_MODEL), FFN_HIDDEN, out_scale),
    }

def reference(x, positions, a_norm, a_w_in, a_w_gate_up, a_b_gate, a_out_norm, a_w_out,
              b_norm, b_w_dq, b_q_latent_norm, b_w_uq, b_q_norm, b_w_out,
              kv_norm, kv_w_down, kv_latent_norm, kv_w_up, k_norm,
              f_norm, f_w_in, f_w_out):
    k_sh, v_sh = None, None
    for layer in range(DEPTH):
        if layer < N_A_LAYERS:
            i = layer
            x = x + gla_mixer(rms_norm(x, a_norm[i]), a_w_in[i], a_w_gate_up[i], a_b_gate[i],
                              a_out_norm[i], a_w_out[i])
        else:
            j = layer - N_A_LAYERS
            x = x + mla_mixer(rms_norm(x, b_norm[j]), positions, k_sh, v_sh, b_w_dq[j],
                              b_q_latent_norm[j], b_w_uq[j], b_q_norm[j], b_w_out[j])
        x = x + swiglu(rms_norm(x, f_norm[layer]), f_w_in[layer], f_w_out[layer])
        if layer == N_A_LAYERS - 1 and N_B_LAYERS > 0:
            k_sh, v_sh = mla_shared_kv(x, positions, kv_norm, kv_w_down, kv_latent_norm, kv_w_up, k_norm)
    return x


_drawn_inputs = setup_inputs


def setup_inputs(seed=0):
    import zlib

    import numpy as np

    out = dict(_drawn_inputs(seed))
    spreads = {}
    factors = {'a_norm': 4.362,
     'a_b_gate': 4.104,
     'a_out_norm': 8.0,
     'b_norm': 8.0,
     'b_q_latent_norm': 8.0,
     'b_q_norm': 8.0,
     'kv_norm': 8.0,
     'kv_latent_norm': 8.0,
     'k_norm': 8.0,
     'f_norm': 5.181}
    for name, (base, spread) in spreads.items():
        noise = np.random.default_rng([zlib.crc32(name.encode()), seed]).standard_normal(out[name].shape)
        drawn = base * np.exp(spread * noise) if base else spread * noise
        out[name] = __import__('jax').numpy.asarray(drawn.astype(out[name].dtype))
    for name, factor in factors.items():
        out[name] = (out[name] * factor).astype(out[name].dtype)
    return out
```

```python
from contextlib import ExitStack

import numpy as np

import concourse.bass as bass
from concourse import mybir

ALU = mybir.AluOpType
ACT = mybir.ActivationFunctionType
F32 = mybir.dt.float32
F32R = mybir.dt.float32r
I32 = mybir.dt.int32
AX_X = mybir.AxisListType.X

P = 128
D = 1024
S = 512
CHUNK = 64
EPS = 1e-6
KT = D // P
NT = S // P
NCH = S // CHUNK

GH, HK, HV, GRANK, TAU = 4, 128, 256, 16, 16.0
DK, DV = GH * HK, GH * HV

MH, NOPE, ROPE, QK, MV = 16, 64, 32, 96, 64
HALF = ROPE // 2
QRANK, KVRANK = 384, 256
QT, CT = QRANK // P, KVRANK // P
THETA = 10000.0
GROUPS = 4
HG = MH // GROUPS
UNITS = HG * NT
AHEAD = 3

FF = -(-8 * D // (3 * 256)) * 256
FT = FF // P
DOWN = ((0, 6), (6, 6), (12, 5), (17, 5))

RING = 4
SLAB = 1024
NEG = -1.0e30
MAGIC = 1.5 * 2.0 ** 23

L_GL = 0
L_Q = L_GL + 1
L_K = L_Q + GH
L_V = L_K + GH
L_R = L_V + 8
L_WO = L_R + KT
L_UP1 = L_WO + KT
L_DN1 = L_UP1 + 2 * FT
L_C = L_DN1 + 4 * KT
L_KR = L_C + CT
L_CQ = L_KR + 1
L_GRP = L_CQ + QT
L_WOB = L_GRP + 4 * GROUPS
L_UP2 = L_WOB + KT
L_DN2 = L_UP2 + 2 * FT
L_END = L_DN2 + 4 * KT

T_X = 0
T_GL = T_X + KT
T_Q = T_GL + 1
T_K = T_Q + GH
T_V = T_K + GH
T_R = T_V + 8
T_WO = T_R + KT
T_UP1 = T_WO + KT
T_DN1 = T_UP1 + 2 * FT
T_C = T_DN1 + KT
T_KR = T_C + CT
T_CQ = T_KR + 1
T_WOB = T_CQ + QT
T_UP2 = T_WOB + KT
T_DN2 = T_UP2 + 2 * FT

V_A, V_BG, V_AO, V_B, V_QL, V_KV, V_CL, V_F, V_QN, V_KN = 0, 8, 12, 14, 22, 25, 33, 35, 51, 52
NVEC = 53

TURN = [int(h, 16) / 2.0 ** (12 * (j + 1)) / 4.0 for j, h in enumerate(("A2F", "983", "6E4", "E44", "152"))]

PIECES = ([("kv", t) for t in range(NT)] + [("q", t) for t in range(NT)]
          + [("kt", 0), ("kt", 1), ("kt", 2), ("qt", 0), ("qt", 1), ("kt", 3), ("qt", 2), ("qt", 3)])
COUNTED = [0]
for _kind, _t in PIECES:
    COUNTED.append(COUNTED[-1] + (not (_kind in ("kv", "q") and _t == NT - 1)))
NCOUNTED = COUNTED[-1]


class Links:

    def __init__(self, engine, sem):
        self.engine, self.sem, self.n, self.off = engine, sem, 0, 0

    def __call__(self, instruction):
        instruction.then_inc(self.sem, 1)
        self.n += 1
        self.engine.wait_ge(self.sem, self.off + self.n)

    def enter(self, i, per, first=0):
        self.start, self.per, self.first, self.off = self.n, per, first, (i - first) * per

    def leave(self, times):
        assert self.n - self.start == self.per, (self.n - self.start, self.per)
        self.n, self.off = self.start + self.per * times, 0


def trunk(nc, x, positions, a_norm, a_w_in, a_w_gate_up, a_b_gate, a_out_norm, a_w_out,
          b_norm, b_w_dq, b_q_latent_norm, b_w_uq, b_q_norm, b_w_out,
          kv_norm, kv_w_down, kv_latent_norm, kv_w_up, k_norm, f_norm, f_w_in, f_w_out, out):
    ctx = ExitStack()
    with ctx:
        def sb(name, shape, dt=F32, stack=ctx):
            return stack.enter_context(nc.sbuf_tensor(name, shape, dt))

        def sem(name):
            return ctx.enter_context(nc.semaphore(name))

        x_t = sb("x_t", [P, KT, S])
        w_raw = sb("w_raw", [P, RING, SLAB])
        w_h = sb("w_h", [P, RING, SLAB], F32R)
        w_l = sb("w_l", [P, RING, SLAB], F32R)
        ident = sb("ident", [P, P])
        ones = sb("ones", [P, P])
        acc = sb("acc", [P, S])
        sq = sb("sq", [P, 2, S])
        rinv_b = sb("rinv_b", [P, S])
        rinvo_b = sb("rinvo_b", [P, S])
        t1 = sb("t1", [P, 2, S])
        t2 = sb("t2", [P, 2, S])
        diag = sb("diag", [P, NT, P])
        vecs = sb("vecs", [P, NVEC + NT])
        r_nat = sb("r_nat", [P, 4, NT])
        nw = sb("nw", [P, 3, UNITS])
        dec = sb("dec", [P, GH, NCH])
        sc_next = sb("sc_next", [P, UNITS])
        sc = sb("sc", [P, UNITS])
        stat = sb("stat", [P, 4, UNITS])

        rope_g = sb("rope_g", [P, 2, ROPE])
        kr_ss = sb("kr_ss", [P, NT])
        trig = sb("trig", [P, 2, NT, HALF])
        inv_freq = sb("inv_freq", [P, HALF])

        def overlay(tag, behind_hi, behind_lo, over_b):
            made = []
            with ExitStack() as stack:
                for n, (group, room) in enumerate(((behind_hi, (FT - KT) * S), (behind_lo, (FT - KT) * S), (over_b, 2 * KT * S))):
                    if n < 2:
                        sb(f"{tag}_under{n}", [P, KT * S], F32, stack)
                    used = 0
                    for name, shape, *dt in group:
                        made.append(sb(f"{tag}_{name}", shape, dt[0] if dt else F32, stack))
                        used += int(np.prod(shape[1:]))
                    assert used <= room, (tag, n, used, room)
                    if used < room:
                        sb(f"{tag}_rest{n}", [P, room - used], F32, stack)
            return made

        (b_t, d_t, q_t, att, k_end, v_g, state, k_ring, sr, e_ring, gt, gl_t, w_gate, mask, rows, pos_i, pos_f) = overlay(
            "gla",
            [("b_t", [P, GH, S]), ("d_t", [P, GH, S]), ("q_t", [P, GH, S]), ("att", [P, NT, P]), ("k_end", [P, NT, HK])],
            [("v", [P, NT, DV]), ("state", [P, NCH, HV]), ("k_ring", [P, 2, S])],
            [("sr", [P, KT, S]), ("e_ring", [P, 2, S]), ("gt", [P, 2, S]), ("gl_t", [P, S]), ("w_gate", [P, DK]),
             ("mask", [P, P]), ("rows", [P, P]), ("pos_i", [P, P]), ("pos_f", [P, P])])
        (kv_n, q_n, k_n, sq_g, rope_c, v_cur, c_h, c_l, cq_h, cq_l, kr, o_n, k_tt, q_tt, prob, prob_t) = overlay(
            "mla",
            [("kv_n", [P, NT, HG * P]), ("q_n", [P, UNITS, QK]), ("k_n", [P, UNITS, QK]), ("sq_g", [P, UNITS, QK]),
             ("rope_c", [P, 8, NT, HALF])],
            [("v_cur", [P, NT, HG, MV]), ("c_h", [P, CT, S], F32R), ("c_l", [P, CT, S], F32R),
             ("cq_h", [P, QT, S], F32R), ("cq_l", [P, QT, S], F32R), ("kr", [P, 4, NT, ROPE]), ("o_n", [P, NT, P])],
            [("k_tt", [P, HG, S]), ("q_tt", [P, HG, S]), ("prob", [P, NT, S]), ("prob_t", [P, 2, S])])
        hid_h = sb("hid_h", [P, FT, S], F32R)
        hid_l = sb("hid_l", [P, FT, S], F32R)
        b_h = sb("b_h", [P, KT, S], F32R)
        b_l = sb("b_l", [P, KT, S], F32R)
        a_h, a_l = hid_h[:, 0:KT, :], hid_l[:, 0:KT, :]

        bank = [ctx.enter_context(nc.psum_tensor(f"bank{n}", [P, S], F32)) for n in range(8)]
        STAT, KV_BANKS, O_BANKS = 4, (4, 5), (6, 7)
        PT_BANKS, PV_BANK, PIECE = (4, 5), 6, 7
        Y_BANKS = (5, 6)

        x_in, vec_in, gate_in = sem("x_in"), sem("vec_in"), sem("gate_in")
        w_in = [sem(f"w_in{n}") for n in range(RING)]
        w_hi, w_lo = sem("w_hi"), sem("w_lo")
        slab_done = sem("slab_done")
        tile_taken = sem("tile_taken")
        const_done, pool_step, w_gate_zero = sem("const_done"), sem("pool_step"), sem("w_gate_zero")
        rows_one, rows_pos = sem("rows_one"), sem("rows_pos")
        vec_ps, vec_sb = sem("vec_ps"), sem("vec_sb")
        x_ps = sem("x_ps")
        x_hi, x_sq, x_lo, x_acc = sem("x_hi"), sem("x_sq"), sem("x_lo"), sem("x_acc")
        stat_ps, stat_read, stat_nat = sem("stat_ps"), sem("stat_read"), sem("stat_nat")
        diag_done, spread_ps, spread_sb = sem("diag_done"), sem("spread_ps"), sem("spread_sb")
        dve_step, act_step = sem("dve_step"), sem("act_step")
        z_ps, z_abs, g_soft, g_cum, g_diff = sem("z_ps"), sem("z_abs"), sem("g_soft"), sem("g_cum"), sem("g_diff")
        g_up, g_down, g_end = sem("g_up"), sem("g_down"), sem("g_end")
        g_prep, r_silu = sem("g_prep"), sem("r_silu")
        kend_ps, kend_sb, att_ps, att_sb = sem("kend_ps"), sem("kend_sb"), sem("att_ps"), sem("att_sb")
        chunk_ps, state_sb = sem("chunk_ps"), sem("state_sb")
        o_ps, o_sq, o_acc, o_gated = sem("o_ps"), sem("o_sq"), sem("o_acc"), sem("o_gated")
        o_fin, o_hi, o_lo = sem("o_fin"), sem("o_hi"), sem("o_lo")
        f_silu, f_prod, f_hi, f_lo = sem("f_silu"), sem("f_prod"), sem("f_hi"), sem("f_lo")
        xb_hi, xb_lo = sem("xb_hi"), sem("xb_lo")
        c_sq, c_hi, c_lo, c_acc = sem("c_sq"), sem("c_hi"), sem("c_lo"), sem("c_acc")
        turns, trig_done = sem("turns"), sem("trig_done")
        piece_ps, piece_taken = sem("piece_ps"), sem("piece_taken")
        ksq, qsq, k_rows, q_rows = sem("ksq"), sem("qsq"), sem("k_rows"), sem("q_rows")
        v_ready, sc_free = sem("v_ready"), sem("sc_free")
        s_ps, s_bias, p_exp = sem("s_ps"), sem("s_bias"), sem("p_exp")
        pt_ps, pt_sb, pv_ps = sem("pt_ps"), [sem("pt_sb0"), sem("pt_sb1")], sem("pv_ps")
        o_nat, ot_ps, ot_hi, ot_lo = sem("o_nat"), sem("ot_ps"), sem("ot_hi"), sem("ot_lo")
        y_ps, y_sb = sem("y_ps"), sem("y_sb")
        y_out = [sem("y_out0"), sem("y_out1")]

        def at_least(eng, s, value):
            if not isinstance(value, int) or value > 0:
                eng.wait_ge(s, value)

        block = ctx.enter_context(nc.Block())

        @block.sync
        def _(sp):
            x_rows = x.rearrange("b (t p) n -> p (b t) n", p=P)
            for t in range(NT):
                sp.dma_start(v_g[:, t, :], x_rows[:, t, :]).then_inc(x_in, 16)

            def load(n, off, src, cols):
                k = src.shape[1]
                if not (isinstance(off, int) and n + off < RING):
                    sp.wait_ge(w_lo, n + off - RING + 1)
                sp.dma_start(w_raw[:, n % RING, 0:k * cols].rearrange("p (k c) -> p k c", c=cols), src)\
                    .then_inc(w_in[n % RING], 16)

            def by_rows(w):
                return w.rearrange("(k p) n -> p k n", p=P)

            def columns(n, w, m0, count):
                for m in range(count):
                    load(n + m, 0, by_rows(w)[:, :, (m0 + m) * P:(m0 + m + 1) * P], P)

            w = a_w_in[0]
            gla_in = by_rows(w)
            load(L_GL, 0, gla_in[:, :, 2 * DK + 2 * DV + GRANK - P:2 * DK + 2 * DV + GRANK], P)
            columns(L_Q, w, 0, GH)
            columns(L_K, w, GH, GH)
            for c in range(2):
                for j in range(4):
                    load(L_V + 4 * c + j, 0, gla_in[:, 2 * j:2 * j + 2, 2 * DK + c * S:2 * DK + (c + 1) * S], S)
            columns(L_R, w, (2 * DK + DV) // P, KT)
            columns(L_WO, a_w_out[0], 0, KT)

            def ffn(n_up, n_dn, layer):
                up, dn = by_rows(f_w_in[layer]), by_rows(f_w_out[layer])
                with sp.Fori(0, FT // 2) as i:
                    for c in range(4):
                        src = up[:, :, (c % 2) * FF:(c % 2 + 1) * FF]
                        load(n_up + c, 4 * i, src[:, :, bass.ts(2 * i + c // 2, P)], P)
                with sp.Fori(0, KT) as i:
                    for c, (k, kn) in enumerate(DOWN):
                        load(n_dn + c, 4 * i, dn[:, k:k + kn, bass.ts(i, P)], P)

            ffn(L_UP1, L_DN1, 0)
            columns(L_C, kv_w_down, 0, CT)
            load(L_KR, 0, by_rows(kv_w_down)[:, :, KVRANK:KVRANK + ROPE], ROPE)
            columns(L_CQ, b_w_dq[0], 0, QT)
            with sp.Fori(0, GROUPS) as g:
                for c in range(2):
                    load(L_GRP + c, 4 * g, by_rows(kv_w_up)[:, :, bass.ts(2 * g + c, 2 * P)], 2 * P)
                for c in range(2):
                    load(L_GRP + 2 + c, 4 * g, by_rows(b_w_uq[0])[:, :, bass.ts(2 * g + c, 2 * QK)], 2 * QK)
            columns(L_WOB, b_w_out[0], 0, KT)
            ffn(L_UP2, L_DN2, 1)

        @block.gpsimd
        def _(pool):
            pool.memset(ident[:, :], 0.0).then_inc(pool_step, 1)
            pool.memset(mask[:, :], 1.0).then_inc(pool_step, 1)
            pool.memset(w_gate[:, :], 0.0).then_inc(w_gate_zero, 1)
            pool.memset(ones[:, :], 1.0)
            pool.memset(att[:, :, :], 0.0)
            for j in range(HALF):
                pool.memset(inv_freq[:, j:j + 1], float(np.float32(THETA ** (-j / HALF))))
            pool.memset(t2[:, 1, :], 1.0).then_inc(pool_step, 1)
            pool.wait_ge(pool_step, 3)
            pool.affine_select(out=ident[:, :], in_=ident[:, :], compare_op=ALU.not_equal, fill=1.0, base=0,
                               pattern=[[-1, P]], channel_multiplier=1).then_inc(pool_step, 1)
            pool.affine_select(out=mask[:, :], in_=mask[:, :], compare_op=ALU.is_ge, fill=0.0, base=0,
                               pattern=[[1, P]], channel_multiplier=-1).then_inc(pool_step, 1)
            pool.memset(t2[:, 1, :].rearrange("p (c n) -> p c n", n=CHUNK)[:, :, 0:1], 0.0).then_inc(pool_step, 1)
            pool.wait_ge(pool_step, 6)
            pool.memset(mask[0:CHUNK, CHUNK:P], 0.0).then_inc(const_done, 1)

            def lo(n, off, size):
                pool.wait_ge(w_hi, n + off + 1)
                s = n % RING
                pool.tensor_tensor(w_l[:, s, 0:size], w_raw[:, s, 0:size], w_h[:, s, 0:size].bitcast(F32),
                                   ALU.subtract).then_inc(w_lo, 1)

            def run(n, size, first, count):
                with pool.Fori(0, count // 4) as i:
                    for c in range(4):
                        lo(n + c, 4 * i, size)

            def down(n):
                with pool.Fori(0, KT) as i:
                    for c, (_, kn) in enumerate(DOWN):
                        lo(n + c, 4 * i, kn * P)

            lo(L_GL, 0, SLAB)
            run(L_Q, SLAB, 0, L_DN1 - L_Q)
            down(L_DN1)
            for n in range(L_C, L_GRP):
                lo(n, 0, KT * ROPE if n == L_KR else SLAB)
            with pool.Fori(0, GROUPS) as g:
                for c in range(4):
                    lo(L_GRP + c, 4 * g, CT * 2 * P if c < 2 else QT * 2 * QK)
            run(L_WOB, SLAB, 0, L_DN2 - L_WOB)
            down(L_DN2)

        @block.tensor
        def _(pe):
            def mm(o, lhs, rhs, start, stop):
                return pe.matmul(o, lhs, rhs, start=start, stop=stop)

            def mm3(o, lhs_h, lhs_l, rhs_h, rhs_l, start, stop):
                mm(o, lhs_h, rhs_l, start, False)
                mm(o, lhs_l, rhs_h, False, False)
                return mm(o, lhs_h, rhs_h, False, stop)

            def slab(n, cols):
                s = n % RING
                return [w[:, s, 0:SLAB // cols * cols].rearrange("p (k c) -> p k c", c=cols) for w in (w_h, w_l)]

            def wait_slab(n, off=0):
                pe.wait_ge(w_lo, n + off + 1)

            def wait_tile(tile, off=0):
                at_least(pe, tile_taken, tile + off - 3)

            def column_tile(n, tile, act_h, act_l, off=0, tile_off=None, parts=None):
                tile_off = off if tile_off is None else tile_off
                wait_slab(n, off)
                wait_tile(tile, tile_off)
                wh, wl = slab(n, P)
                for k in range(KT):
                    if parts is not None:
                        pe.wait_ge(parts[0], parts[1] + k + 1)
                    last = mm3(bank[tile % 4][:, :], wh[:, k, :], wl[:, k, :], act_h[:, k, :], act_l[:, k, :],
                               k == 0, k == KT - 1)
                last.then_inc(slab_done, 1)

            def stat_sum(s, spreads, ready, count, squares=acc, col=0):
                pe.wait_ge(ready, count)
                at_least(pe, stat_read, s)
                at_least(pe, spread_sb, spreads)
                for t in range(NT):
                    last = mm(bank[STAT][:, t:t + 1], squares[:, t * P:(t + 1) * P], ones[:, 0:1], True, True)
                last.then_inc(stat_ps, 1)

            def stat_spread(b):
                pe.wait_ge(diag_done, b + 1)
                for t in range(NT):
                    last = mm(bank[STAT][:, t * P:(t + 1) * P], ones[:, :], diag[:, t, :], True, True)
                last.then_inc(spread_ps, 1)

            pe.wait_ge(const_done, 1)
            pe.wait_ge(vec_in, 16 * 12)
            pe.wait_ge(rows_pos, 1)
            pe.transpose(bank[STAT][:, 0:NVEC], rows[0:NVEC, :], ident[0:NVEC, 0:NVEC])
            pe.transpose(bank[STAT][:, NVEC:NVEC + NT], pos_f[0:NT, :], ident[0:NT, 0:NT]).then_inc(vec_ps, 1)
            pe.wait_ge(x_in, 16 * NT)
            for m in range(KT):
                wait_tile(T_X + m)
                for t in range(NT):
                    last = pe.transpose(bank[(T_X + m) % 4][:, t * P:(t + 1) * P], v_g[:, t, m * P:(m + 1) * P], ident[:, :])
                last.then_inc(x_ps, 1)

            column_tile(L_GL, T_GL, a_h, a_l, parts=(x_lo, 0))
            pe.wait_ge(vec_sb, 1)
            stat_sum(0, 0, x_acc, KT)
            column_tile(L_Q, T_Q, a_h, a_l)
            stat_spread(0)
            column_tile(L_Q + 1, T_Q + 1, a_h, a_l)
            pe.wait_ge(tile_taken, T_GL + 1)
            pe.wait_ge(gate_in, 32)
            for h in range(GH):
                if h == 3:
                    pe.wait_ge(z_abs, 1)
                mm(bank[(5, 6, 7, 5)[h]][:, :], w_gate[:, h * HK:(h + 1) * HK], gl_t[:, :], True, True).then_inc(z_ps, 1)
            for h in range(2, GH):
                column_tile(L_Q + h, T_Q + h, a_h, a_l)
            for h in range(GH):
                column_tile(L_K + h, T_K + h, a_h, a_l)
            for c in range(2):
                for j in range(4):
                    wait_slab(L_V + 4 * c + j)
                    wh, wl = slab(L_V + 4 * c + j, S)
                    for t in range(NT):
                        if j == 0:
                            wait_tile(T_V + 4 * c + t)
                        for k in range(2):
                            kk = 2 * j + k
                            last = mm3(bank[(T_V + t) % 4][:, :], a_h[:, kk, t * P:(t + 1) * P], a_l[:, kk, t * P:(t + 1) * P],
                                       wh[:, k, :], wl[:, k, :], kk == 0, kk == KT - 1)
                    last.then_inc(slab_done, 1)

            def gla_head(h):
                pe.wait_ge(g_prep, h + 1)
                if h == 0:
                    pe.wait_ge(z_abs, GH)
                    pe.wait_ge(spread_sb, 1)
                for t in range(NT):
                    last = pe.transpose(bank[4][:, t * P:(t + 1) * P], d_t[:, h, t * P:(t + 1) * P], ident[:, :])
                last.then_inc(kend_ps, 1)
                for t in range(NT):
                    last = mm(bank[5][:, t * P:(t + 1) * P], b_t[:, h, t * P:(t + 1) * P], q_t[:, h, t * P:(t + 1) * P], True, True)
                last.then_inc(att_ps, 1)
                for c in range(NCH - 1):
                    if c == 0:
                        pe.wait_ge(kend_sb, h + 1)
                        pe.wait_ge(tile_taken, T_V + 8)
                    if c == 1:
                        pe.wait_ge(att_sb, h + 1)
                    if c >= 2:
                        pe.wait_ge(state_sb, (NCH - 1) * h + c - 1)
                    half = slice(CHUNK * (c % 2), CHUNK * (c % 2 + 1))
                    mm(bank[KV_BANKS[c % 2]][:, 0:HV], k_end[half, c // 2, :], v_g[half, c // 2, h * HV:(h + 1) * HV], True, True)\
                        .then_inc(chunk_ps, 1)
                at_least(pe, o_gated, h)
                for t in range(NT):
                    for e in range(2):
                        cols = slice(h * HV + e * P, h * HV + (e + 1) * P)
                        o = bank[O_BANKS[e]]
                        last = mm(o[:, t * P:(t + 1) * P], v_g[:, t, cols], att[:, t, :], True, False)
                        for c in (2 * t, 2 * t + 1):
                            if c:
                                pe.wait_ge(state_sb, (NCH - 1) * h + c)
                                last = mm(o[:, c * CHUNK:(c + 1) * CHUNK], state[:, c, e * P:(e + 1) * P],
                                          q_t[:, h, c * CHUNK:(c + 1) * CHUNK], False, c == 2 * t + 1)
                last.then_inc(o_ps, 1)

            for h in range(GH):
                column_tile(L_R + 2 * h, T_R + 2 * h, a_h, a_l)
                if h:
                    stat_sum(h, h, o_acc, h)
                column_tile(L_R + 2 * h + 1, T_R + 2 * h + 1, a_h, a_l)
                if h:
                    stat_spread(h)
                    pe.wait_ge(spread_sb, h + 1)
                gla_head(h)
            stat_sum(GH, GH, o_acc, GH)
            stat_spread(GH)

            def project_out(n, tile, ready, count):
                with pe.Fori(0, KT // 4) as i:
                    for c in range(4):
                        column_tile(n + c, tile + c, a_h, a_l, 4 * i, parts=(ready, count - KT) if c == 0 else None)

            project_out(L_WO, T_WO, o_lo, KT)

            def ffn_up(n, tile, s, spreads, xs):
                column_tile(n, tile, b_h, b_l, parts=(x_lo, xs - KT))
                stat_sum(s, spreads, x_acc, xs)
                column_tile(n + 1, tile + 1, b_h, b_l)
                stat_spread(spreads)
                for c in (2, 3):
                    column_tile(n + c, tile + c, b_h, b_l)
                with pe.Fori(1, FT // 2) as i:
                    for c in range(4):
                        column_tile(n + c, tile + c, b_h, b_l, 4 * i)

            def ffn_down(n, tile, hidden, last_layer):
                def down_tile(m, i):
                    for c, (k0, kn) in enumerate(DOWN):
                        wait_slab(n + 4 * m + c, 16 * i)
                        wh, wl = slab(n + c, P)
                        if c == 0:
                            wait_tile(tile + m, 4 * i)
                        for k in range(kn):
                            if m == 0:
                                pe.wait_ge(f_lo, hidden - FT + k0 + k + 1)
                            last = mm3(bank[(tile + m) % 4][:, :], wh[:, k, :], wl[:, k, :], hid_h[:, k0 + k, :], hid_l[:, k0 + k, :],
                                       k0 + k == 0, k0 + k == FT - 1)
                        last.then_inc(slab_done, 1)

                def turn_back(m, i, first):
                    pe.wait_ge(tile_taken, tile + m + 4 * i + 1)
                    if not first:
                        pe.wait_ge(y_sb, m + 4 * i - 1)
                    for t in range(NT):
                        last = pe.transpose(bank[Y_BANKS[m % 2]][:, t * P:(t + 1) * P], t2[:, m % 2, t * P:(t + 1) * P], ident[:, :])
                    last.then_inc(y_ps, 1)

                if not last_layer:
                    with pe.Fori(0, KT // 4) as i:
                        for m in range(4):
                            down_tile(m, i)
                else:
                    for m in range(KT):
                        down_tile(m, 0)
                        if m:
                            turn_back(m - 1, 0, m - 1 < 2)
                    turn_back(KT - 1, 0, False)

            ffn_up(L_UP1, T_UP1, 5, 5, 2 * KT)
            ffn_down(L_DN1, T_DN1, FT, False)

            for c in range(CT):
                column_tile(L_C + c, T_C + c, b_h, b_l, parts=(x_lo, 2 * KT) if c == 0 else None)
                if c == 0:
                    stat_sum(6, 6, x_acc, 3 * KT)
            stat_spread(6)
            wait_slab(L_KR)
            wait_tile(T_KR)
            wh, wl = slab(L_KR, ROPE)
            for t in range(NT):
                for k in range(KT):
                    last = mm3(bank[T_KR % 4][:, t * ROPE:(t + 1) * ROPE], b_h[:, k, t * P:(t + 1) * P], b_l[:, k, t * P:(t + 1) * P],
                               wh[:, k, :], wl[:, k, :], k == 0, k == KT - 1)
            last.then_inc(slab_done, 1)
            column_tile(L_CQ, T_CQ, a_h, a_l, parts=(xb_lo, 0))
            stat_sum(7, 7, c_acc, CT)
            for c in range(1, QT):
                column_tile(L_CQ + c, T_CQ + c, a_h, a_l)
            stat_sum(8, 7, c_acc, CT + QT)

            def piece(u, gi):
                kind, t = PIECES[u]
                at_least(pe, piece_taken, 16 * gi + u)
                if kind == "kv" or kind == "q":
                    base, width, split = (0, 2 * P, (c_h, c_l)) if kind == "kv" else (2, 2 * QK, (cq_h, cq_l))
                    kts = CT if kind == "kv" else QT
                    for c in range(2):
                        if t == 0:
                            wait_slab(L_GRP + base + c, 4 * gi)
                        wh, wl = slab(L_GRP + base + c, width)
                        for k in range(kts):
                            last = mm3(bank[PIECE][:, c * width:(c + 1) * width], split[0][:, k, t * P:(t + 1) * P],
                                       split[1][:, k, t * P:(t + 1) * P], wh[:, k, :], wl[:, k, :], k == 0, k == kts - 1)
                        if t == NT - 1:
                            last.then_inc(slab_done, 1)
                    if t < NT - 1:
                        last.then_inc(piece_ps, 1)
                else:
                    src = k_n if kind == "kt" else q_n
                    pe.wait_ge(k_rows if kind == "kt" else q_rows, gi + 1)
                    for j in range(NT):
                        last = pe.transpose(bank[PIECE][0:QK, j * P:(j + 1) * P], src[:, HG * j + t, :], ident[:, :])
                    last.then_inc(piece_ps, 1)

            def scores(v, gi):
                h, t = v // NT % HG, v % NT
                n = 16 * gi + v
                at_least(pe, p_exp, n - NT + 1)
                if t == 0:
                    gk = 16 * (gi + v // UNITS)
                    pe.wait_ge(piece_taken, gk + 1 + max(PIECES.index(("kt", h)), PIECES.index(("qt", h))))
                mm(bank[t][:, 0:(t + 1) * P], q_tt[0:QK, h, t * P:(t + 1) * P], k_tt[0:QK, h, 0:(t + 1) * P], True, True)\
                    .then_inc(s_ps, 1)

            def turn(u, gi):
                h, t = divmod(u, NT)
                n = 16 * gi + u
                pe.wait_ge(p_exp, n + 1)
                at_least(pe, pt_sb[u % 2], 8 * gi + u // 2)
                for j in range(t + 1):
                    last = pe.transpose(bank[PT_BANKS[u % 2]][:, j * P:(j + 1) * P], prob[:, t, j * P:(j + 1) * P], ident[:, :])
                last.then_inc(pt_ps, 1)

            def values(u, gi):
                h, t = divmod(u, NT)
                pe.wait_ge(pt_sb[u % 2], 8 * gi + u // 2 + 1)
                if t == 0:
                    at_least(pe, o_nat, 4 * gi + h)
                if u == 0:
                    pe.wait_ge(v_ready, gi + 1)
                for j in range(t + 1):
                    last = mm(bank[PV_BANK][:, t * MV:(t + 1) * MV], prob_t[:, u % 2, j * P:(j + 1) * P], v_cur[:, j, h, :],
                              j == 0, j == t)
                last.then_inc(pv_ps, 1)

            def outputs(pair, gi, pieces):
                pe.wait_ge(o_nat, 4 * gi + 2 * pair + 2)
                pe.wait_ge(piece_taken, pieces)
                for t in range(NT):
                    last = pe.transpose(bank[PIECE][:, t * P:(t + 1) * P], o_n[:, t, :], ident[:, :])
                last.then_inc(ot_ps, 1)
                pe.wait_ge(ot_lo, 2 * gi + pair + 1)

            def group(gi, first, more):
                for u in range(UNITS):
                    turn(u, gi)
                    if u + AHEAD < UNITS or more:
                        scores(u + AHEAD, gi)
                    if u == 2 and not first:
                        outputs(1, gi - 1, 16 * gi + (16 + u if more else 16))
                    if u == 10:
                        outputs(0, gi, 16 * gi + (16 + u if more else 16))
                    if more:
                        piece(u, gi + 1)
                    values(u, gi)

            pe.wait_ge(tile_taken, T_CQ + QT)
            pe.wait_ge(stat_read, 9)
            pe.wait_ge(c_lo, CT + QT)
            for u in range(UNITS):
                piece(u, 0)
            for v in range(AHEAD):
                scores(v, 0)
            group(0, True, True)
            with pe.Fori(1, GROUPS - 1) as g:
                group(g, False, True)
            group(GROUPS - 1, False, False)
            outputs(1, GROUPS - 1, 16 * GROUPS)

            project_out(L_WOB, T_WOB, ot_lo, KT)
            ffn_up(L_UP2, T_UP2, 9, 7, 4 * KT)
            ffn_down(L_DN2, T_DN2, 2 * FT, True)

        @block.scalar
        def _(act):
            link = Links(act, act_step)

            def copy(o, i, **kw):
                return act.activation(o, i, ACT.Copy, **kw)

            def hi(n, off, size):
                s = n % RING
                act.wait_ge(w_in[s], 16 * (n // RING + 1) + 4 * off)
                if not (isinstance(off, int) and n + off < RING):
                    act.wait_ge(slab_done, n + off - RING + 1)
                copy(w_h[:, s, 0:size], w_raw[:, s, 0:size]).then_inc(w_hi, 1)

            def size_of(n):
                if L_DN1 <= n < L_C:
                    return DOWN[(n - L_DN1) % 4][1] * P
                if n >= L_DN2:
                    return DOWN[(n - L_DN2) % 4][1] * P
                if n == L_KR:
                    return KT * ROPE
                if L_GRP <= n < L_WOB:
                    return CT * 2 * P if (n - L_GRP) % 4 < 2 else QT * 2 * QK
                return SLAB

            def hi_next(n, off=0):
                if n + RING < L_END:
                    hi(n + RING, off, size_of(n + RING))

            act.wait_ge(rows_one, 1)
            vec_rows = ((V_A, a_norm, KT), (V_BG, a_b_gate, GH), (V_AO, a_out_norm, HV // P), (V_B, b_norm, KT),
                        (V_QL, b_q_latent_norm, QT), (V_F, f_norm, 2 * KT))
            for row, src, count in vec_rows:
                act.dma_start(rows[row:row + count, :], src.rearrange("a (k p) -> (a k) p", p=P)).then_inc(vec_in, 16)
            for row, src, count in ((V_KV, kv_norm, KT), (V_CL, kv_latent_norm, CT)):
                act.dma_start(rows[row:row + count, :], src.rearrange("(k p) -> k p", p=P)).then_inc(vec_in, 16)
            act.dma_start(rows[V_QN:V_QN + 1, 0:NOPE], b_q_norm[:, 0:NOPE]).then_inc(vec_in, 16)
            act.dma_start(rows[V_KN:V_KN + 1, 0:NOPE], k_norm.rearrange("(a n) -> a n", a=1)[:, 0:NOPE]).then_inc(vec_in, 16)
            act.dma_start(rope_g[:, 0, :], b_q_norm[0:1, NOPE:QK].to_broadcast([P, ROPE])).then_inc(vec_in, 16)
            act.dma_start(rope_g[:, 1, :], k_norm.rearrange("(a n) -> a n", a=1)[:, NOPE:QK].to_broadcast([P, ROPE])).then_inc(vec_in, 16)
            act.wait_ge(w_gate_zero, 1)
            act.dma_start(w_gate[P - GRANK:P, :], a_w_gate_up[0]).then_inc(gate_in, 16)
            act.dma_start(pos_i[0:NT, :].bitcast(I32), positions.rearrange("b (t p) -> (b t) p", p=P)).then_inc(gate_in, 16)

            def x_tile(m, n_x, tile, gain, dst):
                act.wait_ge(tile_taken, tile + m + 1)
                copy(dst[:, m, :], x_t[:, m, :], scale=vecs[:, gain + m:gain + m + 1]).then_inc(x_hi, 1)
                at_least(act, x_acc, n_x + m - 1)
                act.activation(sq[:, m % 2, :], x_t[:, m, :], ACT.Square).then_inc(x_sq, 1)

            def spread(b, dst):
                act.wait_ge(spread_ps, b + 1)
                copy(dst[:, :], bank[STAT][:, :]).then_inc(spread_sb, 1)

            act.wait_ge(vec_sb, 1)
            for m in range(KT):
                x_tile(m, 0, T_X, V_A, a_h)
                if m % 2:
                    hi(m // 2, 0, SLAB)

            hi_next(L_GL)
            hi_next(L_Q)
            spread(0, rinv_b)
            for h in range(GH):
                act.wait_ge(z_abs, h + 1)
                link(act.activation(gt[:, h % 2, :], gt[:, h % 2, :], ACT.Exp))
                act.activation(gt[:, h % 2, :], gt[:, h % 2, :], ACT.Ln, bias=1.0).then_inc(g_soft, 1)
                if h < 3:
                    hi_next(L_Q + 1 + h)
            for h in range(GH):
                hi_next(L_K + h)
                act.wait_ge(g_cum, h + 1)
                at_least(act, g_prep, h - 1)
                act.activation(e_ring[:, h % 2, :], b_t[:, h, :], ACT.Exp, scale=1.0 / TAU).then_inc(g_up, 1)
                ends = b_t[:, h, :].rearrange("p (c n) -> p c n", n=CHUNK)[:, :, CHUNK - 1]
                link(act.activation(dec[:, h, :], ends, ACT.Exp, scale=1.0 / TAU))
                act.wait_ge(g_diff, h + 1)
                act.activation(b_t[:, h, :], b_t[:, h, :], ACT.Exp, scale=-1.0 / TAU).then_inc(g_down, 1)
                act.activation(d_t[:, h, :], d_t[:, h, :], ACT.Exp, scale=1.0 / TAU).then_inc(g_end, 1)
            for n in range(4):
                hi_next(L_V + n)
            act.wait_ge(turns, 1)
            act.activation(trig[:, :, :, :], t1[:, 0, 0:2 * NT * HALF].rearrange("p (a t j) -> p a t j", a=2, t=NT), ACT.Sin,
                           scale=float(2.0 * np.pi)).then_inc(trig_done, 1)
            for n in range(4, 8):
                hi_next(L_V + n)

            def o_split(h):
                for e in range(2):
                    act.wait_ge(o_fin, 2 * h + e + 1)
                    copy(a_h[:, 2 * h + e, :], sr[:, 2 * h + e, :]).then_inc(o_hi, 1)

            for h in range(GH):
                for e in range(2):
                    m = 2 * h + e
                    hi_next(L_R + m)
                    act.wait_ge(tile_taken, T_R + m + 1)
                    act.activation(sr[:, m, :], t1[:, m % 2, :], ACT.Silu).then_inc(r_silu, 1)
                    if e and h:
                        spread(h, rinvo_b)
                act.wait_ge(kend_ps, h + 1)
                at_least(act, chunk_ps, (NCH - 1) * h)
                copy(k_end[:, :, :], bank[4][:, :].rearrange("p (t n) -> p t n", n=HK)).then_inc(kend_sb, 1)
                act.wait_ge(o_ps, h + 1)
                at_least(act, o_acc, h)
                for e in range(2):
                    act.activation(sq[:, e, :], bank[O_BANKS[e]][:, :], ACT.Square).then_inc(o_sq, 1)
                if h == GH - 1:
                    for hh in range(GH - 1):
                        o_split(hh)
            spread(GH, rinvo_b)
            o_split(GH - 1)

            def project_out(n, tile, n_x, gain):
                for m in range(KT):
                    hi_next(n + m)
                    x_tile(m, n_x, tile, gain, b_h)

            project_out(L_WO, T_WO, KT, V_F)

            def ffn_up(n, tile, hidden, b):
                def pair(i, c, off, last):
                    m = hidden + 2 * i + c
                    hi_next(n + 2 * c + (2 * FT - 4 if last else 0), 0 if last else off)
                    if b is not None and c == 0 and isinstance(i, int) and i == 0:
                        spread(b, rinv_b)
                    act.wait_ge(tile_taken, tile + 4 * i + 2 * c + 1)
                    act.activation(t1[:, c, :], t1[:, c, :], ACT.Silu).then_inc(f_silu, 1)
                    hi_next(n + 2 * c + 1 + (2 * FT - 4 if last else 0), 0 if last else off)
                    act.wait_ge(f_prod, m + 1)
                    copy(hid_h[:, bass.ts(2 * i + c, 1), :] if not isinstance(i, int) else hid_h[:, 2 * i + c:2 * i + c + 1, :],
                         t2[:, c:c + 1, :]).then_inc(f_hi, 1)

                for c in range(2):
                    pair(0, c, 0, False)
                with act.Fori(1, FT // 2 - 1) as i:
                    for c in range(2):
                        pair(i, c, 4 * i, False)
                for c in range(2):
                    pair(FT // 2 - 1, c, 0, True)

            def ffn_down(n, tile, n_x, gain):
                for m in range(KT):
                    for c in range(4):
                        hi_next(n + 4 * m + c)
                    if gain is not None:
                        x_tile(m, n_x, tile, gain, b_h)
                    elif m:
                        turn_back(m - 1)

            def turn_back(m):
                act.wait_ge(y_ps, m + 1)
                if m >= 2:
                    act.wait_ge(y_out[m % 2], 16 * (m // 2))
                copy(t1[:, m % 2, :], bank[Y_BANKS[m % 2]][:, :]).then_inc(y_sb, 1)
                act.wait_ge(y_sb, m + 1)
                y_cols = out.rearrange("b (t p) n -> p (b t) n", p=P)
                act.dma_start(y_cols[:, :, m * P:(m + 1) * P], t1[:, m % 2, :].rearrange("p (t n) -> p t n", n=P))\
                    .then_inc(y_out[m % 2], 16)

            ffn_up(L_UP1, T_UP1, 0, 5)
            ffn_down(L_DN1, T_DN1, 2 * KT, V_KV)

            def latent(j, gain, dst, m):
                act.wait_ge(tile_taken, (T_C + j if j < CT else T_CQ + j - CT) + 1)
                copy(dst[:, m, :], t1[:, j % 2, :], scale=vecs[:, gain + m:gain + m + 1]).then_inc(c_hi, 1)
                act.wait_ge(x_acc, 3 * KT)
                at_least(act, c_acc, j - 1)
                act.activation(sq[:, j % 2, :], t1[:, j % 2, :], ACT.Square).then_inc(c_sq, 1)

            act.wait_ge(slab_done, L_C)
            for m in range(KT):
                copy(a_h[:, m, :], x_t[:, m, :], scale=vecs[:, V_B + m:V_B + m + 1]).then_inc(xb_hi, 1)
                if m == 3:
                    hi_next(L_C)
            hi_next(L_C + 1)
            spread(6, rinv_b)
            for j in range(CT):
                latent(j, V_CL, c_h, j)
            hi_next(L_KR)
            for j in range(QT):
                hi_next(L_CQ + j)
                latent(CT + j, V_QL, cq_h, j)

            def piece(u, gi, last=False):
                kind, t = PIECES[u]
                if kind in ("kv", "q") and t == NT - 1:
                    act.wait_ge(slab_done, L_GRP + 4 * gi + (2 if kind == "kv" else 4))
                else:
                    act.wait_ge(piece_ps, NCOUNTED * gi + COUNTED[u] + 1)
                if kind == "kv":
                    if t == 0:
                        at_least(act, v_ready, gi)
                    copy(kv_n[:, t, :], bank[PIECE][:, :], scale=r_nat[:, 1, t:t + 1]).then_inc(piece_taken, 1)
                elif kind == "q":
                    copy(q_n[:, HG * t:HG * (t + 1), :], bank[PIECE][:, 0:HG * QK].rearrange("p (h n) -> p h n", n=QK),
                         scale=r_nat[:, 2, t:t + 1]).then_inc(piece_taken, 1)
                else:
                    dst, gain = (k_tt, V_KN) if kind == "kt" else (q_tt, V_QN)
                    copy(dst[0:QK, t, :], bank[PIECE][0:QK, :], scale=vecs[0:QK, gain:gain + 1]).then_inc(piece_taken, 1)
                if kind == "kv" and t == NT - 1:
                    act.wait_ge(piece_taken, 16 * gi + u + 1)
                    at_least(act, q_rows, gi)
                    act.activation(sq_g[:, :, 0:NOPE].rearrange("p (t h) n -> p t h n", h=HG),
                                   kv_n[:, :, :].rearrange("p t (h n) -> p t h n", n=P)[:, :, :, 0:NOPE], ACT.Square).then_inc(ksq, 1)
                if kind == "q" and t == NT - 1:
                    act.wait_ge(piece_taken, 16 * gi + u + 1)
                    act.wait_ge(k_rows, gi + 1)
                    act.activation(sq_g[:, :, :], q_n[:, :, :], ACT.Square).then_inc(qsq, 1)
                if kind in ("kv", "q") and t == NT - 1:
                    for c in range(2):
                        n = L_GRP + (0 if kind == "kv" else 2) + c
                        if last:
                            hi_next(n + 4 * (GROUPS - 1))
                        else:
                            hi_next(n, 4 * gi)

            def exps(v, gi):
                h, t = v // NT % HG, v % NT
                n = 16 * gi + v
                act.wait_ge(s_bias, n + 1)
                at_least(act, pt_ps, n - NT + 1)
                w = (t + 1) * P
                col = v % UNITS
                act.activation(prob[:, t, 0:w], bank[t][:, 0:w], ACT.Exp, scale=sc[:, HG * t + h:HG * t + h + 1],
                               bias=stat[:, 1, col:col + 1], accum_out=stat[:, 2, col:col + 1]).then_inc(p_exp, 1)

            def turned(u, gi):
                if u % 2 == 0:
                    act.wait_ge(pt_ps, 16 * gi + u + 1)
                    at_least(act, pv_ps, 16 * gi + u - 1)
                    w = (u % NT + 1) * P
                    copy(prob_t[:, 0, 0:w], bank[PT_BANKS[0]][:, 0:w]).then_inc(pt_sb[0], 1)

            def outputs(pair, gi):
                act.wait_ge(ot_ps, 2 * gi + pair + 1)
                dst = a_h[:, 2 * gi + pair:2 * gi + pair + 1, :] if isinstance(gi, int) else a_h[:, bass.ts(2 * gi + pair, 1), :]
                copy(dst, bank[PIECE][:, :].rearrange("p (a n) -> p a n", a=1)).then_inc(ot_hi, 1)

            def group(gi, first, more, last=False):
                for u in range(UNITS):
                    turned(u, gi)
                    if u == 2 and not first:
                        outputs(1, gi - 1)
                    if u == 10:
                        outputs(0, gi)
                    if more:
                        piece(u, gi + 1, last)
                    if u + AHEAD < UNITS or more:
                        exps(u + AHEAD, gi)

            act.wait_ge(stat_nat, 2)
            for u in range(UNITS):
                piece(u, 0)
            for v in range(AHEAD):
                exps(v, 0)
            group(0, True, True)
            with act.Fori(1, GROUPS - 2) as g:
                group(g, False, True)
            group(GROUPS - 2, False, True, True)
            group(GROUPS - 1, False, False)
            outputs(1, GROUPS - 1)

            project_out(L_WOB, T_WOB, 3 * KT, V_F + KT)
            ffn_up(L_UP2, T_UP2, FT, 7)
            ffn_down(L_DN2, T_DN2, 0, None)
            turn_back(KT - 1)
            for s in y_out:
                act.wait_ge(s, 16 * KT // 2)

        @block.vector
        def _(dve):
            link = Links(dve, dve_step)

            def tt(o, a, b, op):
                return dve.tensor_tensor(o, a, b, op)

            def stt(o, a, scalar, b, op0, op1):
                return dve.scalar_tensor_tensor(out=o, in0=a, scalar=scalar, in1=b, op0=op0, op1=op1)

            def ts(o, a, s1, s2, op0, op1=None):
                if op1 is None:
                    return dve.tensor_scalar(o, a, s1, None, op0)
                return dve.tensor_scalar(o, a, s1, s2, op0, op1)

            def rsqrt(sums, width, count, dst, signal=None):
                m, y, a = (nw[:, j, 0:count] for j in range(3))
                first = ts(m, sums, 1.0 / width, EPS, ALU.mult, ALU.add)
                if signal is not None:
                    first.then_inc(signal[0], 1)
                    dve.wait_ge(signal[0], signal[1])
                else:
                    link(first)
                link(ts(y.bitcast(I32), m.bitcast(I32), -0.5, float(0x5f3759df), ALU.mult, ALU.add))
                for j in range(3):
                    link(tt(a, y, y, ALU.mult))
                    link(stt(a, a, -0.5, m, ALU.mult, ALU.mult))
                    last = stt(y if j < 2 else dst, a, 1.5, y, ALU.add, ALU.mult)
                    if j < 2:
                        link(last)
                return last

            def x_tile(m, n_x, gain, dst_h, dst_l):
                n = n_x + m
                dve.wait_ge(x_hi, n + 1)
                stt(dst_l[:, m, :], x_t[:, m, :], vecs[:, gain + m:gain + m + 1], dst_h[:, m, :].bitcast(F32),
                    ALU.mult, ALU.subtract).then_inc(x_lo, 1)
                dve.wait_ge(x_sq, n + 1)
                if m == 0:
                    dve.tensor_copy(acc[:, :], sq[:, 0, :]).then_inc(x_acc, 1)
                else:
                    dve.wait_ge(x_acc, n)
                    tt(acc[:, :], acc[:, :], sq[:, m % 2, :], ALU.add).then_inc(x_acc, 1)

            def norm(s, row, spreads=None, width=D):
                dve.wait_ge(stat_ps, s + 1)
                last = rsqrt(bank[STAT][:, 0:NT], width, NT, r_nat[:, row, :], (stat_read, s + 1))
                if spreads is None:
                    last.then_inc(stat_nat, 1)
                    return
                link(last)
                at_least(dve, spread_ps, spreads)
                for t in range(NT):
                    last = ts(diag[:, t, :], ident[:, :], r_nat[:, row, t:t + 1], None, ALU.mult)
                last.then_inc(diag_done, 1)

            dve.memset(rows[:, :], 1.0).then_inc(rows_one, 1)
            dve.wait_ge(gate_in, 32)
            dve.tensor_copy(pos_f[0:NT, :], pos_i[0:NT, :].bitcast(I32)).then_inc(rows_pos, 1)
            dve.wait_ge(vec_ps, 1)
            dve.tensor_copy(vecs[:, :], bank[STAT][:, 0:NVEC + NT]).then_inc(vec_sb, 1)
            dve.wait_ge(vec_sb, 1)

            for m in range(KT):
                dve.wait_ge(x_ps, m + 1)
                dve.tensor_copy(x_t[:, m, :], bank[(T_X + m) % 4][:, :]).then_inc(tile_taken, 1)
                x_tile(m, 0, V_A, a_h, a_l)

            norm(0, 0, 0)
            dve.wait_ge(spread_sb, 1)
            dve.wait_ge(slab_done, L_GL + 1)
            tt(gl_t[:, :], bank[T_GL % 4][:, :], rinv_b[:, :], ALU.mult).then_inc(tile_taken, 1)
            for h in range(GH):
                dve.wait_ge(z_ps, h + 1)
                if h >= 2:
                    log_gate = (h - 2,)
                    dve.wait_ge(g_soft, h - 1)
                    link(stt(gt[:, h % 2, :], b_t[:, h - 2, :], 0.0, gt[:, h % 2, :], ALU.min, ALU.subtract))
                    dve.tensor_tensor_scan(b_t[:, h - 2, :], t2[:, 1, :], gt[:, h % 2, :], 0.0, ALU.mult, ALU.add).then_inc(g_cum, 1)
                    dve.wait_ge(g_cum, h - 1)
                link(ts(b_t[:, h, :], bank[(5, 6, 7, 5)[h]][:, :], vecs[:, V_BG + h:V_BG + h + 1], None, ALU.add))
                stt(gt[:, h % 2, :], b_t[:, h, :], -1.0, b_t[:, h, :], ALU.mult, ALU.min).then_inc(z_abs, 1)
                dve.wait_ge(slab_done, L_Q + h + 1)
                tt(q_t[:, h, :], bank[(T_Q + h) % 4][:, :], rinv_b[:, :], ALU.mult).then_inc(tile_taken, 1)
            for h in (2, 3):
                dve.wait_ge(g_soft, h + 1)
                link(stt(gt[:, h % 2, :], b_t[:, h, :], 0.0, gt[:, h % 2, :], ALU.min, ALU.subtract))
                dve.tensor_tensor_scan(b_t[:, h, :], t2[:, 1, :], gt[:, h % 2, :], 0.0, ALU.mult, ALU.add).then_inc(g_cum, 1)
            dve.wait_ge(g_cum, GH)
            for h in range(GH):
                chunks = b_t[:, h, :].rearrange("p (c n) -> p c n", n=CHUNK)
                tt(d_t[:, h, :].rearrange("p (c n) -> p c n", n=CHUNK), chunks[:, :, CHUNK - 1:CHUNK].to_broadcast([P, NCH, CHUNK]),
                   chunks, ALU.subtract).then_inc(g_diff, 1)
            for h in range(GH):
                dve.wait_ge(slab_done, L_K + h + 1)
                tt(k_ring[:, h % 2, :], bank[(T_K + h) % 4][:, :], rinv_b[:, :], ALU.mult).then_inc(tile_taken, 1)
                dve.wait_ge(g_up, h + 1)
                stt(q_t[:, h, :], q_t[:, h, :], HK ** -0.5, e_ring[:, h % 2, :], ALU.mult, ALU.mult)
                dve.wait_ge(tile_taken, T_K + h + 1)
                dve.wait_ge(g_down, h + 1)
                tt(b_t[:, h, :], b_t[:, h, :], k_ring[:, h % 2, :], ALU.mult)
                dve.wait_ge(g_end, h + 1)
                tt(d_t[:, h, :], d_t[:, h, :], k_ring[:, h % 2, :], ALU.mult).then_inc(g_prep, 1)

            n_ang = NT * HALF
            ang, high, low = t2[:, 0, 0:n_ang], t2[:, 0, n_ang:2 * n_ang], t2[:, 0, 2 * n_ang:3 * n_ang]
            prods = t1[:, :, :].rearrange("p a n -> p (a n)")[:, 0:10 * n_ang]
            whole = sq[:, :, :].rearrange("p a n -> p (a n)")[:, 0:10 * n_ang]
            for t in range(NT):
                last = ts(t2[:, 0, t * HALF:(t + 1) * HALF], inv_freq[:, :], vecs[:, NVEC + t:NVEC + t + 1], None, ALU.mult)
            link(last)
            link(dve.tensor_single_scalar(high.bitcast(I32), ang.bitcast(I32), -4096, op=ALU.bitwise_and))
            link(tt(low, ang, high, ALU.subtract))
            for j, piece_ in enumerate(TURN):
                ts(prods[:, 2 * j * n_ang:(2 * j + 1) * n_ang], high, piece_, None, ALU.mult)
                last = ts(prods[:, (2 * j + 1) * n_ang:(2 * j + 2) * n_ang], low, piece_, None, ALU.mult)
            link(last)

            def drop_whole(values_, space):
                link(ts(space, values_, MAGIC, MAGIC, ALU.add, ALU.subtract))
                link(tt(values_, values_, space, ALU.subtract))

            for _ in range(2):
                drop_whole(prods, whole)
            link(dve.tensor_reduce(ang, prods.rearrange("p (j n) -> p n j", j=10), AX_X, ALU.add))
            both = t1[:, 0, 0:2 * n_ang]
            link(ts(both[:, 0:n_ang], ang, 0.25, None, ALU.add))
            link(dve.tensor_copy(both[:, n_ang:2 * n_ang], ang))
            drop_whole(both, whole[:, 0:2 * n_ang])
            ts(both, both, 0.4999999, -0.4999999, ALU.min, ALU.max).then_inc(turns, 1)

            for c in range(2):
                dve.wait_ge(slab_done, L_V + 4 * c + 4)
                for t in range(NT):
                    ts(v_g[:, t, c * S:(c + 1) * S], bank[(T_V + t) % 4][:, :], r_nat[:, 0, t:t + 1], None, ALU.mult)\
                        .then_inc(tile_taken, 1)

            def o_final(h):
                dve.wait_ge(o_gated, h + 1)
                for e in range(2):
                    m = 2 * h + e
                    stt(sr[:, m, :], sr[:, m, :], vecs[:, V_AO + e:V_AO + e + 1], rinvo_b[:, :], ALU.mult, ALU.mult).then_inc(o_fin, 1)

            def o_split(h):
                for e in range(2):
                    m = 2 * h + e
                    dve.wait_ge(o_hi, m + 1)
                    tt(a_l[:, m, :], sr[:, m, :], a_h[:, m, :].bitcast(F32), ALU.subtract).then_inc(o_lo, 1)

            dve.wait_ge(trig_done, 1)
            for h in range(GH):
                for e in range(2):
                    m = 2 * h + e
                    dve.wait_ge(slab_done, L_R + m + 1)
                    at_least(dve, r_silu, m - 1)
                    tt(t1[:, m % 2, :], bank[(T_R + m) % 4][:, :], rinv_b[:, :], ALU.mult).then_inc(tile_taken, 1)
                    if h and not e:
                        norm(h, 3, h, HV)
                    if h and e:
                        dve.wait_ge(spread_sb, h + 1)
                        o_final(h - 1)
                dve.wait_ge(att_ps, h + 1)
                at_least(dve, o_ps, h)
                dve.copy_predicated(att[:, :, :], mask[:, :].bitcast(I32).rearrange("p (a n) -> p a n", a=1).to_broadcast([P, NT, P]),
                                    bank[5][:, :].rearrange("p (t n) -> p t n", n=P)).then_inc(att_sb, 1)
                for c in range(NCH - 1):
                    n = (NCH - 1) * h + c
                    dve.wait_ge(chunk_ps, n + 1)
                    kv = bank[KV_BANKS[c % 2]][:, 0:HV]
                    if c == 0:
                        dve.tensor_copy(state[:, 1, :], kv).then_inc(state_sb, 1)
                    else:
                        dve.wait_ge(state_sb, n)
                        stt(state[:, c + 1, :], state[:, c, :], dec[:, h, c:c + 1], kv, ALU.mult, ALU.add).then_inc(state_sb, 1)
                dve.wait_ge(o_sq, 2 * h + 2)
                tt(acc[:, :], sq[:, 0, :], sq[:, 1, :], ALU.add).then_inc(o_acc, 1)
                dve.wait_ge(r_silu, 2 * h + 2)
                for e in range(2):
                    m = 2 * h + e
                    last = tt(sr[:, m, :], sr[:, m, :], bank[O_BANKS[e]][:, :], ALU.mult)
                last.then_inc(o_gated, 1)
                if h == GH - 1:
                    for hh in range(GH - 1):
                        o_split(hh)
            norm(GH, 3, GH, HV)
            dve.wait_ge(spread_sb, GH + 1)
            o_final(GH - 1)
            o_split(GH - 1)

            def project_out(n, tile, n_x, gain):
                for m in range(KT):
                    dve.wait_ge(slab_done, n + m + 1)
                    tt(x_t[:, m, :], x_t[:, m, :], bank[(tile + m) % 4][:, :], ALU.add).then_inc(tile_taken, 1)
                    x_tile(m, n_x, gain, b_h, b_l)

            project_out(L_WO, T_WO, KT, V_F)

            def ffn_up(n, tile, hidden):
                with dve.Fori(0, FT // 2) as i:
                    for c in range(2):
                        m = hidden + 2 * i + c
                        dve.wait_ge(slab_done, n + 4 * i + 2 * c + 1)
                        tt(t1[:, c, :], bank[(tile + 2 * c) % 4][:, :], rinv_b[:, :], ALU.mult).then_inc(tile_taken, 1)
                        dve.wait_ge(slab_done, n + 4 * i + 2 * c + 2)
                        tt(t2[:, c, :], bank[(tile + 2 * c + 1) % 4][:, :], rinv_b[:, :], ALU.mult).then_inc(tile_taken, 1)
                        dve.wait_ge(tile_taken, tile + 4 * i + 2 * c + 2)
                        dve.wait_ge(f_silu, m + 1)
                        tt(t2[:, c, :], t2[:, c, :], t1[:, c, :], ALU.mult).then_inc(f_prod, 1)
                        dve.wait_ge(f_hi, m + 1)
                        tt(hid_l[:, bass.ts(2 * i + c, 1), :], t2[:, c:c + 1, :], hid_h[:, bass.ts(2 * i + c, 1), :].bitcast(F32),
                           ALU.subtract).then_inc(f_lo, 1)

            def ffn_down(n, tile, n_x, gain):
                for m in range(KT):
                    dve.wait_ge(slab_done, n + 4 * m + 4)
                    ps = bank[(tile + m) % 4][:, :]
                    if gain is not None:
                        tt(x_t[:, m, :], x_t[:, m, :], ps, ALU.add).then_inc(tile_taken, 1)
                        x_tile(m, n_x, gain, b_h, b_l)
                    else:
                        if m == 0:
                            dve.wait_ge(f_hi, 2 * FT)
                        at_least(dve, y_ps, m - 1)
                        tt(t2[:, m % 2, :], x_t[:, m, :], ps, ALU.add).then_inc(tile_taken, 1)

            dve.wait_ge(x_acc, 2 * KT)
            norm(5, 0, 5)
            dve.wait_ge(spread_sb, 6)
            ffn_up(L_UP1, T_UP1, 0)
            ffn_down(L_DN1, T_DN1, 2 * KT, V_KV)

            norm(6, 0, 6)
            for m in range(KT):
                dve.wait_ge(xb_hi, m + 1)
                stt(a_l[:, m, :], x_t[:, m, :], vecs[:, V_B + m:V_B + m + 1], a_h[:, m, :].bitcast(F32),
                    ALU.mult, ALU.subtract).then_inc(xb_lo, 1)
            for j, (kind, g_half, f) in enumerate([(kind, a, f) for kind in range(2) for a, f in ((0, 0), (1, 1), (0, 1), (1, 0))]):
                gains = rope_g[:, kind:kind + 1, g_half * HALF:(g_half + 1) * HALF].to_broadcast([P, NT, HALF])
                last = tt(rope_c[:, j, :, :], trig[:, f, :, :], gains, ALU.mult)
            link(last)
            dve.wait_ge(spread_sb, 7)

            def latent(j, gain, split_h, split_l, m):
                tile = T_C + j if j < CT else T_CQ + j - CT
                dve.wait_ge(slab_done, (L_C + j if j < CT else L_CQ + j - CT) + 1)
                at_least(dve, c_sq, j - 1)
                tt(t1[:, j % 2, :], bank[tile % 4][:, :], rinv_b[:, :], ALU.mult).then_inc(tile_taken, 1)
                dve.wait_ge(tile_taken, tile + 1)
                dve.wait_ge(c_hi, j + 1)
                stt(split_l[:, m, :], t1[:, j % 2, :], vecs[:, gain + m:gain + m + 1], split_h[:, m, :].bitcast(F32),
                    ALU.mult, ALU.subtract).then_inc(c_lo, 1)
                dve.wait_ge(c_sq, j + 1)
                if m == 0:
                    if j:
                        dve.wait_ge(stat_ps, 8)
                    dve.tensor_copy(acc[:, :], sq[:, j % 2, :]).then_inc(c_acc, 1)
                else:
                    dve.wait_ge(c_acc, j)
                    tt(acc[:, :], acc[:, :], sq[:, j % 2, :], ALU.add).then_inc(c_acc, 1)

            def rotate(src, dst, table, space, shape):
                x1, x2 = src
                y1, y2 = dst
                cs = [rope_c[:, table + j, :, :] for j in range(4)]
                if shape is not None:
                    cs = [c.rearrange("p t (a j) -> p t a j", a=1).to_broadcast(shape) for c in cs]
                tt(space[0], x1, cs[0], ALU.mult)
                tt(space[1], x2, cs[1], ALU.mult)
                tt(space[2], x1, cs[2], ALU.mult)
                link(tt(space[3], x2, cs[3], ALU.mult))
                tt(y1, space[0], space[1], ALU.subtract)
                return tt(y2, space[2], space[3], ALU.add)

            for j in range(CT):
                latent(j, V_CL, c_h, c_l, j)
            dve.wait_ge(slab_done, L_KR + 1)
            for t in range(NT):
                last = ts(kr[:, 0, t, :], bank[T_KR % 4][:, t * ROPE:(t + 1) * ROPE], r_nat[:, 0, t:t + 1], None, ALU.mult)
            last.then_inc(tile_taken, 1)
            dve.wait_ge(tile_taken, T_KR + 1)
            link(tt(kr[:, 1, :, :], kr[:, 0, :, :], kr[:, 0, :, :], ALU.mult))
            link(dve.tensor_reduce(kr_ss[:, :], kr[:, 1, :, :], AX_X, ALU.add))
            space = [kr[:, 2 + j // 2, :, (j % 2) * HALF:(j % 2 + 1) * HALF] for j in range(4)]
            link(rotate((kr[:, 0, :, 0:HALF], kr[:, 0, :, HALF:ROPE]), (kr[:, 1, :, 0:HALF], kr[:, 1, :, HALF:ROPE]), 4, space, None))
            for j in range(QT):
                latent(CT + j, V_QL, cq_h, cq_l, j)
                if j == 0:
                    norm(7, 1, None, KVRANK)
            norm(8, 2, None, QRANK)

            wide = [P, NT, HG, HALF]

            def key_rows(gi):
                dve.wait_ge(ksq, gi + 1)
                sums = sc_next[:, :]
                link(dve.tensor_reduce(nw[:, 1, :], sq_g[:, :, 0:NOPE], AX_X, ALU.add))
                link(tt(nw[:, 1, :].rearrange("p (t h) -> p t h", h=HG), nw[:, 1, :].rearrange("p (t h) -> p t h", h=HG),
                        kr_ss[:, :].rearrange("p (t a) -> p t a", a=1).to_broadcast([P, NT, HG]), ALU.add))
                link(rsqrt(nw[:, 1, :], QK, UNITS, stat[:, 3, :]))
                factors = stat[:, 3, :].rearrange("p (t h) -> p t h", h=HG)
                for t in range(NT):
                    f = factors[:, t, :].rearrange("p (h a) -> p h a", a=1)
                    rows_ = k_n[:, HG * t:HG * (t + 1), :]
                    tt(rows_[:, :, 0:NOPE], kv_n[:, t, :].rearrange("p (h n) -> p h n", n=P)[:, :, 0:NOPE], f.to_broadcast([P, HG, NOPE]), ALU.mult)
                    last = tt(rows_[:, :, NOPE:QK], kr[:, 1, t:t + 1, :].to_broadcast([P, HG, ROPE]), f.to_broadcast([P, HG, ROPE]), ALU.mult)
                last.then_inc(k_rows, 1)

            def query_rows(gi):
                dve.wait_ge(qsq, gi + 1)
                link(dve.tensor_reduce(nw[:, 1, :], sq_g[:, :, :], AX_X, ALU.add))
                link(rsqrt(nw[:, 1, :], QK, UNITS, stat[:, 3, :]))
                ts(sc_next[:, :], stat[:, 3, :], QK ** -0.5, None, ALU.mult)
                rows_ = q_n[:, :, :].rearrange("p (t h) n -> p t h n", h=HG)
                space_ = [sq_g[:, :, j * HALF:(j + 1) * HALF].rearrange("p (t h) n -> p t h n", h=HG) for j in range(4)]
                halves = (rows_[:, :, :, NOPE:NOPE + HALF], rows_[:, :, :, NOPE + HALF:QK])
                rotate(halves, halves, 0, space_, wide).then_inc(q_rows, 1)

            def bias(v, gi):
                h, t = v // NT % HG, v % NT
                n = 16 * gi + v
                col = v % UNITS
                dve.wait_ge(s_ps, n + 1)
                link(dve.memset(bank[t][0:CHUNK, t * P + CHUNK:(t + 1) * P], NEG))
                link(dve.tensor_reduce(stat[:, 0, col:col + 1], bank[t][:, 0:(t + 1) * P], AX_X, ALU.max))
                ts(stat[:, 1, col:col + 1], stat[:, 0, col:col + 1], sc[:, HG * t + h:HG * t + h + 1], -1.0, ALU.mult, ALU.mult)\
                    .then_inc(s_bias, 1)

            def take_scale(gi):
                at_least(dve, p_exp, 16 * gi)
                dve.wait_ge(q_rows, gi + 1)
                link(dve.tensor_copy(sc[:, :], sc_next[:, :]))

            def turned(u, gi):
                if u % 2:
                    dve.wait_ge(pt_ps, 16 * gi + u + 1)
                    at_least(dve, pv_ps, 16 * gi + u - 1)
                    w = (u % NT + 1) * P
                    dve.tensor_copy(prob_t[:, 1, 0:w], bank[PT_BANKS[1]][:, 0:w]).then_inc(pt_sb[1], 1)

            def head_out(h, gi):
                dve.wait_ge(pv_ps, 16 * gi + NT * (h + 1))
                cols = slice(NT * h, NT * (h + 1))
                link(dve.reciprocal(stat[:, 3, cols], stat[:, 2, cols]))
                if h % 2 == 0:
                    at_least(dve, ot_ps, 2 * gi + h // 2)
                tt(o_n[:, :, (h % 2) * MV:(h % 2 + 1) * MV], bank[PV_BANK][:, 0:NT * MV].rearrange("p (t n) -> p t n", n=MV),
                   stat[:, 3, cols].rearrange("p (t a) -> p t a", a=1).to_broadcast([P, NT, MV]), ALU.mult).then_inc(o_nat, 1)

            def outputs(pair, gi):
                dve.wait_ge(ot_hi, 2 * gi + pair + 1)
                m = 2 * gi + pair
                cut = slice(m, m + 1) if isinstance(gi, int) else bass.ts(m, 1)
                tt(a_l[:, cut, :], bank[PIECE][:, :].rearrange("p (a n) -> p a n", a=1), a_h[:, cut, :].bitcast(F32),
                   ALU.subtract).then_inc(ot_lo, 1)

            def take_values(gi):
                at_least(dve, pv_ps, 16 * gi)
                dve.wait_ge(piece_taken, 16 * gi + NT)
                dve.tensor_copy(v_cur[:, :, :, :], kv_n[:, :, :].rearrange("p t (h n) -> p t h n", n=P)[:, :, :, NOPE:P]).then_inc(v_ready, 1)

            def group(gi, first, more):
                for u in range(UNITS):
                    if u % NT == 0 and not (first and u == 0):
                        head_out((u // NT - 1) % HG, gi if u else gi - 1)
                    if u == 0:
                        take_values(gi)
                    if u == 2 and not first:
                        outputs(1, gi - 1)
                    if u == 10:
                        outputs(0, gi)
                    turned(u, gi)
                    if u + AHEAD == UNITS and more:
                        take_scale(gi + 1)
                    if u + AHEAD < UNITS or more:
                        bias(u + AHEAD, gi)
                    if u == 4 and more:
                        key_rows(gi + 1)
                    if u == 8 and more:
                        query_rows(gi + 1)

            key_rows(0)
            query_rows(0)
            take_scale(0)
            for v in range(AHEAD):
                bias(v, 0)
            group(0, True, True)
            with dve.Fori(1, GROUPS - 1) as g:
                link.enter(g, 2 * UNITS + HG + 13 + 13 + 1, 1)
                group(g, False, True)
            link.leave(GROUPS - 2)
            group(GROUPS - 1, False, False)
            head_out(HG - 1, GROUPS - 1)
            outputs(1, GROUPS - 1)

            project_out(L_WOB, T_WOB, 3 * KT, V_F + KT)
            norm(9, 0, 7)
            dve.wait_ge(spread_sb, 8)
            ffn_up(L_UP2, T_UP2, FT)
            ffn_down(L_DN2, T_DN2, 0, None)


_INS = ['x', 'positions', 'a_norm', 'a_w_in', 'a_w_gate_up', 'a_b_gate', 'a_out_norm', 'a_w_out',
        'b_norm', 'b_w_dq', 'b_q_latent_norm', 'b_w_uq', 'b_q_norm', 'b_w_out',
        'kv_norm', 'kv_w_down', 'kv_latent_norm', 'kv_w_up', 'k_norm', 'f_norm', 'f_w_in', 'f_w_out']
_OUTS = [((1, S, D), 'float32')]


def kernel(**inputs):
    import numpy as _np
    import concourse.bacc as _bacc
    from concourse import mybir as _mybir
    from concourse.bass_utils import run_bass_kernel_spmd as _run

    nc = _bacc.Bacc("TRN2", target_bir_lowering=False, num_devices=1)
    arrays, args = {}, []
    for name in _INS:
        a = _np.ascontiguousarray(inputs[name])
        arrays[f"in_{name}_dram"] = a
        args.append(nc.dram_tensor(f"in_{name}_dram", a.shape, _mybir.dt.from_np(a.dtype), kind="ExternalInput").ap())
    for i, (shape, dtype) in enumerate(_OUTS):
        dt = _mybir.dt.from_np(_np.dtype(dtype))
        args.append(nc.dram_tensor(f"out_{i}_dram", shape, dt, kind="ExternalOutput").ap())
    trunk(nc, *args)
    r = _run(nc, [arrays], core_ids=[0])
    return r.results[0]["out_0_dram"]
```

```python
from contextlib import ExitStack

import numpy as np

import concourse.bass as bass
from concourse import mybir

ALU = mybir.AluOpType
ACT = mybir.ActivationFunctionType
F32 = mybir.dt.float32
F32R = mybir.dt.float32r
I32 = mybir.dt.int32
AX_X = mybir.AxisListType.X

P = 128
D = 1024
S = 512
CHUNK = 64
EPS = 1e-6
KT = D // P
NT = S // P
NCH = S // CHUNK

GH, HK, HV, GRANK, TAU = 4, 128, 256, 16, 16.0
DK, DV = GH * HK, GH * HV

MH, NOPE, ROPE, QK, MV = 16, 64, 32, 96, 64
HALF = ROPE // 2
QRANK, KVRANK = 384, 256
QT, CT = QRANK // P, KVRANK // P
THETA = 10000.0
GROUPS = 4
HG = MH // GROUPS
UNITS = HG * NT
AHEAD = 3

FF = -(-8 * D // (3 * 256)) * 256
FT = FF // P
DOWN = ((0, 6), (6, 6), (12, 5), (17, 5))

RING = 4
SLAB = 1024
NEG = -1.0e30
MAGIC = 1.5 * 2.0 ** 23

L_GL = 0
L_Q = L_GL + 1
L_K = L_Q + GH
L_V = L_K + GH
L_R = L_V + 8
L_WO = L_R + KT
L_UP1 = L_WO + KT
L_DN1 = L_UP1 + 2 * FT
L_CQ = L_DN1 + 4 * KT
L_C = L_CQ + QT
L_KR = L_C + CT
L_GRP = L_KR + 1
L_WOB = L_GRP + 4 * GROUPS
L_UP2 = L_WOB + KT
L_DN2 = L_UP2 + 2 * FT
L_END = L_DN2 + 4 * KT

T_X = 0
T_GL = T_X + KT
T_Q = T_GL + 1
T_K = T_Q + GH
T_V = T_K + GH
T_R = T_V + 8
T_WO = T_R + KT
T_UP1 = T_WO + KT
T_DN1 = T_UP1 + 2 * FT
T_CQ = T_DN1 + KT
T_C = T_CQ + QT
T_KR = T_C + CT
T_WOB = T_KR + 1
T_UP2 = T_WOB + KT
T_DN2 = T_UP2 + 2 * FT

V_A, V_BG, V_AO, V_B, V_QL, V_KV, V_CL, V_F, V_QN, V_KN = 0, 8, 12, 14, 22, 25, 33, 35, 51, 52
NVEC = 53

TURN = [int(h, 16) / 2.0 ** (12 * (j + 1)) / 4.0 for j, h in enumerate(("A2F", "983", "6E4", "E44", "152"))]

PIECES = ([("q", t) for t in range(NT)] + [("kv", t) for t in range(NT)]
          + [("qt", 0), ("qt", 1), ("qt", 2), ("kt", 0), ("kt", 1), ("kt", 2), ("kt", 3), ("qt", 3)])
COUNTED = [0]
for _kind, _t in PIECES:
    COUNTED.append(COUNTED[-1] + (not (_kind in ("kv", "q") and _t == NT - 1)))
NCOUNTED = COUNTED[-1]


def group_slab(c):
    return QT * 2 * QK if c < 2 else CT * 2 * P


class Links:

    def __init__(self, engine, sem):
        self.engine, self.sem, self.n, self.off = engine, sem, 0, 0

    def __call__(self, instruction):
        instruction.then_inc(self.sem, 1)
        self.n += 1
        self.engine.wait_ge(self.sem, self.off + self.n)

    def enter(self, i, per, first=0):
        self.start, self.per, self.first, self.off = self.n, per, first, (i - first) * per

    def leave(self, times):
        assert self.n - self.start == self.per, (self.n - self.start, self.per)
        self.n, self.off = self.start + self.per * times, 0


def trunk(nc, x, positions, a_norm, a_w_in, a_w_gate_up, a_b_gate, a_out_norm, a_w_out,
          b_norm, b_w_dq, b_q_latent_norm, b_w_uq, b_q_norm, b_w_out,
          kv_norm, kv_w_down, kv_latent_norm, kv_w_up, k_norm, f_norm, f_w_in, f_w_out, out):
    ctx = ExitStack()
    with ctx:
        def sb(name, shape, dt=F32, stack=ctx):
            return stack.enter_context(nc.sbuf_tensor(name, shape, dt))

        def sem(name):
            return ctx.enter_context(nc.semaphore(name))

        x_t = sb("x_t", [P, KT, S])
        w_raw = sb("w_raw", [P, RING, SLAB])
        w_h = sb("w_h", [P, RING, SLAB], F32R)
        w_l = sb("w_l", [P, RING, SLAB], F32R)
        ident = sb("ident", [P, P])
        ones = sb("ones", [P, P])
        acc = sb("acc", [P, S])
        sq = sb("sq", [P, 2, S])
        rinv_b = sb("rinv_b", [P, S])
        rinvo_b = sb("rinvo_b", [P, S])
        t1 = sb("t1", [P, 2, S])
        t2 = sb("t2", [P, 2, S])
        diag = sb("diag", [P, NT, P])
        vecs = sb("vecs", [P, NVEC + NT])
        r_nat = sb("r_nat", [P, 4, NT])
        nw = sb("nw", [P, 3, UNITS])
        dec = sb("dec", [P, GH, NCH])
        q_scale = sb("q_scale", [P, UNITS])
        k_scale = sb("k_scale", [P, UNITS])
        stat = sb("stat", [P, 3, UNITS])

        rope_g = sb("rope_g", [P, 2, ROPE])
        kr_ss = sb("kr_ss", [P, NT])
        trig = sb("trig", [P, 2, NT, HALF])
        inv_freq = sb("inv_freq", [P, HALF])

        def overlay(tag, behind_hi, behind_lo, over_b):
            made = []
            with ExitStack() as stack:
                for n, (group, room) in enumerate(((behind_hi, (FT - KT) * S), (behind_lo, (FT - KT) * S), (over_b, 2 * KT * S))):
                    if n < 2:
                        sb(f"{tag}_under{n}", [P, KT * S], F32, stack)
                    used = 0
                    for name, shape, *dt in group:
                        made.append(sb(f"{tag}_{name}", shape, dt[0] if dt else F32, stack))
                        used += int(np.prod(shape[1:]))
                    assert used <= room, (tag, n, used, room)
                    if used < room:
                        sb(f"{tag}_rest{n}", [P, room - used], F32, stack)
            return made

        (b_t, d_t, q_t, att, k_end, v_g, state, k_ring, sr, e_ring, gt, gl_t, w_gate, mask, rows, pos_i, pos_f) = overlay(
            "gla",
            [("b_t", [P, GH, S]), ("d_t", [P, GH, S]), ("q_t", [P, GH, S]), ("att", [P, NT, P]), ("k_end", [P, NT, HK])],
            [("v", [P, NT, DV]), ("state", [P, NCH, HV]), ("k_ring", [P, 2, S])],
            [("sr", [P, KT, S]), ("e_ring", [P, 2, S]), ("gt", [P, 2, S]), ("gl_t", [P, S]), ("w_gate", [P, DK]),
             ("mask", [P, P]), ("rows", [P, P]), ("pos_i", [P, P]), ("pos_f", [P, P])])
        (kv_n, q_n, k_n, sq_g, rope_c, v_cur, c_h, c_l, cq_h, cq_l, kr, o_n, k_tt, q_tt, prob, prob_t) = overlay(
            "mla",
            [("kv_n", [P, NT, HG * P]), ("q_n", [P, UNITS, QK]), ("k_n", [P, UNITS, QK]), ("sq_g", [P, UNITS, QK]),
             ("rope_c", [P, 8, NT, HALF])],
            [("v_cur", [P, NT, HG, MV]), ("c_h", [P, CT, S], F32R), ("c_l", [P, CT, S], F32R),
             ("cq_h", [P, QT, S], F32R), ("cq_l", [P, QT, S], F32R), ("kr", [P, 4, NT, ROPE]), ("o_n", [P, NT, P])],
            [("k_tt", [P, HG, S]), ("q_tt", [P, HG, S]), ("prob", [P, NT, S]), ("prob_t", [P, 2, S])])
        hid_h = sb("hid_h", [P, FT, S], F32R)
        hid_l = sb("hid_l", [P, FT, S], F32R)
        b_h = sb("b_h", [P, KT, S], F32R)
        b_l = sb("b_l", [P, KT, S], F32R)
        a_h, a_l = hid_h[:, 0:KT, :], hid_l[:, 0:KT, :]

        bank = [ctx.enter_context(nc.psum_tensor(f"bank{n}", [P, S], F32)) for n in range(8)]
        STAT, KV_BANKS, O_BANKS = 4, (4, 5), (6, 7)
        PT_BANK, PV_BANKS, PIECE = 4, (5, 6), 7
        FIRST_PIECES = (5, 6, 7)
        Y_BANKS = (5, 6)

        x_in, vec_in, gate_in = sem("x_in"), sem("vec_in"), sem("gate_in")
        w_in = [sem(f"w_in{n}") for n in range(RING)]
        w_hi, w_lo = sem("w_hi"), sem("w_lo")
        slab_done = sem("slab_done")
        tile_taken = sem("tile_taken")
        const_done, pool_step, w_gate_zero = sem("const_done"), sem("pool_step"), sem("w_gate_zero")
        rows_one, rows_pos = sem("rows_one"), sem("rows_pos")
        vec_ps, vec_sb = sem("vec_ps"), sem("vec_sb")
        x_ps = sem("x_ps")
        x_hi, x_sq, x_lo, x_acc = sem("x_hi"), sem("x_sq"), sem("x_lo"), sem("x_acc")
        stat_ps, stat_read, stat_nat = sem("stat_ps"), sem("stat_read"), sem("stat_nat")
        diag_done, spread_ps, spread_sb = sem("diag_done"), sem("spread_ps"), sem("spread_sb")
        dve_step, act_step = sem("dve_step"), sem("act_step")
        z_ps, z_abs, g_soft, g_cum, g_diff = sem("z_ps"), sem("z_abs"), sem("g_soft"), sem("g_cum"), sem("g_diff")
        g_up, g_down, g_end = sem("g_up"), sem("g_down"), sem("g_end")
        g_prep, r_silu = sem("g_prep"), sem("r_silu")
        kend_ps, kend_sb, att_ps, att_sb = sem("kend_ps"), sem("kend_sb"), sem("att_ps"), sem("att_sb")
        chunk_ps, state_sb = sem("chunk_ps"), sem("state_sb")
        o_ps, o_sq, o_acc, o_gated = sem("o_ps"), sem("o_sq"), sem("o_acc"), sem("o_gated")
        o_fin, o_hi, o_lo = sem("o_fin"), sem("o_hi"), sem("o_lo")
        f_silu, f_prod, f_hi, f_lo = sem("f_silu"), sem("f_prod"), sem("f_hi"), sem("f_lo")
        xb_hi, xb_lo = sem("xb_hi"), sem("xb_lo")
        c_sq, c_hi, c_lo, c_acc = sem("c_sq"), sem("c_hi"), sem("c_lo"), sem("c_acc")
        turns, trig_done = sem("turns"), sem("trig_done")
        piece_ps, piece_taken = sem("piece_ps"), sem("piece_taken")
        ksq, qsq, k_rows, q_rows = sem("ksq"), sem("qsq"), sem("k_rows"), sem("q_rows")
        k_sum, q_sum, k_fac, q_fac = sem("k_sum"), sem("q_sum"), sem("k_fac"), sem("q_fac")
        mask_rows = sem("mask_rows")
        v_ready, pool_link = sem("v_ready"), sem("pool_link")
        s_ps, s_bias, p_exp = sem("s_ps"), sem("s_bias"), sem("p_exp")
        pt_ps, pt_sb, pv_ps = sem("pt_ps"), [sem("pt_sb0"), sem("pt_sb1")], sem("pv_ps")
        o_nat, ot_ps, ot_hi, ot_lo = sem("o_nat"), sem("ot_ps"), sem("ot_hi"), sem("ot_lo")
        y_ps, y_sb = sem("y_ps"), sem("y_sb")
        y_out = [sem("y_out0"), sem("y_out1")]

        def at_least(eng, s, value):
            if not isinstance(value, int) or value > 0:
                eng.wait_ge(s, value)

        block = ctx.enter_context(nc.Block())

        @block.sync
        def _(sp):
            x_rows = x.rearrange("b (t p) n -> p (b t) n", p=P)
            for t in range(NT):
                sp.dma_start(v_g[:, t, :], x_rows[:, t, :]).then_inc(x_in, 16)

            def load(n, off, src, cols):
                k = src.shape[1]
                if not (isinstance(off, int) and n + off < RING):
                    sp.wait_ge(w_lo, n + off - RING + 1)
                sp.dma_start(w_raw[:, n % RING, 0:k * cols].rearrange("p (k c) -> p k c", c=cols), src)\
                    .then_inc(w_in[n % RING], 16)

            def by_rows(w):
                return w.rearrange("(k p) n -> p k n", p=P)

            def columns(n, w, m0, count):
                for m in range(count):
                    load(n + m, 0, by_rows(w)[:, :, (m0 + m) * P:(m0 + m + 1) * P], P)

            w = a_w_in[0]
            gla_in = by_rows(w)
            load(L_GL, 0, gla_in[:, :, 2 * DK + 2 * DV + GRANK - P:2 * DK + 2 * DV + GRANK], P)
            columns(L_Q, w, 0, GH)
            columns(L_K, w, GH, GH)
            for c in range(2):
                for j in range(4):
                    load(L_V + 4 * c + j, 0, gla_in[:, 2 * j:2 * j + 2, 2 * DK + c * S:2 * DK + (c + 1) * S], S)
            columns(L_R, w, (2 * DK + DV) // P, KT)
            columns(L_WO, a_w_out[0], 0, KT)

            def ffn(n_up, n_dn, layer):
                up, dn = by_rows(f_w_in[layer]), by_rows(f_w_out[layer])
                with sp.Fori(0, FT // 2) as i:
                    for c in range(4):
                        src = up[:, :, (c % 2) * FF:(c % 2 + 1) * FF]
                        load(n_up + c, 4 * i, src[:, :, bass.ts(2 * i + c // 2, P)], P)
                with sp.Fori(0, KT) as i:
                    for c, (k, kn) in enumerate(DOWN):
                        load(n_dn + c, 4 * i, dn[:, k:k + kn, bass.ts(i, P)], P)

            ffn(L_UP1, L_DN1, 0)
            columns(L_CQ, b_w_dq[0], 0, QT)
            columns(L_C, kv_w_down, 0, CT)
            load(L_KR, 0, by_rows(kv_w_down)[:, :, KVRANK:KVRANK + ROPE], ROPE)
            with sp.Fori(0, GROUPS) as g:
                for c in range(2):
                    load(L_GRP + c, 4 * g, by_rows(b_w_uq[0])[:, :, bass.ts(2 * g + c, 2 * QK)], 2 * QK)
                for c in range(2):
                    load(L_GRP + 2 + c, 4 * g, by_rows(kv_w_up)[:, :, bass.ts(2 * g + c, 2 * P)], 2 * P)
            columns(L_WOB, b_w_out[0], 0, KT)
            ffn(L_UP2, L_DN2, 1)

        @block.gpsimd
        def _(pool):
            pool.memset(ident[:, :], 0.0).then_inc(pool_step, 1)
            pool.memset(mask[:, :], 1.0).then_inc(pool_step, 1)
            pool.memset(w_gate[:, :], 0.0).then_inc(w_gate_zero, 1)
            pool.memset(ones[:, :], 1.0)
            pool.memset(att[:, :, :], 0.0)
            for j in range(HALF):
                pool.memset(inv_freq[:, j:j + 1], float(np.float32(THETA ** (-j / HALF))))
            pool.memset(t2[:, 1, :], 1.0).then_inc(pool_step, 1)
            pool.wait_ge(pool_step, 3)
            pool.affine_select(out=ident[:, :], in_=ident[:, :], compare_op=ALU.not_equal, fill=1.0, base=0,
                               pattern=[[-1, P]], channel_multiplier=1).then_inc(pool_step, 1)
            pool.affine_select(out=mask[:, :], in_=mask[:, :], compare_op=ALU.is_ge, fill=0.0, base=0,
                               pattern=[[1, P]], channel_multiplier=-1).then_inc(pool_step, 1)
            pool.memset(t2[:, 1, :].rearrange("p (c n) -> p c n", n=CHUNK)[:, :, 0:1], 0.0).then_inc(pool_step, 1)
            pool.wait_ge(pool_step, 6)
            pool.memset(mask[0:CHUNK, CHUNK:P], 0.0).then_inc(const_done, 1)

            def lo(n, off, size):
                pool.wait_ge(w_hi, n + off + 1)
                s = n % RING
                pool.tensor_tensor(w_l[:, s, 0:size], w_raw[:, s, 0:size], w_h[:, s, 0:size].bitcast(F32),
                                   ALU.subtract).then_inc(w_lo, 1)

            def run(n, size, first, count):
                with pool.Fori(0, count // 4) as i:
                    for c in range(4):
                        lo(n + c, 4 * i, size)

            def down(n):
                with pool.Fori(0, KT) as i:
                    for c, (_, kn) in enumerate(DOWN):
                        lo(n + c, 4 * i, kn * P)

            lo(L_GL, 0, SLAB)
            run(L_Q, SLAB, 0, L_DN1 - L_Q)
            down(L_DN1)
            for n in range(L_CQ, L_GRP):
                lo(n, 0, KT * ROPE if n == L_KR else SLAB)
            for c in range(4):
                lo(L_GRP + c, 0, group_slab(c))

            link = Links(pool, pool_link)
            by_head = [w[:, :, :].rearrange("p (t h) n -> p t h n", h=HG) for w in (q_n, k_n)]

            def factors(scale, h):
                return scale[:, :].rearrange("p (t h) -> p t h", h=HG)[:, :, h:h + 1]

            def query_rows(gi):
                pool.wait_ge(qsq, gi + 1)
                x1, x2 = (by_head[0][:, :, :, NOPE + j * HALF:NOPE + (j + 1) * HALF] for j in range(2))
                space = [t1[:, j // 2, (j % 2) * (S // 2):(j % 2 + 1) * (S // 2)].rearrange("p (t h n) -> p t h n", h=HG, n=HALF)
                         for j in range(4)]
                for j, x_half in enumerate((x1, x2, x1, x2)):
                    last = pool.tensor_tensor(space[j], x_half,
                                              rope_c[:, j, :, :].rearrange("p t (a n) -> p t a n", a=1).to_broadcast([P, NT, HG, HALF]),
                                              ALU.mult)
                link(last)
                pool.tensor_tensor(x1, space[0], space[1], ALU.subtract)
                link(pool.tensor_tensor(x2, space[2], space[3], ALU.add))
                pool.wait_ge(q_fac, gi + 1)
                for h in range(HG):
                    rows_ = by_head[0][:, :, h, :]
                    pool.tensor_tensor(rows_, rows_, factors(q_scale, h).to_broadcast([P, NT, QK]), ALU.mult).then_inc(q_rows, 1)

            def key_rows(gi):
                pool.wait_ge(k_fac, gi + 1)
                for h in range(HG):
                    rows_ = by_head[1][:, :, h, :]
                    pool.tensor_tensor(rows_[:, :, 0:NOPE], kv_n[:, :, h * P:h * P + NOPE],
                                       factors(k_scale, h).to_broadcast([P, NT, NOPE]), ALU.mult)
                    pool.tensor_tensor(rows_[:, :, NOPE:QK], kr[:, 1, :, :], factors(k_scale, h).to_broadcast([P, NT, ROPE]),
                                       ALU.mult).then_inc(k_rows, 1)

            pool.wait_ge(c_lo, QT + CT)
            with pool.Fori(0, GROUPS - 1) as g:
                link.enter(g, 2)
                query_rows(g)
                for c in range(2):
                    lo(L_GRP + 4 + c, 4 * g, group_slab(c))
                key_rows(g)
                for c in range(2, 4):
                    lo(L_GRP + 4 + c, 4 * g, group_slab(c))
            link.leave(GROUPS - 1)
            query_rows(GROUPS - 1)
            for c in range(2):
                lo(L_WOB + c, 0, SLAB)
            key_rows(GROUPS - 1)
            for c in range(2, 4):
                lo(L_WOB + c, 0, SLAB)
            run(L_WOB + 4, SLAB, 0, L_DN2 - L_WOB - 4)
            down(L_DN2)

        @block.tensor
        def _(pe):
            def mm(o, lhs, rhs, start, stop):
                return pe.matmul(o, lhs, rhs, start=start, stop=stop)

            def mm3(o, lhs_h, lhs_l, rhs_h, rhs_l, start, stop):
                mm(o, lhs_h, rhs_l, start, False)
                mm(o, lhs_l, rhs_h, False, False)
                return mm(o, lhs_h, rhs_h, False, stop)

            def slab(n, cols):
                s = n % RING
                return [w[:, s, 0:SLAB // cols * cols].rearrange("p (k c) -> p k c", c=cols) for w in (w_h, w_l)]

            def wait_slab(n, off=0):
                pe.wait_ge(w_lo, n + off + 1)

            def wait_tile(tile, off=0):
                at_least(pe, tile_taken, tile + off - 3)

            def column_tile(n, tile, act_h, act_l, off=0, tile_off=None, parts=None):
                tile_off = off if tile_off is None else tile_off
                wait_slab(n, off)
                wait_tile(tile, tile_off)
                wh, wl = slab(n, P)
                for k in range(KT):
                    if parts is not None:
                        pe.wait_ge(parts[0], parts[1] + k + 1)
                    last = mm3(bank[tile % 4][:, :], wh[:, k, :], wl[:, k, :], act_h[:, k, :], act_l[:, k, :],
                               k == 0, k == KT - 1)
                last.then_inc(slab_done, 1)

            def stat_sum(s, spreads, ready, count, squares=acc, col=0):
                pe.wait_ge(ready, count)
                at_least(pe, stat_read, s)
                at_least(pe, spread_sb, spreads)
                for t in range(NT):
                    last = mm(bank[STAT][:, t:t + 1], squares[:, t * P:(t + 1) * P], ones[:, 0:1], True, True)
                last.then_inc(stat_ps, 1)

            def stat_spread(b):
                pe.wait_ge(diag_done, b + 1)
                for t in range(NT):
                    last = mm(bank[STAT][:, t * P:(t + 1) * P], ones[:, :], diag[:, t, :], True, True)
                last.then_inc(spread_ps, 1)

            pe.wait_ge(const_done, 1)
            pe.wait_ge(vec_in, 16 * 12)
            pe.wait_ge(rows_pos, 1)
            pe.transpose(bank[STAT][:, 0:NVEC], rows[0:NVEC, :], ident[0:NVEC, 0:NVEC])
            pe.transpose(bank[STAT][:, NVEC:NVEC + NT], pos_f[0:NT, :], ident[0:NT, 0:NT]).then_inc(vec_ps, 1)
            pe.wait_ge(x_in, 16 * NT)
            for m in range(KT):
                wait_tile(T_X + m)
                for t in range(NT):
                    last = pe.transpose(bank[(T_X + m) % 4][:, t * P:(t + 1) * P], v_g[:, t, m * P:(m + 1) * P], ident[:, :])
                last.then_inc(x_ps, 1)

            column_tile(L_GL, T_GL, a_h, a_l, parts=(x_lo, 0))
            pe.wait_ge(vec_sb, 1)
            stat_sum(0, 0, x_acc, KT)
            column_tile(L_Q, T_Q, a_h, a_l)
            stat_spread(0)
            column_tile(L_Q + 1, T_Q + 1, a_h, a_l)
            pe.wait_ge(tile_taken, T_GL + 1)
            pe.wait_ge(gate_in, 32)
            for h in range(GH):
                if h == 3:
                    pe.wait_ge(z_abs, 1)
                mm(bank[(5, 6, 7, 5)[h]][:, :], w_gate[:, h * HK:(h + 1) * HK], gl_t[:, :], True, True).then_inc(z_ps, 1)
            for h in range(2, GH):
                column_tile(L_Q + h, T_Q + h, a_h, a_l)
            for h in range(GH):
                column_tile(L_K + h, T_K + h, a_h, a_l)
            for c in range(2):
                for j in range(4):
                    wait_slab(L_V + 4 * c + j)
                    wh, wl = slab(L_V + 4 * c + j, S)
                    for t in range(NT):
                        if j == 0:
                            wait_tile(T_V + 4 * c + t)
                        for k in range(2):
                            kk = 2 * j + k
                            last = mm3(bank[(T_V + t) % 4][:, :], a_h[:, kk, t * P:(t + 1) * P], a_l[:, kk, t * P:(t + 1) * P],
                                       wh[:, k, :], wl[:, k, :], kk == 0, kk == KT - 1)
                    last.then_inc(slab_done, 1)

            def gla_head(h):
                pe.wait_ge(g_prep, h + 1)
                if h == 0:
                    pe.wait_ge(z_abs, GH)
                    pe.wait_ge(spread_sb, 1)
                for t in range(NT):
                    last = pe.transpose(bank[4][:, t * P:(t + 1) * P], d_t[:, h, t * P:(t + 1) * P], ident[:, :])
                last.then_inc(kend_ps, 1)
                for t in range(NT):
                    last = mm(bank[5][:, t * P:(t + 1) * P], b_t[:, h, t * P:(t + 1) * P], q_t[:, h, t * P:(t + 1) * P], True, True)
                last.then_inc(att_ps, 1)
                for c in range(NCH - 1):
                    if c == 0:
                        pe.wait_ge(kend_sb, h + 1)
                        pe.wait_ge(tile_taken, T_V + 8)
                    if c == 1:
                        pe.wait_ge(att_sb, h + 1)
                    if c >= 2:
                        pe.wait_ge(state_sb, (NCH - 1) * h + c - 1)
                    half = slice(CHUNK * (c % 2), CHUNK * (c % 2 + 1))
                    mm(bank[KV_BANKS[c % 2]][:, 0:HV], k_end[half, c // 2, :], v_g[half, c // 2, h * HV:(h + 1) * HV], True, True)\
                        .then_inc(chunk_ps, 1)
                at_least(pe, o_gated, h)
                for t in range(NT):
                    for e in range(2):
                        cols = slice(h * HV + e * P, h * HV + (e + 1) * P)
                        o = bank[O_BANKS[e]]
                        last = mm(o[:, t * P:(t + 1) * P], v_g[:, t, cols], att[:, t, :], True, False)
                        for c in (2 * t, 2 * t + 1):
                            if c:
                                pe.wait_ge(state_sb, (NCH - 1) * h + c)
                                last = mm(o[:, c * CHUNK:(c + 1) * CHUNK], state[:, c, e * P:(e + 1) * P],
                                          q_t[:, h, c * CHUNK:(c + 1) * CHUNK], False, c == 2 * t + 1)
                last.then_inc(o_ps, 1)

            for h in range(GH):
                column_tile(L_R + 2 * h, T_R + 2 * h, a_h, a_l)
                if h:
                    stat_sum(h, h, o_acc, h)
                column_tile(L_R + 2 * h + 1, T_R + 2 * h + 1, a_h, a_l)
                if h:
                    stat_spread(h)
                    pe.wait_ge(spread_sb, h + 1)
                gla_head(h)
            stat_sum(GH, GH, o_acc, GH)
            stat_spread(GH)

            def project_out(n, tile, ready, count):
                with pe.Fori(0, KT // 4) as i:
                    for c in range(4):
                        column_tile(n + c, tile + c, a_h, a_l, 4 * i, parts=(ready, count - KT) if c == 0 else None)

            project_out(L_WO, T_WO, o_lo, KT)

            def ffn_up(n, tile, s, spreads, xs):
                column_tile(n, tile, b_h, b_l, parts=(x_lo, xs - KT))
                stat_sum(s, spreads, x_acc, xs)
                column_tile(n + 1, tile + 1, b_h, b_l)
                stat_spread(spreads)
                for c in (2, 3):
                    column_tile(n + c, tile + c, b_h, b_l)
                with pe.Fori(1, FT // 2) as i:
                    for c in range(4):
                        column_tile(n + c, tile + c, b_h, b_l, 4 * i)

            def ffn_down(n, tile, hidden, last_layer):
                def down_tile(m, i):
                    for c, (k0, kn) in enumerate(DOWN):
                        wait_slab(n + 4 * m + c, 16 * i)
                        wh, wl = slab(n + c, P)
                        if c == 0:
                            wait_tile(tile + m, 4 * i)
                        for k in range(kn):
                            if m == 0:
                                pe.wait_ge(f_lo, hidden - FT + k0 + k + 1)
                            last = mm3(bank[(tile + m) % 4][:, :], wh[:, k, :], wl[:, k, :], hid_h[:, k0 + k, :], hid_l[:, k0 + k, :],
                                       k0 + k == 0, k0 + k == FT - 1)
                        last.then_inc(slab_done, 1)

                def turn_back(m, i, first):
                    pe.wait_ge(tile_taken, tile + m + 4 * i + 1)
                    if not first:
                        pe.wait_ge(y_sb, m + 4 * i - 1)
                    for t in range(NT):
                        last = pe.transpose(bank[Y_BANKS[m % 2]][:, t * P:(t + 1) * P], t2[:, m % 2, t * P:(t + 1) * P], ident[:, :])
                    last.then_inc(y_ps, 1)

                if not last_layer:
                    with pe.Fori(0, KT // 4) as i:
                        for m in range(4):
                            down_tile(m, i)
                else:
                    for m in range(KT):
                        down_tile(m, 0)
                        if m:
                            turn_back(m - 1, 0, m - 1 < 2)
                    turn_back(KT - 1, 0, False)

            ffn_up(L_UP1, T_UP1, 5, 5, 2 * KT)
            ffn_down(L_DN1, T_DN1, FT, False)

            column_tile(L_CQ, T_CQ, b_h, b_l, parts=(x_lo, 2 * KT))
            stat_sum(6, 6, x_acc, 3 * KT)
            column_tile(L_CQ + 1, T_CQ + 1, b_h, b_l)
            stat_spread(6)
            column_tile(L_CQ + 2, T_CQ + 2, b_h, b_l)
            column_tile(L_C, T_C, a_h, a_l, parts=(xb_lo, 0))
            stat_sum(7, 7, c_acc, QT)
            column_tile(L_C + 1, T_C + 1, a_h, a_l)
            wait_slab(L_KR)
            wait_tile(T_KR)
            wh, wl = slab(L_KR, ROPE)
            for t in range(NT):
                for k in range(KT):
                    last = mm3(bank[T_KR % 4][:, t * ROPE:(t + 1) * ROPE], a_h[:, k, t * P:(t + 1) * P], a_l[:, k, t * P:(t + 1) * P],
                               wh[:, k, :], wl[:, k, :], k == 0, k == KT - 1)
            last.then_inc(slab_done, 1)

            def piece(u, gi, dst, waiting):
                kind, t = PIECES[u]
                at_least(pe, piece_taken, 16 * gi + u - waiting + 1)
                if kind == "kv" or kind == "q":
                    base, width, split = (2, 2 * P, (c_h, c_l)) if kind == "kv" else (0, 2 * QK, (cq_h, cq_l))
                    kts = CT if kind == "kv" else QT
                    for c in range(2):
                        if t == 0:
                            wait_slab(L_GRP + base + c, 4 * gi)
                        wh, wl = slab(L_GRP + base + c, width)
                        for k in range(kts):
                            last = mm3(dst[:, c * width:(c + 1) * width], split[0][:, k, t * P:(t + 1) * P],
                                       split[1][:, k, t * P:(t + 1) * P], wh[:, k, :], wl[:, k, :], k == 0, k == kts - 1)
                        if t == NT - 1:
                            last.then_inc(slab_done, 1)
                    if t < NT - 1:
                        last.then_inc(piece_ps, 1)
                else:
                    src = k_n if kind == "kt" else q_n
                    pe.wait_ge(k_rows if kind == "kt" else q_rows, HG * gi + t + 1)
                    for j in range(NT):
                        last = pe.transpose(dst[0:QK, j * P:(j + 1) * P], src[:, HG * j + t, :], ident[:, :])
                    last.then_inc(piece_ps, 1)

            def scores(v, gi):
                h, t = v // NT % HG, v % NT
                n = 16 * gi + v
                at_least(pe, p_exp, n - NT + 1)
                if t == 0:
                    gk = 16 * (gi + v // UNITS)
                    pe.wait_ge(piece_taken, gk + 1 + max(PIECES.index(("kt", h)), PIECES.index(("qt", h))))
                mm(bank[t][:, 0:(t + 1) * P], q_tt[0:QK + NT, h, t * P:(t + 1) * P], k_tt[0:QK + NT, h, 0:(t + 1) * P], True, True)\
                    .then_inc(s_ps, 1)

            def turn(u, gi):
                h, t = divmod(u, NT)
                n = 16 * gi + u
                pe.wait_ge(p_exp, n + 1)
                at_least(pe, pt_sb[1 - u % 2], 8 * gi + (u + 1) // 2)
                for j in range(t + 1):
                    last = pe.transpose(bank[PT_BANK][:, j * P:(j + 1) * P], prob[:, t, j * P:(j + 1) * P], ident[:, :])
                last.then_inc(pt_ps, 1)

            def values(u, gi):
                h, t = divmod(u, NT)
                pe.wait_ge(pt_sb[u % 2], 8 * gi + u // 2 + 1)
                if t == 0:
                    pe.wait_ge(v_ready, HG * gi + h + 1)
                    at_least(pe, o_nat, HG * gi + h - 1)
                    if h % 2:
                        at_least(pe, ot_lo, 2 * gi + h // 2)
                for j in range(t + 1):
                    last = mm(bank[PV_BANKS[h % 2]][:, t * MV:(t + 1) * MV], prob_t[:, u % 2, j * P:(j + 1) * P], v_cur[:, j, h, :],
                              j == 0, j == t)
                last.then_inc(pv_ps, 1)

            def outputs(pair, gi):
                pe.wait_ge(o_nat, HG * gi + 2 * pair + 2)
                for t in range(NT):
                    last = pe.transpose(bank[PV_BANKS[1]][:, t * P:(t + 1) * P], o_n[:, t, :], ident[:, :])
                last.then_inc(ot_ps, 1)

            def group(gi, first, more):
                for u in range(UNITS):
                    turn(u, gi)
                    if u + AHEAD < UNITS or more:
                        scores(u + AHEAD, gi)
                    if u == 2 and not first:
                        outputs(1, gi - 1)
                    if u == 10:
                        outputs(0, gi)
                    if more:
                        piece(u, gi + 1, bank[PIECE], 1)
                    if u:
                        values(u - 1, gi)
                    elif not first:
                        values(UNITS - 1, gi - 1)

            pe.wait_ge(c_lo, QT)
            for u in range(UNITS):
                if PIECES[u] == ("kv", 0):
                    stat_sum(8, 7, c_acc, QT + CT)
                    pe.wait_ge(c_lo, QT + CT)
                piece(u, 0, bank[FIRST_PIECES[u % 3]], 3)
            pe.wait_ge(tile_taken, T_KR + 1)
            pe.wait_ge(mask_rows, 3)
            for v in range(AHEAD):
                scores(v, 0)
            pe.wait_ge(stat_read, 9)
            pe.wait_ge(piece_taken, UNITS)
            group(0, True, True)
            with pe.Fori(1, GROUPS - 1) as g:
                group(g, False, True)
            group(GROUPS - 1, False, False)
            values(UNITS - 1, GROUPS - 1)
            outputs(1, GROUPS - 1)

            project_out(L_WOB, T_WOB, ot_lo, KT)
            ffn_up(L_UP2, T_UP2, 9, 7, 4 * KT)
            ffn_down(L_DN2, T_DN2, 2 * FT, True)

        @block.scalar
        def _(act):
            link = Links(act, act_step)

            def copy(o, i, **kw):
                return act.activation(o, i, ACT.Copy, **kw)

            def hi(n, off, size):
                s = n % RING
                act.wait_ge(w_in[s], 16 * (n // RING + 1) + 4 * off)
                if not (isinstance(off, int) and n + off < RING):
                    act.wait_ge(slab_done, n + off - RING + 1)
                copy(w_h[:, s, 0:size], w_raw[:, s, 0:size]).then_inc(w_hi, 1)

            def size_of(n):
                if L_DN1 <= n < L_CQ:
                    return DOWN[(n - L_DN1) % 4][1] * P
                if n >= L_DN2:
                    return DOWN[(n - L_DN2) % 4][1] * P
                if n == L_KR:
                    return KT * ROPE
                if L_GRP <= n < L_WOB:
                    return group_slab((n - L_GRP) % 4)
                return SLAB

            def hi_next(n, off=0):
                if n + RING < L_END:
                    hi(n + RING, off, size_of(n + RING))

            act.wait_ge(rows_one, 1)
            vec_rows = ((V_A, a_norm, KT), (V_BG, a_b_gate, GH), (V_AO, a_out_norm, HV // P), (V_B, b_norm, KT),
                        (V_QL, b_q_latent_norm, QT), (V_F, f_norm, 2 * KT))
            for row, src, count in vec_rows:
                act.dma_start(rows[row:row + count, :], src.rearrange("a (k p) -> (a k) p", p=P)).then_inc(vec_in, 16)
            for row, src, count in ((V_KV, kv_norm, KT), (V_CL, kv_latent_norm, CT)):
                act.dma_start(rows[row:row + count, :], src.rearrange("(k p) -> k p", p=P)).then_inc(vec_in, 16)
            act.dma_start(rows[V_QN:V_QN + 1, 0:NOPE], b_q_norm[:, 0:NOPE]).then_inc(vec_in, 16)
            act.dma_start(rows[V_KN:V_KN + 1, 0:NOPE], k_norm.rearrange("(a n) -> a n", a=1)[:, 0:NOPE]).then_inc(vec_in, 16)
            act.dma_start(rope_g[:, 0, :], b_q_norm[0:1, NOPE:QK].to_broadcast([P, ROPE])).then_inc(vec_in, 16)
            act.dma_start(rope_g[:, 1, :], k_norm.rearrange("(a n) -> a n", a=1)[:, NOPE:QK].to_broadcast([P, ROPE])).then_inc(vec_in, 16)
            act.wait_ge(w_gate_zero, 1)
            act.dma_start(w_gate[P - GRANK:P, :], a_w_gate_up[0]).then_inc(gate_in, 16)
            act.dma_start(pos_i[0:NT, :].bitcast(I32), positions.rearrange("b (t p) -> (b t) p", p=P)).then_inc(gate_in, 16)

            def x_tile(m, n_x, tile, gain, dst):
                act.wait_ge(tile_taken, tile + m + 1)
                copy(dst[:, m, :], x_t[:, m, :], scale=vecs[:, gain + m:gain + m + 1]).then_inc(x_hi, 1)
                at_least(act, x_acc, n_x + m - 1)
                act.activation(sq[:, m % 2, :], x_t[:, m, :], ACT.Square).then_inc(x_sq, 1)

            def spread(b, dst):
                act.wait_ge(spread_ps, b + 1)
                copy(dst[:, :], bank[STAT][:, :]).then_inc(spread_sb, 1)

            act.wait_ge(vec_sb, 1)
            for m in range(KT):
                x_tile(m, 0, T_X, V_A, a_h)
                if m % 2:
                    hi(m // 2, 0, SLAB)

            hi_next(L_GL)
            hi_next(L_Q)
            spread(0, rinv_b)
            for h in range(GH):
                act.wait_ge(z_abs, h + 1)
                link(act.activation(gt[:, h % 2, :], gt[:, h % 2, :], ACT.Exp))
                act.activation(gt[:, h % 2, :], gt[:, h % 2, :], ACT.Ln, bias=1.0).then_inc(g_soft, 1)
                if h < 3:
                    hi_next(L_Q + 1 + h)
            for h in range(GH):
                hi_next(L_K + h)
                act.wait_ge(g_cum, h + 1)
                at_least(act, g_prep, h - 1)
                act.activation(e_ring[:, h % 2, :], b_t[:, h, :], ACT.Exp, scale=1.0 / TAU).then_inc(g_up, 1)
                ends = b_t[:, h, :].rearrange("p (c n) -> p c n", n=CHUNK)[:, :, CHUNK - 1]
                link(act.activation(dec[:, h, :], ends, ACT.Exp, scale=1.0 / TAU))
                act.wait_ge(g_diff, h + 1)
                act.activation(b_t[:, h, :], b_t[:, h, :], ACT.Exp, scale=-1.0 / TAU).then_inc(g_down, 1)
                act.activation(d_t[:, h, :], d_t[:, h, :], ACT.Exp, scale=1.0 / TAU).then_inc(g_end, 1)
            for n in range(4):
                hi_next(L_V + n)
            act.wait_ge(turns, 1)
            act.activation(trig[:, :, :, :], t1[:, 0, 0:2 * NT * HALF].rearrange("p (a t j) -> p a t j", a=2, t=NT), ACT.Sin,
                           scale=float(2.0 * np.pi)).then_inc(trig_done, 1)
            for n in range(4, 8):
                hi_next(L_V + n)

            def o_split(h):
                for e in range(2):
                    act.wait_ge(o_fin, 2 * h + e + 1)
                    copy(a_h[:, 2 * h + e, :], sr[:, 2 * h + e, :]).then_inc(o_hi, 1)

            for h in range(GH):
                for e in range(2):
                    m = 2 * h + e
                    hi_next(L_R + m)
                    act.wait_ge(tile_taken, T_R + m + 1)
                    act.activation(sr[:, m, :], t1[:, m % 2, :], ACT.Silu).then_inc(r_silu, 1)
                    if e and h:
                        spread(h, rinvo_b)
                act.wait_ge(kend_ps, h + 1)
                at_least(act, chunk_ps, (NCH - 1) * h)
                copy(k_end[:, :, :], bank[4][:, :].rearrange("p (t n) -> p t n", n=HK)).then_inc(kend_sb, 1)
                act.wait_ge(o_ps, h + 1)
                at_least(act, o_acc, h)
                for e in range(2):
                    act.activation(sq[:, e, :], bank[O_BANKS[e]][:, :], ACT.Square).then_inc(o_sq, 1)
                if h == GH - 1:
                    for hh in range(GH - 1):
                        o_split(hh)
            spread(GH, rinvo_b)
            o_split(GH - 1)

            def project_out(n, tile, n_x, gain):
                for m in range(KT):
                    hi_next(n + m)
                    x_tile(m, n_x, tile, gain, b_h)

            project_out(L_WO, T_WO, KT, V_F)

            def ffn_up(n, tile, hidden, b):
                def pair(i, c, off, last):
                    m = hidden + 2 * i + c
                    hi_next(n + 2 * c + (2 * FT - 4 if last else 0), 0 if last else off)
                    if b is not None and c == 0 and isinstance(i, int) and i == 0:
                        spread(b, rinv_b)
                    act.wait_ge(tile_taken, tile + 4 * i + 2 * c + 1)
                    act.activation(t1[:, c, :], t1[:, c, :], ACT.Silu).then_inc(f_silu, 1)
                    hi_next(n + 2 * c + 1 + (2 * FT - 4 if last else 0), 0 if last else off)
                    act.wait_ge(f_prod, m + 1)
                    copy(hid_h[:, bass.ts(2 * i + c, 1), :] if not isinstance(i, int) else hid_h[:, 2 * i + c:2 * i + c + 1, :],
                         t2[:, c:c + 1, :]).then_inc(f_hi, 1)

                for c in range(2):
                    pair(0, c, 0, False)
                with act.Fori(1, FT // 2 - 1) as i:
                    for c in range(2):
                        pair(i, c, 4 * i, False)
                for c in range(2):
                    pair(FT // 2 - 1, c, 0, True)

            def ffn_down(n, tile, n_x, gain):
                for m in range(KT):
                    for c in range(4):
                        hi_next(n + 4 * m + c)
                    if gain is not None:
                        x_tile(m, n_x, tile, gain, b_h)
                    elif m:
                        turn_back(m - 1)

            def turn_back(m):
                act.wait_ge(y_ps, m + 1)
                if m >= 2:
                    act.wait_ge(y_out[m % 2], 16 * (m // 2))
                copy(t1[:, m % 2, :], bank[Y_BANKS[m % 2]][:, :]).then_inc(y_sb, 1)
                act.wait_ge(y_sb, m + 1)
                y_cols = out.rearrange("b (t p) n -> p (b t) n", p=P)
                act.dma_start(y_cols[:, :, m * P:(m + 1) * P], t1[:, m % 2, :].rearrange("p (t n) -> p t n", n=P))\
                    .then_inc(y_out[m % 2], 16)

            ffn_up(L_UP1, T_UP1, 0, 5)
            ffn_down(L_DN1, T_DN1, 2 * KT, V_B)

            def latent(j, gain, dst, m):
                act.wait_ge(tile_taken, T_CQ + j + 1)
                copy(dst[:, m, :], t1[:, j % 2, :], scale=vecs[:, gain + m:gain + m + 1]).then_inc(c_hi, 1)
                act.wait_ge(x_acc, 3 * KT)
                at_least(act, c_acc, j - 1)
                act.activation(sq[:, j % 2, :], t1[:, j % 2, :], ACT.Square).then_inc(c_sq, 1)

            act.wait_ge(slab_done, L_CQ)
            for m in range(KT):
                copy(a_h[:, m, :], x_t[:, m, :], scale=vecs[:, V_KV + m:V_KV + m + 1]).then_inc(xb_hi, 1)
            hi_next(L_CQ)
            spread(6, rinv_b)
            hi_next(L_CQ + 1)
            for j in range(QT):
                if j == 2:
                    hi_next(L_CQ + 2)
                latent(j, V_QL, cq_h, j)
            for j in range(CT):
                hi_next(L_C + j)
                latent(QT + j, V_CL, c_h, j)
            hi_next(L_KR)

            def piece(u, gi, src, last=False):
                kind, t = PIECES[u]
                if kind in ("kv", "q") and t == NT - 1:
                    act.wait_ge(slab_done, L_GRP + 4 * gi + (4 if kind == "kv" else 2))
                else:
                    act.wait_ge(piece_ps, NCOUNTED * gi + COUNTED[u] + 1)
                if kind == "kv":
                    if t == 0:
                        at_least(act, v_ready, HG * gi)
                    copy(kv_n[:, t, :], src[:, :], scale=r_nat[:, 1, t:t + 1]).then_inc(piece_taken, 1)
                elif kind == "q":
                    copy(q_n[:, HG * t:HG * (t + 1), :], src[:, 0:HG * QK].rearrange("p (h n) -> p h n", n=QK),
                         scale=r_nat[:, 2, t:t + 1]).then_inc(piece_taken, 1)
                else:
                    dst, gain = (k_tt, V_KN) if kind == "kt" else (q_tt, V_QN)
                    copy(dst[0:QK, t, :], src[0:QK, :], scale=vecs[0:QK, gain:gain + 1]).then_inc(piece_taken, 1)
                if kind == "q" and t == NT - 1:
                    act.wait_ge(piece_taken, 16 * gi + u + 1)
                    at_least(act, k_sum, gi)
                    act.activation(sq_g[:, :, :], q_n[:, :, :], ACT.Square).then_inc(qsq, 1)
                if kind == "kv" and t == NT - 1:
                    act.wait_ge(piece_taken, 16 * gi + u + 1)
                    act.wait_ge(q_sum, gi + 1)
                    act.activation(sq_g[:, :, 0:NOPE].rearrange("p (t h) n -> p t h n", h=HG),
                                   kv_n[:, :, :].rearrange("p t (h n) -> p t h n", n=P)[:, :, :, 0:NOPE], ACT.Square).then_inc(ksq, 1)
                if kind in ("kv", "q") and t == NT - 1:
                    for c in range(2):
                        n = L_GRP + (2 if kind == "kv" else 0) + c
                        if last:
                            hi_next(n + 4 * (GROUPS - 1))
                        else:
                            hi_next(n, 4 * gi)

            def exps(v, gi):
                t = v % NT
                n = 16 * gi + v
                act.wait_ge(s_bias, n + 1)
                at_least(act, pt_ps, n - NT + 1)
                w = (t + 1) * P
                col = v % UNITS
                act.activation(prob[:, t, 0:w], bank[t][:, 0:w], ACT.Exp,
                               bias=stat[:, 0, col:col + 1], accum_out=stat[:, 1, col:col + 1]).then_inc(p_exp, 1)

            def turned(u, gi):
                if u % 2 == 0:
                    act.wait_ge(pt_ps, 16 * gi + u + 1)
                    at_least(act, pv_ps, 16 * gi + u - 1)
                    w = (u % NT + 1) * P
                    copy(prob_t[:, 0, 0:w], bank[PT_BANK][:, 0:w]).then_inc(pt_sb[0], 1)

            def outputs(pair, gi):
                act.wait_ge(ot_ps, 2 * gi + pair + 1)
                dst = a_h[:, 2 * gi + pair:2 * gi + pair + 1, :] if isinstance(gi, int) else a_h[:, bass.ts(2 * gi + pair, 1), :]
                copy(dst, bank[PV_BANKS[1]][:, :].rearrange("p (a n) -> p a n", a=1)).then_inc(ot_hi, 1)

            def group(gi, first, more, last=False):
                for u in range(UNITS):
                    turned(u, gi)
                    if u + AHEAD - 1 < UNITS or more:
                        exps(u + AHEAD - 1, gi)
                    if u == 2 and not first:
                        outputs(1, gi - 1)
                    if u == 10:
                        outputs(0, gi)
                    if more:
                        piece(u, gi + 1, bank[PIECE], last)

            for u in range(UNITS):
                if PIECES[u][1] == 0 and u <= NT:
                    act.wait_ge(stat_nat, 1 + u // NT)
                piece(u, 0, bank[FIRST_PIECES[u % 3]])
            for v in range(AHEAD - 1):
                exps(v, 0)
            group(0, True, True)
            with act.Fori(1, GROUPS - 2) as g:
                group(g, False, True)
            group(GROUPS - 2, False, True, True)
            group(GROUPS - 1, False, False)
            outputs(1, GROUPS - 1)

            project_out(L_WOB, T_WOB, 3 * KT, V_F + KT)
            ffn_up(L_UP2, T_UP2, FT, 7)
            ffn_down(L_DN2, T_DN2, 0, None)
            turn_back(KT - 1)
            for s in y_out:
                act.wait_ge(s, 16 * KT // 2)

        @block.vector
        def _(dve):
            link = Links(dve, dve_step)

            def tt(o, a, b, op):
                return dve.tensor_tensor(o, a, b, op)

            def stt(o, a, scalar, b, op0, op1):
                return dve.scalar_tensor_tensor(out=o, in0=a, scalar=scalar, in1=b, op0=op0, op1=op1)

            def ts(o, a, s1, s2, op0, op1=None):
                if op1 is None:
                    return dve.tensor_scalar(o, a, s1, None, op0)
                return dve.tensor_scalar(o, a, s1, s2, op0, op1)

            def guess(sums, width, eps, count, signal=None):
                m, y = (nw[:, j, 0:count] for j in range(2))
                first = ts(m, sums, 1.0 / width, eps, ALU.mult, ALU.add)
                if signal is not None:
                    first.then_inc(signal[0], 1)
                    dve.wait_ge(signal[0], signal[1])
                else:
                    link(first)
                link(ts(y.bitcast(I32), m.bitcast(I32), -0.5, float(0x5f3759df), ALU.mult, ALU.add))

            def newton(count, dst=None):
                m, y, a = (nw[:, j, 0:count] for j in range(3))
                link(tt(a, y, y, ALU.mult))
                link(stt(a, a, -0.5, m, ALU.mult, ALU.mult))
                last = stt(y if dst is None else dst, a, 1.5, y, ALU.add, ALU.mult)
                if dst is None:
                    link(last)
                return last

            def x_tile(m, n_x, gain, dst_h, dst_l):
                n = n_x + m
                dve.wait_ge(x_hi, n + 1)
                stt(dst_l[:, m, :], x_t[:, m, :], vecs[:, gain + m:gain + m + 1], dst_h[:, m, :].bitcast(F32),
                    ALU.mult, ALU.subtract).then_inc(x_lo, 1)
                dve.wait_ge(x_sq, n + 1)
                if m == 0:
                    dve.tensor_copy(acc[:, :], sq[:, 0, :]).then_inc(x_acc, 1)
                else:
                    dve.wait_ge(x_acc, n)
                    tt(acc[:, :], acc[:, :], sq[:, m % 2, :], ALU.add).then_inc(x_acc, 1)

            def norm(s, row, spreads=None, width=D):
                dve.wait_ge(stat_ps, s + 1)
                guess(bank[STAT][:, 0:NT], width, EPS, NT, (stat_read, s + 1))
                newton(NT)
                newton(NT)
                last = newton(NT, r_nat[:, row, :])
                if spreads is None:
                    last.then_inc(stat_nat, 1)
                    return
                link(last)
                at_least(dve, spread_ps, spreads)
                for t in range(NT):
                    last = ts(diag[:, t, :], ident[:, :], r_nat[:, row, t:t + 1], None, ALU.mult)
                last.then_inc(diag_done, 1)

            dve.memset(rows[:, :], 1.0).then_inc(rows_one, 1)
            dve.wait_ge(gate_in, 32)
            dve.tensor_copy(pos_f[0:NT, :], pos_i[0:NT, :].bitcast(I32)).then_inc(rows_pos, 1)
            dve.wait_ge(vec_ps, 1)
            dve.tensor_copy(vecs[:, :], bank[STAT][:, 0:NVEC + NT]).then_inc(vec_sb, 1)
            dve.wait_ge(vec_sb, 1)

            for m in range(KT):
                dve.wait_ge(x_ps, m + 1)
                dve.tensor_copy(x_t[:, m, :], bank[(T_X + m) % 4][:, :]).then_inc(tile_taken, 1)
                x_tile(m, 0, V_A, a_h, a_l)

            norm(0, 0, 0)
            dve.wait_ge(spread_sb, 1)
            dve.wait_ge(slab_done, L_GL + 1)
            tt(gl_t[:, :], bank[T_GL % 4][:, :], rinv_b[:, :], ALU.mult).then_inc(tile_taken, 1)
            for h in range(GH):
                dve.wait_ge(z_ps, h + 1)
                if h >= 2:
                    log_gate = (h - 2,)
                    dve.wait_ge(g_soft, h - 1)
                    link(stt(gt[:, h % 2, :], b_t[:, h - 2, :], 0.0, gt[:, h % 2, :], ALU.min, ALU.subtract))
                    dve.tensor_tensor_scan(b_t[:, h - 2, :], t2[:, 1, :], gt[:, h % 2, :], 0.0, ALU.mult, ALU.add).then_inc(g_cum, 1)
                    dve.wait_ge(g_cum, h - 1)
                link(ts(b_t[:, h, :], bank[(5, 6, 7, 5)[h]][:, :], vecs[:, V_BG + h:V_BG + h + 1], None, ALU.add))
                stt(gt[:, h % 2, :], b_t[:, h, :], -1.0, b_t[:, h, :], ALU.mult, ALU.min).then_inc(z_abs, 1)
                dve.wait_ge(slab_done, L_Q + h + 1)
                tt(q_t[:, h, :], bank[(T_Q + h) % 4][:, :], rinv_b[:, :], ALU.mult).then_inc(tile_taken, 1)
            for h in (2, 3):
                dve.wait_ge(g_soft, h + 1)
                link(stt(gt[:, h % 2, :], b_t[:, h, :], 0.0, gt[:, h % 2, :], ALU.min, ALU.subtract))
                dve.tensor_tensor_scan(b_t[:, h, :], t2[:, 1, :], gt[:, h % 2, :], 0.0, ALU.mult, ALU.add).then_inc(g_cum, 1)
            dve.wait_ge(g_cum, GH)
            for h in range(GH):
                chunks = b_t[:, h, :].rearrange("p (c n) -> p c n", n=CHUNK)
                tt(d_t[:, h, :].rearrange("p (c n) -> p c n", n=CHUNK), chunks[:, :, CHUNK - 1:CHUNK].to_broadcast([P, NCH, CHUNK]),
                   chunks, ALU.subtract).then_inc(g_diff, 1)
            for h in range(GH):
                dve.wait_ge(slab_done, L_K + h + 1)
                tt(k_ring[:, h % 2, :], bank[(T_K + h) % 4][:, :], rinv_b[:, :], ALU.mult).then_inc(tile_taken, 1)
                dve.wait_ge(g_up, h + 1)
                stt(q_t[:, h, :], q_t[:, h, :], HK ** -0.5, e_ring[:, h % 2, :], ALU.mult, ALU.mult)
                dve.wait_ge(tile_taken, T_K + h + 1)
                dve.wait_ge(g_down, h + 1)
                tt(b_t[:, h, :], b_t[:, h, :], k_ring[:, h % 2, :], ALU.mult)
                dve.wait_ge(g_end, h + 1)
                tt(d_t[:, h, :], d_t[:, h, :], k_ring[:, h % 2, :], ALU.mult).then_inc(g_prep, 1)

            n_ang = NT * HALF
            ang, high, low = t2[:, 0, 0:n_ang], t2[:, 0, n_ang:2 * n_ang], t2[:, 0, 2 * n_ang:3 * n_ang]
            prods = t1[:, :, :].rearrange("p a n -> p (a n)")[:, 0:10 * n_ang]
            whole = sq[:, :, :].rearrange("p a n -> p (a n)")[:, 0:10 * n_ang]
            for t in range(NT):
                last = ts(t2[:, 0, t * HALF:(t + 1) * HALF], inv_freq[:, :], vecs[:, NVEC + t:NVEC + t + 1], None, ALU.mult)
            link(last)
            link(dve.tensor_single_scalar(high.bitcast(I32), ang.bitcast(I32), -4096, op=ALU.bitwise_and))
            link(tt(low, ang, high, ALU.subtract))
            for j, piece_ in enumerate(TURN):
                ts(prods[:, 2 * j * n_ang:(2 * j + 1) * n_ang], high, piece_, None, ALU.mult)
                last = ts(prods[:, (2 * j + 1) * n_ang:(2 * j + 2) * n_ang], low, piece_, None, ALU.mult)
            link(last)

            def drop_whole(values_, space):
                link(ts(space, values_, MAGIC, MAGIC, ALU.add, ALU.subtract))
                link(tt(values_, values_, space, ALU.subtract))

            for _ in range(2):
                drop_whole(prods, whole)
            link(dve.tensor_reduce(ang, prods.rearrange("p (j n) -> p n j", j=10), AX_X, ALU.add))
            both = t1[:, 0, 0:2 * n_ang]
            link(ts(both[:, 0:n_ang], ang, 0.25, None, ALU.add))
            link(dve.tensor_copy(both[:, n_ang:2 * n_ang], ang))
            drop_whole(both, whole[:, 0:2 * n_ang])
            ts(both, both, 0.4999999, -0.4999999, ALU.min, ALU.max).then_inc(turns, 1)

            for c in range(2):
                dve.wait_ge(slab_done, L_V + 4 * c + 4)
                for t in range(NT):
                    ts(v_g[:, t, c * S:(c + 1) * S], bank[(T_V + t) % 4][:, :], r_nat[:, 0, t:t + 1], None, ALU.mult)\
                        .then_inc(tile_taken, 1)

            def o_final(h):
                dve.wait_ge(o_gated, h + 1)
                for e in range(2):
                    m = 2 * h + e
                    stt(sr[:, m, :], sr[:, m, :], vecs[:, V_AO + e:V_AO + e + 1], rinvo_b[:, :], ALU.mult, ALU.mult).then_inc(o_fin, 1)

            def o_split(h):
                for e in range(2):
                    m = 2 * h + e
                    dve.wait_ge(o_hi, m + 1)
                    tt(a_l[:, m, :], sr[:, m, :], a_h[:, m, :].bitcast(F32), ALU.subtract).then_inc(o_lo, 1)

            dve.wait_ge(trig_done, 1)
            for h in range(GH):
                for e in range(2):
                    m = 2 * h + e
                    dve.wait_ge(slab_done, L_R + m + 1)
                    at_least(dve, r_silu, m - 1)
                    tt(t1[:, m % 2, :], bank[(T_R + m) % 4][:, :], rinv_b[:, :], ALU.mult).then_inc(tile_taken, 1)
                    if h and not e:
                        norm(h, 3, h, HV)
                    if h and e:
                        dve.wait_ge(spread_sb, h + 1)
                        o_final(h - 1)
                dve.wait_ge(att_ps, h + 1)
                at_least(dve, o_ps, h)
                dve.copy_predicated(att[:, :, :], mask[:, :].bitcast(I32).rearrange("p (a n) -> p a n", a=1).to_broadcast([P, NT, P]),
                                    bank[5][:, :].rearrange("p (t n) -> p t n", n=P)).then_inc(att_sb, 1)
                for c in range(NCH - 1):
                    n = (NCH - 1) * h + c
                    dve.wait_ge(chunk_ps, n + 1)
                    kv = bank[KV_BANKS[c % 2]][:, 0:HV]
                    if c == 0:
                        dve.tensor_copy(state[:, 1, :], kv).then_inc(state_sb, 1)
                    else:
                        dve.wait_ge(state_sb, n)
                        stt(state[:, c + 1, :], state[:, c, :], dec[:, h, c:c + 1], kv, ALU.mult, ALU.add).then_inc(state_sb, 1)
                dve.wait_ge(o_sq, 2 * h + 2)
                tt(acc[:, :], sq[:, 0, :], sq[:, 1, :], ALU.add).then_inc(o_acc, 1)
                dve.wait_ge(r_silu, 2 * h + 2)
                for e in range(2):
                    m = 2 * h + e
                    last = tt(sr[:, m, :], sr[:, m, :], bank[O_BANKS[e]][:, :], ALU.mult)
                last.then_inc(o_gated, 1)
                if h == GH - 1:
                    for hh in range(GH - 1):
                        o_split(hh)
            norm(GH, 3, GH, HV)
            dve.wait_ge(spread_sb, GH + 1)
            o_final(GH - 1)
            o_split(GH - 1)

            def project_out(n, tile, n_x, gain):
                for m in range(KT):
                    dve.wait_ge(slab_done, n + m + 1)
                    tt(x_t[:, m, :], x_t[:, m, :], bank[(tile + m) % 4][:, :], ALU.add).then_inc(tile_taken, 1)
                    x_tile(m, n_x, gain, b_h, b_l)

            project_out(L_WO, T_WO, KT, V_F)

            def ffn_up(n, tile, hidden):
                with dve.Fori(0, FT // 2) as i:
                    for c in range(2):
                        m = hidden + 2 * i + c
                        dve.wait_ge(slab_done, n + 4 * i + 2 * c + 1)
                        tt(t1[:, c, :], bank[(tile + 2 * c) % 4][:, :], rinv_b[:, :], ALU.mult).then_inc(tile_taken, 1)
                        dve.wait_ge(slab_done, n + 4 * i + 2 * c + 2)
                        tt(t2[:, c, :], bank[(tile + 2 * c + 1) % 4][:, :], rinv_b[:, :], ALU.mult).then_inc(tile_taken, 1)
                        dve.wait_ge(tile_taken, tile + 4 * i + 2 * c + 2)
                        dve.wait_ge(f_silu, m + 1)
                        tt(t2[:, c, :], t2[:, c, :], t1[:, c, :], ALU.mult).then_inc(f_prod, 1)
                        dve.wait_ge(f_hi, m + 1)
                        tt(hid_l[:, bass.ts(2 * i + c, 1), :], t2[:, c:c + 1, :], hid_h[:, bass.ts(2 * i + c, 1), :].bitcast(F32),
                           ALU.subtract).then_inc(f_lo, 1)

            def ffn_down(n, tile, n_x, gain):
                for m in range(KT):
                    dve.wait_ge(slab_done, n + 4 * m + 4)
                    ps = bank[(tile + m) % 4][:, :]
                    if gain is not None:
                        tt(x_t[:, m, :], x_t[:, m, :], ps, ALU.add).then_inc(tile_taken, 1)
                        x_tile(m, n_x, gain, b_h, b_l)
                    else:
                        if m == 0:
                            dve.wait_ge(f_hi, 2 * FT)
                        at_least(dve, y_ps, m - 1)
                        tt(t2[:, m % 2, :], x_t[:, m, :], ps, ALU.add).then_inc(tile_taken, 1)

            dve.wait_ge(x_acc, 2 * KT)
            norm(5, 0, 5)
            dve.wait_ge(spread_sb, 6)
            ffn_up(L_UP1, T_UP1, 0)
            ffn_down(L_DN1, T_DN1, 2 * KT, V_B)

            for m in range(KT):
                dve.wait_ge(xb_hi, m + 1)
                stt(a_l[:, m, :], x_t[:, m, :], vecs[:, V_KV + m:V_KV + m + 1], a_h[:, m, :].bitcast(F32),
                    ALU.mult, ALU.subtract).then_inc(xb_lo, 1)
            norm(6, 0, 6)
            for j, (kind, g_half, f) in enumerate([(kind, a, f) for kind in range(2) for a, f in ((0, 0), (1, 1), (0, 1), (1, 0))]):
                gains = rope_g[:, kind:kind + 1, g_half * HALF:(g_half + 1) * HALF].to_broadcast([P, NT, HALF])
                last = tt(rope_c[:, j, :, :], trig[:, f, :, :], gains, ALU.mult)
            link(last)
            dve.wait_ge(spread_sb, 7)

            def latent(j, gain, split_h, split_l, m):
                tile = T_CQ + j
                dve.wait_ge(slab_done, L_CQ + j + 1)
                at_least(dve, c_sq, j - 1)
                tt(t1[:, j % 2, :], bank[tile % 4][:, :], rinv_b[:, :], ALU.mult).then_inc(tile_taken, 1)
                dve.wait_ge(tile_taken, tile + 1)
                dve.wait_ge(c_hi, j + 1)
                stt(split_l[:, m, :], t1[:, j % 2, :], vecs[:, gain + m:gain + m + 1], split_h[:, m, :].bitcast(F32),
                    ALU.mult, ALU.subtract).then_inc(c_lo, 1)
                dve.wait_ge(c_sq, j + 1)
                if m == 0:
                    if j:
                        dve.wait_ge(stat_ps, 8)
                    dve.tensor_copy(acc[:, :], sq[:, j % 2, :]).then_inc(c_acc, 1)
                else:
                    dve.wait_ge(c_acc, j)
                    tt(acc[:, :], acc[:, :], sq[:, j % 2, :], ALU.add).then_inc(c_acc, 1)

            for j in range(QT):
                latent(j, V_QL, cq_h, cq_l, j)
            dve.wait_ge(slab_done, L_C)
            dve.memset(q_tt[QK:QK + NT, :, :], 0.0)
            dve.memset(k_tt[QK:QK + NT, :, :], 0.0).then_inc(mask_rows, 1)
            dve.wait_ge(mask_rows, 1)
            by_tile = ident[QK:QK + NT, QK:QK + NT].rearrange("p (t a) -> p t a", a=1).to_broadcast([NT, NT, CHUNK])
            for h in range(HG):
                queries, keys = (w[QK:QK + NT, h, :].rearrange("p (t c n) -> p t c n", c=2, n=CHUNK) for w in (q_tt, k_tt))
                q_ones = dve.tensor_copy(queries[:, :, 0, :], by_tile)
                k_neg = ts(keys[:, :, 1, :], by_tile, NEG, None, ALU.mult)
                if h == HG - 1:
                    q_ones.then_inc(mask_rows, 1)
                    k_neg.then_inc(mask_rows, 1)
            for j in range(CT):
                latent(QT + j, V_CL, c_h, c_l, j)
                if j == 0:
                    norm(7, 2, None, QRANK)
            dve.wait_ge(slab_done, L_KR + 1)
            for t in range(NT):
                last = ts(kr[:, 0, t, :], bank[T_KR % 4][:, t * ROPE:(t + 1) * ROPE], r_nat[:, 0, t:t + 1], None, ALU.mult)
            last.then_inc(tile_taken, 1)
            dve.wait_ge(tile_taken, T_KR + 1)
            link(tt(kr[:, 1, :, :], kr[:, 0, :, :], kr[:, 0, :, :], ALU.mult))
            link(dve.tensor_reduce(kr_ss[:, :], kr[:, 1, :, :], AX_X, ALU.add))
            space = [kr[:, 2 + j // 2, :, (j % 2) * HALF:(j % 2 + 1) * HALF] for j in range(4)]
            x1, x2 = kr[:, 0, :, 0:HALF], kr[:, 0, :, HALF:ROPE]
            for j, x_half in enumerate((x1, x2, x1, x2)):
                last = tt(space[j], x_half, rope_c[:, 4 + j, :, :], ALU.mult)
            link(last)
            tt(kr[:, 1, :, 0:HALF], space[0], space[1], ALU.subtract)
            link(tt(kr[:, 1, :, HALF:ROPE], space[2], space[3], ALU.add))
            norm(8, 1, None, KVRANK)

            sums = nw[:, 1, :]

            def query_sums(gi):
                dve.wait_ge(qsq, gi + 1)
                if isinstance(gi, int) and gi == 0:
                    dve.wait_ge(stat_nat, 2)
                else:
                    dve.wait_ge(k_fac, gi)
                dve.tensor_reduce(sums, sq_g[:, :, :], AX_X, ALU.add).then_inc(q_sum, 1)
                dve.wait_ge(q_sum, gi + 1)

            def key_sums(gi):
                dve.wait_ge(ksq, gi + 1)
                dve.wait_ge(q_fac, gi + 1)
                dve.tensor_reduce(sums, sq_g[:, :, 0:NOPE], AX_X, ALU.add).then_inc(k_sum, 1)
                dve.wait_ge(k_sum, gi + 1)
                by_token = sums.rearrange("p (t h) -> p t h", h=HG)
                link(tt(by_token, by_token, kr_ss[:, :].rearrange("p (t a) -> p t a", a=1).to_broadcast([P, NT, HG]), ALU.add))

            def bias(v, gi):
                t = v % NT
                col = v % UNITS
                dve.wait_ge(s_ps, 16 * gi + v + 1)
                dve.tensor_reduce(stat[:, 0, col:col + 1], bank[t][:, 0:(t + 1) * P], AX_X, ALU.max, negate=True).then_inc(s_bias, 1)

            def turned(u, gi):
                if u % 2:
                    dve.wait_ge(pt_ps, 16 * gi + u + 1)
                    at_least(dve, pv_ps, 16 * gi + u - 1)
                    w = (u % NT + 1) * P
                    dve.tensor_copy(prob_t[:, 1, 0:w], bank[PT_BANK][:, 0:w]).then_inc(pt_sb[1], 1)

            def head_out(h, gi):
                dve.wait_ge(pv_ps, 16 * gi + NT * (h + 1))
                cols = slice(NT * h, NT * (h + 1))
                link(dve.reciprocal(stat[:, 2, cols], stat[:, 1, cols]))
                if h % 2 == 0:
                    at_least(dve, ot_ps, 2 * gi + h // 2)
                tt(o_n[:, :, (h % 2) * MV:(h % 2 + 1) * MV], bank[PV_BANKS[h % 2]][:, 0:NT * MV].rearrange("p (t n) -> p t n", n=MV),
                   stat[:, 2, cols].rearrange("p (t a) -> p t a", a=1).to_broadcast([P, NT, MV]), ALU.mult).then_inc(o_nat, 1)

            def outputs(pair, gi):
                dve.wait_ge(ot_hi, 2 * gi + pair + 1)
                m = 2 * gi + pair
                cut = slice(m, m + 1) if isinstance(gi, int) else bass.ts(m, 1)
                tt(a_l[:, cut, :], bank[PV_BANKS[1]][:, :].rearrange("p (a n) -> p a n", a=1), a_h[:, cut, :].bitcast(F32),
                   ALU.subtract).then_inc(ot_lo, 1)

            def take_values(h, gi):
                at_least(dve, pv_ps, 16 * (gi - 1) + NT * (h + 1))
                dve.wait_ge(piece_taken, 16 * gi + 2 * NT)
                dve.tensor_copy(v_cur[:, :, h, :], kv_n[:, :, h * P + NOPE:(h + 1) * P]).then_inc(v_ready, 1)

            def beside(u, gi):
                if u == 4:
                    query_sums(gi + 1)
                if u == 5:
                    guess(sums, 1.0, QK * EPS, UNITS)
                    newton(UNITS)
                if u == 6:
                    newton(UNITS)
                    newton(UNITS, q_scale[:, :]).then_inc(q_fac, 1)
                if u == 8:
                    key_sums(gi + 1)
                    guess(sums, QK, EPS, UNITS)
                if u == 9:
                    newton(UNITS)
                if u == 10:
                    newton(UNITS)
                    newton(UNITS, k_scale[:, :]).then_inc(k_fac, 1)

            BESIDE_LINKS = (2 + 8) + (1 + 2 + 8)

            def group(gi, first, more):
                for u in range(UNITS):
                    if u % NT == 1 and not (first and u == 1):
                        head_out((u // NT - 1) % HG, gi if u > 1 else gi - 1)
                    if u == 1 and not first:
                        take_values(3, gi)
                    if u == 3 and not first:
                        outputs(1, gi - 1)
                    if u == 11:
                        outputs(0, gi)
                    turned(u, gi)
                    if u + AHEAD < UNITS or more:
                        bias(u + AHEAD, gi)
                    if more:
                        beside(u, gi)
                        for h in {9: (0, 1), 13: (2,)}.get(u, ()):
                            take_values(h, gi + 1)

            for u in range(UNITS):
                beside(u, -1)
            for h in range(HG):
                take_values(h, 0)
            for v in range(AHEAD):
                bias(v, 0)
            group(0, True, True)
            with dve.Fori(1, GROUPS - 1) as g:
                link.enter(g, HG + BESIDE_LINKS, 1)
                group(g, False, True)
            link.leave(GROUPS - 2)
            group(GROUPS - 1, False, False)
            head_out(HG - 1, GROUPS - 1)
            outputs(1, GROUPS - 1)

            project_out(L_WOB, T_WOB, 3 * KT, V_F + KT)
            norm(9, 0, 7)
            dve.wait_ge(spread_sb, 8)
            ffn_up(L_UP2, T_UP2, FT)
            ffn_down(L_DN2, T_DN2, 0, None)


_INS = ['x', 'positions', 'a_norm', 'a_w_in', 'a_w_gate_up', 'a_b_gate', 'a_out_norm', 'a_w_out',
        'b_norm', 'b_w_dq', 'b_q_latent_norm', 'b_w_uq', 'b_q_norm', 'b_w_out',
        'kv_norm', 'kv_w_down', 'kv_latent_norm', 'kv_w_up', 'k_norm', 'f_norm', 'f_w_in', 'f_w_out']
_OUTS = [((1, S, D), 'float32')]


def kernel(**inputs):
    import numpy as _np
    import concourse.bacc as _bacc
    from concourse import mybir as _mybir
    from concourse.bass_utils import run_bass_kernel_spmd as _run

    nc = _bacc.Bacc("TRN2", target_bir_lowering=False, num_devices=1)
    arrays, args = {}, []
    for name in _INS:
        a = _np.ascontiguousarray(inputs[name])
        arrays[f"in_{name}_dram"] = a
        args.append(nc.dram_tensor(f"in_{name}_dram", a.shape, _mybir.dt.from_np(a.dtype), kind="ExternalInput").ap())
    for i, (shape, dtype) in enumerate(_OUTS):
        dt = _mybir.dt.from_np(_np.dtype(dtype))
        args.append(nc.dram_tensor(f"out_{i}_dram", shape, dt, kind="ExternalOutput").ap())
    trunk(nc, *args)
    r = _run(nc, [arrays], core_ids=[0])
    return r.results[0]["out_0_dram"]
```

```python
from contextlib import ExitStack

import numpy as np

import concourse.bass as bass
from concourse import mybir

ALU = mybir.AluOpType
ACT = mybir.ActivationFunctionType
F32 = mybir.dt.float32
F32R = mybir.dt.float32r
I32 = mybir.dt.int32
AX_X = mybir.AxisListType.X

P = 128
D = 1024
S = 512
CHUNK = 64
EPS = 1e-6
KT = D // P
NT = S // P
NCH = S // CHUNK

GH, HK, HV, GRANK, TAU = 4, 128, 256, 16, 16.0
DK, DV = GH * HK, GH * HV

MH, NOPE, ROPE, QK, MV = 16, 64, 32, 96, 64
HALF = ROPE // 2
QRANK, KVRANK = 384, 256
QT, CT = QRANK // P, KVRANK // P
THETA = 10000.0
GROUPS = 4
HG = MH // GROUPS
UNITS = HG * NT
AHEAD = 3

FF = -(-8 * D // (3 * 256)) * 256
FT = FF // P
DOWN = ((0, 6), (6, 6), (12, 5), (17, 5))

RING = 4
SLAB = 1024
NEG = -1.0e30
MAGIC = 1.5 * 2.0 ** 23

L_GL = 0
L_Q = L_GL + 1
L_K = L_Q + GH
L_V = L_K + GH
L_R = L_V + 8
L_WO = L_R + KT
L_UP1 = L_WO + KT
L_DN1 = L_UP1 + 2 * FT
L_CQ = L_DN1 + 4 * KT
L_C = L_CQ + QT
L_Q0 = L_C + 1
L_C1 = L_Q0 + 2
L_KR = L_C1 + 1
L_GRP = L_KR + 1 - 2
L_WOB = L_GRP + 4 * GROUPS
L_UP2 = L_WOB + KT
L_DN2 = L_UP2 + 2 * FT
L_END = L_DN2 + 4 * KT

T_GL = 0
T_Q = T_GL + 1
T_K = T_Q + GH
T_V = T_K + GH
T_R = T_V + 8
T_WO = T_R + KT
T_UP1 = T_WO + KT
T_DN1 = T_UP1 + 2 * FT
T_CQ = T_DN1 + KT
T_C = T_CQ + QT
T_KR = T_C + CT
T_KRT = T_KR + 1
T_WOB = T_KRT + 1
T_UP2 = T_WOB + KT
T_DN2 = T_UP2 + 2 * FT

V_A, V_BG, V_AO, V_B, V_QL, V_KV, V_CL, V_F, V_QN, V_KN = 0, 8, 12, 14, 22, 25, 33, 35, 51, 52
NVEC = 53

TURN = [int(h, 16) / 2.0 ** (12 * (j + 1)) / 4.0 for j, h in enumerate(("A2F", "983", "6E4", "E44", "152"))]

PIECES = ([("q", t) for t in range(NT)] + [("kv", t) for t in range(NT)]
          + [("qt", 0), ("qt", 1), ("qt", 2), ("kt", 0), ("kt", 1), ("kt", 2), ("kt", 3), ("qt", 3)])
COUNTED = [0]
for _kind, _t in PIECES:
    COUNTED.append(COUNTED[-1] + (not (_kind in ("kv", "q") and _t == NT - 1)))
NCOUNTED = COUNTED[-1]


GROUP_SLABS = ((0, 2, HG * QK), (2, 1, HG * QK), (0, 1, HG * P), (1, 1, HG * P))


def group_slab(c):
    return GROUP_SLABS[c][1] * GROUP_SLABS[c][2]


class Links:

    def __init__(self, engine, sem):
        self.engine, self.sem, self.n, self.off = engine, sem, 0, 0

    def __call__(self, instruction):
        instruction.then_inc(self.sem, 1)
        self.n += 1
        self.engine.wait_ge(self.sem, self.off + self.n)

    def enter(self, i, per, first=0):
        self.start, self.per, self.first, self.off = self.n, per, first, (i - first) * per

    def leave(self, times):
        assert self.n - self.start == self.per, (self.n - self.start, self.per)
        self.n, self.off = self.start + self.per * times, 0


def trunk(nc, x, positions, a_norm, a_w_in, a_w_gate_up, a_b_gate, a_out_norm, a_w_out,
          b_norm, b_w_dq, b_q_latent_norm, b_w_uq, b_q_norm, b_w_out,
          kv_norm, kv_w_down, kv_latent_norm, kv_w_up, k_norm, f_norm, f_w_in, f_w_out, out):
    ctx = ExitStack()
    with ctx:
        def sb(name, shape, dt=F32, stack=ctx):
            return stack.enter_context(nc.sbuf_tensor(name, shape, dt))

        def sem(name):
            return ctx.enter_context(nc.semaphore(name))

        x_t = sb("x_t", [P, KT, S])
        w_raw = sb("w_raw", [P, RING, SLAB])
        w_h = sb("w_h", [P, RING, SLAB], F32R)
        w_l = sb("w_l", [P, RING, SLAB], F32R)
        ident = sb("ident", [P, P])
        ones = sb("ones", [P, P])
        acc = sb("acc", [P, S])
        sq = sb("sq", [P, 2, S])
        rinv_b = sb("rinv_b", [P, S])
        rinvo_b = sb("rinvo_b", [P, S])
        t1 = sb("t1", [P, 2, S])
        t2 = sb("t2", [P, 2, S])
        diag = sb("diag", [P, NT, P])
        vecs = sb("vecs", [P, NVEC + NT])
        r_nat = sb("r_nat", [P, 4, NT])
        nw = sb("nw", [P, 3, UNITS])
        dec = sb("dec", [P, GH, NCH])
        q_scale = sb("q_scale", [P, UNITS])
        k_scale = sb("k_scale", [P, UNITS])
        stat = sb("stat", [P, 3, UNITS])

        rope_g = sb("rope_g", [P, 2, ROPE])
        kr_ss = sb("kr_ss", [P, NT])
        trig = sb("trig", [P, 2, NT, HALF])
        inv_freq = sb("inv_freq", [P, HALF])

        def overlay(tag, behind_hi, behind_lo, over_b):
            made = []
            with ExitStack() as stack:
                for n, (group, room) in enumerate(((behind_hi, (FT - KT) * S), (behind_lo, (FT - KT) * S), (over_b, 2 * KT * S))):
                    if n < 2:
                        sb(f"{tag}_under{n}", [P, KT * S], F32, stack)
                    used = 0
                    for name, shape, *dt in group:
                        made.append(sb(f"{tag}_{name}", shape, dt[0] if dt else F32, stack))
                        used += int(np.prod(shape[1:]))
                    assert used <= room, (tag, n, used, room)
                    if used < room:
                        sb(f"{tag}_rest{n}", [P, room - used], F32, stack)
            return made

        (b_t, d_t, q_t, att, k_end, v_g, state, k_ring, sr, e_ring, gt, gl_t, w_gate, mask, rows, pos_i, pos_f) = overlay(
            "gla",
            [("b_t", [P, GH, S]), ("d_t", [P, GH, S]), ("q_t", [P, GH, S]), ("att", [P, NT, P]), ("k_end", [P, NT, HK])],
            [("v", [P, NT, DV]), ("state", [P, NCH, HV]), ("k_ring", [P, 2, S])],
            [("sr", [P, KT, S]), ("e_ring", [P, 2, S]), ("gt", [P, 2, S]), ("gl_t", [P, S]), ("w_gate", [P, DK]),
             ("mask", [P, P]), ("rows", [P, P]), ("pos_i", [P, P]), ("pos_f", [P, P])])
        (kv_n, q_n, k_n, sq_g, rope_c, v_cur, c_h, c_l, cq_h, cq_l, kr, o_n, k_tt, q_tt, prob, prob_t) = overlay(
            "mla",
            [("kv_n", [P, NT, HG * P]), ("q_n", [P, UNITS, QK]), ("k_n", [P, UNITS, QK]), ("sq_g", [P, UNITS, QK]),
             ("rope_c", [P, 8, NT, HALF])],
            [("v_cur", [P, NT, HG, MV]), ("c_h", [P, CT, S], F32R), ("c_l", [P, CT, S], F32R),
             ("cq_h", [P, QT, S], F32R), ("cq_l", [P, QT, S], F32R), ("kr", [P, 4, NT, ROPE]), ("o_n", [P, NT, P])],
            [("k_tt", [P, HG, S]), ("q_tt", [P, HG, S]), ("prob", [P, NT, S]), ("prob_t", [P, 2, S])])
        hid_h = sb("hid_h", [P, FT, S], F32R)
        hid_l = sb("hid_l", [P, FT, S], F32R)
        b_h = sb("b_h", [P, KT, S], F32R)
        b_l = sb("b_l", [P, KT, S], F32R)
        a_h, a_l = hid_h[:, 0:KT, :], hid_l[:, 0:KT, :]

        bank = [ctx.enter_context(nc.psum_tensor(f"bank{n}", [P, S], F32)) for n in range(8)]
        STAT, KV_BANKS, O_BANKS = 4, (4, 5), (6, 7)
        GATE_BANKS, GAIN = (5, 6, 7, 5), 7
        PT_BANK, PV_BANKS, PIECE = 4, (5, 6), 7
        FIRST_PIECES = (5, 6, 7)
        Y_BANKS = (5, 6)

        x_in = [sem(f"x_in{t}") for t in range(NT)]
        gain_in, vec_in, gate_in = sem("gain_in"), sem("vec_in"), sem("gate_in")
        rows_one, rows_pos = sem("rows_one"), sem("rows_pos")
        gain_ps, gain_sb, vec_ps, vec_sb = sem("gain_ps"), sem("gain_sb"), sem("vec_ps"), sem("vec_sb")
        x_ps, x_taken, x_gain = sem("x_ps"), sem("x_taken"), sem("x_gain")
        x_nat = sem("x_nat")
        ident_done, const_done, pool_step, w_gate_zero = sem("ident_done"), sem("const_done"), sem("pool_step"), sem("w_gate_zero")
        w_in = [sem(f"w_in{n}") for n in range(RING)]
        w_hi, w_lo = sem("w_hi"), sem("w_lo")
        slab_done = sem("slab_done")
        tile_taken = sem("tile_taken")
        x_hi, x_lo, x_sq, x_acc = sem("x_hi"), sem("x_lo"), sem("x_sq"), sem("x_acc")
        xb_hi, xb_lo = sem("xb_hi"), sem("xb_lo")
        stat_ps, stat_read, stat_nat = sem("stat_ps"), sem("stat_read"), sem("stat_nat")
        diag_done, spread_ps, spread_sb = sem("diag_done"), sem("spread_ps"), sem("spread_sb")
        dve_step, act_step, pool_link = sem("dve_step"), sem("act_step"), sem("pool_link")
        z_ps, z_abs, g_soft, g_cum, g_diff = sem("z_ps"), sem("z_abs"), sem("g_soft"), sem("g_cum"), sem("g_diff")
        g_up, g_down, g_end = sem("g_up"), sem("g_down"), sem("g_end")
        g_prep, v_ps, r_silu = sem("g_prep"), sem("v_ps"), sem("r_silu")
        kend_ps, kend_sb, att_ps, att_sb = sem("kend_ps"), sem("kend_sb"), sem("att_ps"), sem("att_sb")
        chunk_ps, state_sb = sem("chunk_ps"), sem("state_sb")
        o_ps, o_sq, o_acc, o_gated = sem("o_ps"), sem("o_sq"), sem("o_acc"), sem("o_gated")
        o_fin, o_hi, o_lo = sem("o_fin"), sem("o_hi"), sem("o_lo")
        f_silu, f_prod, f_hi, f_lo = sem("f_silu"), sem("f_prod"), sem("f_hi"), sem("f_lo")
        c_sq, c_hi, c_lo, c_acc = sem("c_sq"), sem("c_hi"), sem("c_lo"), sem("c_acc")
        turns, trig_done, kr_ps, mask_rows = sem("turns"), sem("trig_done"), sem("kr_ps"), sem("mask_rows")
        piece_ps, piece_taken = sem("piece_ps"), sem("piece_taken")
        qsq, q_sum, q_fac, q_rows = sem("qsq"), sem("q_sum"), sem("q_fac"), sem("q_rows")
        ksq, k_sum, k_fac, k_rows = sem("ksq"), sem("k_sum"), sem("k_fac"), sem("k_rows")
        v_ready = sem("v_ready")
        s_ps, s_bias, p_exp = sem("s_ps"), sem("s_bias"), sem("p_exp")
        pt_ps, pt_sb = sem("pt_ps"), [sem("pt_sb0"), sem("pt_sb1")]
        pv_ps, o_nat = sem("pv_ps"), sem("o_nat")
        ot_ps, ot_hi, ot_lo = sem("ot_ps"), sem("ot_hi"), sem("ot_lo")
        y_ps, y_sb = sem("y_ps"), sem("y_sb")
        y_out = [sem("y_out0"), sem("y_out1")]

        def at_least(eng, s, value):
            if not isinstance(value, int) or value > 0:
                eng.wait_ge(s, value)

        block = ctx.enter_context(nc.Block())

        @block.sync
        def _(sp):
            x_rows = x.rearrange("b (t p) n -> p (b t) n", p=P)

            def load_x(t):
                sp.dma_start(v_g[:, t, :], x_rows[:, t, :]).then_inc(x_in[t], 16)

            load_x(0)

            def load(n, off, src, cols):
                k = src.shape[1]
                if not (isinstance(off, int) and n + off < RING):
                    sp.wait_ge(w_lo, n + off - RING + 1)
                sp.dma_start(w_raw[:, n % RING, 0:k * cols].rearrange("p (k c) -> p k c", c=cols), src)\
                    .then_inc(w_in[n % RING], 16)

            def by_rows(w):
                return w.rearrange("(k p) n -> p k n", p=P)

            def columns(n, w, m0, count):
                for m in range(count):
                    load(n + m, 0, by_rows(w)[:, :, (m0 + m) * P:(m0 + m + 1) * P], P)

            w = a_w_in[0]
            gla_in = by_rows(w)
            load(L_GL, 0, gla_in[:, :, 2 * DK + 2 * DV + GRANK - P:2 * DK + 2 * DV + GRANK], P)
            for t in range(1, NT):
                load_x(t)
            columns(L_Q, w, 0, 3)
            sp.wait_ge(rows_one, 1)
            vec_rows = ((V_BG, a_b_gate, GH), (V_AO, a_out_norm, HV // P), (V_B, b_norm, KT),
                        (V_QL, b_q_latent_norm, QT), (V_F, f_norm, 2 * KT))
            for row, src, count in vec_rows:
                sp.dma_start(rows[row:row + count, :], src.rearrange("a (k p) -> (a k) p", p=P)).then_inc(vec_in, 16)
            for row, src, count in ((V_KV, kv_norm, KT), (V_CL, kv_latent_norm, CT)):
                sp.dma_start(rows[row:row + count, :], src.rearrange("(k p) -> k p", p=P)).then_inc(vec_in, 16)
            sp.dma_start(rows[V_QN:V_QN + 1, 0:NOPE], b_q_norm[:, 0:NOPE]).then_inc(vec_in, 16)
            sp.dma_start(rows[V_KN:V_KN + 1, 0:NOPE], k_norm.rearrange("(a n) -> a n", a=1)[:, 0:NOPE]).then_inc(vec_in, 16)
            sp.dma_start(rope_g[:, 0, :], b_q_norm[0:1, NOPE:QK].to_broadcast([P, ROPE])).then_inc(vec_in, 16)
            sp.dma_start(rope_g[:, 1, :], k_norm.rearrange("(a n) -> a n", a=1)[:, NOPE:QK].to_broadcast([P, ROPE])).then_inc(vec_in, 16)
            sp.wait_ge(w_gate_zero, 1)
            sp.dma_start(w_gate[P - GRANK:P, :], a_w_gate_up[0]).then_inc(gate_in, 16)
            sp.dma_start(pos_i[0:NT, :].bitcast(I32), positions.rearrange("b (t p) -> (b t) p", p=P)).then_inc(gate_in, 16)
            load(L_Q + 3, 0, gla_in[:, :, 3 * P:4 * P], P)
            columns(L_K, w, GH, GH)
            for c in range(2):
                for j in range(4):
                    load(L_V + 4 * c + j, 0, gla_in[:, 2 * j:2 * j + 2, 2 * DK + c * S:2 * DK + (c + 1) * S], S)
            columns(L_R, w, (2 * DK + DV) // P, KT)
            columns(L_WO, a_w_out[0], 0, KT)

            def ffn(n_up, n_dn, layer):
                up, dn = by_rows(f_w_in[layer]), by_rows(f_w_out[layer])
                with sp.Fori(0, FT // 2) as i:
                    for c in range(4):
                        src = up[:, :, (c % 2) * FF:(c % 2 + 1) * FF]
                        load(n_up + c, 4 * i, src[:, :, bass.ts(2 * i + c // 2, P)], P)
                with sp.Fori(0, KT) as i:
                    for c, (k, kn) in enumerate(DOWN):
                        load(n_dn + c, 4 * i, dn[:, k:k + kn, bass.ts(i, P)], P)

            ffn(L_UP1, L_DN1, 0)
            columns(L_CQ, b_w_dq[0], 0, QT)
            def group_load(n, off, g, c):
                k, kn, cols = GROUP_SLABS[c]
                load(n, off, by_rows(b_w_uq[0] if c < 2 else kv_w_up)[:, k:k + kn, bass.ts(g, cols)], cols)

            columns(L_C, kv_w_down, 0, 1)
            for c in range(2):
                group_load(L_Q0 + c, 0, 0, c)
            columns(L_C1, kv_w_down, 1, 1)
            load(L_KR, 0, by_rows(kv_w_down)[:, :, KVRANK + ROPE - P:KVRANK + ROPE], P)
            for c in range(2, 4):
                group_load(L_GRP + c, 0, 0, c)
            with sp.Fori(1, GROUPS) as g:
                for c in range(4):
                    group_load(L_GRP + c, 4 * g, g, c)
            columns(L_WOB, b_w_out[0], 0, KT)
            ffn(L_UP2, L_DN2, 1)

        @block.gpsimd
        def _(pool):
            pool.memset(ident[:, :], 0.0).then_inc(pool_step, 1)
            pool.wait_ge(pool_step, 1)
            pool.affine_select(out=ident[:, :], in_=ident[:, :], compare_op=ALU.not_equal, fill=1.0, base=0,
                               pattern=[[-1, P]], channel_multiplier=1).then_inc(ident_done, 1)
            pool.memset(mask[:, :], 1.0).then_inc(pool_step, 1)
            pool.memset(w_gate[:, :], 0.0).then_inc(w_gate_zero, 1)
            pool.memset(ones[:, :], 1.0)
            pool.memset(att[:, :, :], 0.0)
            for j in range(HALF):
                pool.memset(inv_freq[:, j:j + 1], float(np.float32(THETA ** (-j / HALF))))
            pool.memset(t2[:, 1, :], 1.0).then_inc(pool_step, 1)
            pool.wait_ge(pool_step, 3)
            pool.affine_select(out=mask[:, :], in_=mask[:, :], compare_op=ALU.is_ge, fill=0.0, base=0,
                               pattern=[[1, P]], channel_multiplier=-1).then_inc(pool_step, 1)
            pool.memset(t2[:, 1, :].rearrange("p (c n) -> p c n", n=CHUNK)[:, :, 0:1], 0.0).then_inc(pool_step, 1)
            pool.wait_ge(pool_step, 5)
            pool.memset(mask[0:CHUNK, CHUNK:P], 0.0).then_inc(const_done, 1)

            def lo(n, off, size):
                pool.wait_ge(w_hi, n + off + 1)
                s = n % RING
                pool.tensor_tensor(w_l[:, s, 0:size], w_raw[:, s, 0:size], w_h[:, s, 0:size].bitcast(F32),
                                   ALU.subtract).then_inc(w_lo, 1)

            def run(n, count):
                with pool.Fori(0, count // 4) as i:
                    for c in range(4):
                        lo(n + c, 4 * i, SLAB)

            def down(n):
                with pool.Fori(0, KT) as i:
                    for c, (_, kn) in enumerate(DOWN):
                        lo(n + c, 4 * i, kn * P)

            lo(L_GL, 0, SLAB)
            run(L_Q, L_DN1 - L_Q)
            down(L_DN1)
            for n in range(L_CQ, L_GRP + 4):
                if n == L_C1:
                    pool.wait_ge(slab_done, L_C)
                    for w in (q_tt, k_tt):
                        last = pool.memset(w[:, :, :], 0.0)
                    last.then_inc(mask_rows, 1)
                lo(n, 0, group_slab(n - L_Q0) if L_Q0 <= n < L_C1 else group_slab(n - L_GRP) if n > L_KR else SLAB)

            link = Links(pool, pool_link)
            by_head = [w[:, :, :].rearrange("p (t h) n -> p t h n", h=HG) for w in (q_n, k_n)]

            def factors(scale, h):
                return scale[:, :].rearrange("p (t h) -> p t h", h=HG)[:, :, h:h + 1]

            def query_rows(gi):
                pool.wait_ge(qsq, NT * gi + NT)
                x1, x2 = (by_head[0][:, :, :, NOPE + j * HALF:NOPE + (j + 1) * HALF] for j in range(2))
                space = [t2[:, j // 2, (j % 2) * (S // 2):(j % 2 + 1) * (S // 2)].rearrange("p (t h n) -> p t h n", h=HG, n=HALF)
                         for j in range(4)]
                for j, x_half in enumerate((x1, x2, x1, x2)):
                    last = pool.tensor_tensor(space[j], x_half,
                                              rope_c[:, j, :, :].rearrange("p t (a n) -> p t a n", a=1).to_broadcast([P, NT, HG, HALF]),
                                              ALU.mult)
                link(last)
                pool.tensor_tensor(x1, space[0], space[1], ALU.subtract)
                link(pool.tensor_tensor(x2, space[2], space[3], ALU.add))
                pool.wait_ge(q_fac, gi + 1)
                for h in range(HG):
                    rows_ = by_head[0][:, :, h, :]
                    pool.tensor_tensor(rows_, rows_, factors(q_scale, h).to_broadcast([P, NT, QK]), ALU.mult).then_inc(q_rows, 1)

            def key_rows(gi):
                pool.wait_ge(k_fac, gi + 1)
                for h in range(HG):
                    rows_ = by_head[1][:, :, h, :]
                    pool.tensor_tensor(rows_[:, :, 0:NOPE], kv_n[:, :, h * P:h * P + NOPE],
                                       factors(k_scale, h).to_broadcast([P, NT, NOPE]), ALU.mult)
                    pool.tensor_tensor(rows_[:, :, NOPE:QK], kr[:, 1, :, :], factors(k_scale, h).to_broadcast([P, NT, ROPE]),
                                       ALU.mult).then_inc(k_rows, 1)

            with pool.Fori(0, GROUPS - 1) as g:
                link.enter(g, 2)
                query_rows(g)
                for c in range(2):
                    lo(L_GRP + 4 + c, 4 * g, group_slab(c))
                key_rows(g)
                for c in range(2, 4):
                    lo(L_GRP + 4 + c, 4 * g, group_slab(c))
            link.leave(GROUPS - 1)
            query_rows(GROUPS - 1)
            for c in range(2):
                lo(L_WOB + c, 0, SLAB)
            key_rows(GROUPS - 1)
            for c in range(2, 4):
                lo(L_WOB + c, 0, SLAB)
            run(L_WOB + 4, L_DN2 - L_WOB - 4)
            down(L_DN2)

        @block.tensor
        def _(pe):
            def mm(o, lhs, rhs, start, stop):
                return pe.matmul(o, lhs, rhs, start=start, stop=stop)

            def mm3(o, lhs_h, lhs_l, rhs_h, rhs_l, start, stop):
                mm(o, lhs_h, rhs_l, start, False)
                mm(o, lhs_l, rhs_h, False, False)
                return mm(o, lhs_h, rhs_h, False, stop)

            def slab(n, cols):
                s = n % RING
                return [w[:, s, 0:SLAB // cols * cols].rearrange("p (k c) -> p k c", c=cols) for w in (w_h, w_l)]

            def wait_slab(n, off=0):
                pe.wait_ge(w_lo, n + off + 1)

            def wait_tile(tile, off=0):
                at_least(pe, tile_taken, tile + off - 3)
                if isinstance(tile + off, int) and tile + off < 4:
                    pe.wait_ge(x_taken, tile + 1)

            def column_tile(n, tile, act_h, act_l, off=0, parts=None, between={}):
                wait_slab(n, off)
                wait_tile(tile, off)
                wh, wl = slab(n, P)
                for k in range(KT):
                    if k in between:
                        between[k]()
                    if parts is not None:
                        pe.wait_ge(parts[0], parts[1] + k + 1)
                    last = mm3(bank[tile % 4][:, :], wh[:, k, :], wl[:, k, :], act_h[:, k, :], act_l[:, k, :],
                               k == 0, k == KT - 1)
                last.then_inc(slab_done, 1)

            def stat_sum(s, spreads, ready, count, where=STAT):
                pe.wait_ge(ready, count)
                at_least(pe, stat_read, s)
                at_least(pe, spread_sb, spreads)
                for t in range(NT):
                    last = mm(bank[where][:, t:t + 1], acc[:, t * P:(t + 1) * P], ones[:, 0:1], True, True)
                last.then_inc(stat_ps, 1)

            def stat_spread(b, where=STAT):
                pe.wait_ge(diag_done, b + 1)
                for t in range(NT):
                    last = mm(bank[where][:, t * P:(t + 1) * P], ones[:, :], diag[:, t, :], True, True)
                last.then_inc(spread_ps, 1)

            pe.wait_ge(ident_done, 1)
            pe.wait_ge(gain_in, 16)
            pe.transpose(bank[GAIN][:, 0:KT], rows[0:KT, :], ident[0:KT, 0:KT]).then_inc(gain_ps, 1)
            for t in range(NT):
                pe.wait_ge(x_in[t], 16)
                if t == NT - 1:
                    pe.wait_ge(gain_sb, 1)
                for m in range(KT):
                    last = pe.transpose(bank[2 * t + m // 4][:, m % 4 * P:(m % 4 + 1) * P], v_g[:, t, m * P:(m + 1) * P], ident[:, :])
                    if m % 4 == 3:
                        last.then_inc(x_ps, 1)

            wait_slab(L_GL)
            wait_tile(T_GL)
            wh, wl = slab(L_GL, P)
            for half in range(2):
                pe.wait_ge(x_lo, NT * (half + 1))
                cols = slice(half * (S // 2), (half + 1) * (S // 2))
                for k in range(KT):
                    last = mm3(bank[T_GL][:, cols], wh[:, k, :], wl[:, k, :], a_h[:, k, cols], a_l[:, k, cols], k == 0, k == KT - 1)
            last.then_inc(slab_done, 1)
            pe.wait_ge(vec_in, 16 * 11)
            pe.wait_ge(rows_pos, 1)
            pe.wait_ge(x_taken, STAT + 1)
            pe.transpose(bank[STAT][:, 0:NVEC], rows[0:NVEC, :], ident[0:NVEC, 0:NVEC])
            pe.transpose(bank[STAT][:, NVEC:NVEC + NT], pos_f[0:NT, :], ident[0:NT, 0:NT]).then_inc(vec_ps, 1)
            column_tile(L_Q, T_Q, a_h, a_l)
            pe.wait_ge(vec_sb, 1)
            column_tile(L_Q + 1, T_Q + 1, a_h, a_l)
            stat_spread(0)

            def gate_logits(h):
                if h == 0:
                    pe.wait_ge(tile_taken, T_GL + 1)
                    pe.wait_ge(gate_in, 32)
                    pe.wait_ge(const_done, 1)
                    pe.wait_ge(x_taken, KT)
                if h == 3:
                    pe.wait_ge(z_abs, 1)
                mm(bank[GATE_BANKS[h]][:, :], w_gate[:, h * HK:(h + 1) * HK], gl_t[:, :], True, True).then_inc(z_ps, 1)

            column_tile(L_Q + 2, T_Q + 2, a_h, a_l, between={k: lambda h=k - 4: gate_logits(h) for k in (4, 5, 6)})
            column_tile(L_Q + 3, T_Q + 3, a_h, a_l, between={0: lambda: gate_logits(3)})
            for h in range(GH):
                column_tile(L_K + h, T_K + h, a_h, a_l)
            for c in range(2):
                for j in range(4):
                    wait_slab(L_V + 4 * c + j)
                    wh, wl = slab(L_V + 4 * c + j, S)
                    for t in range(NT):
                        if j == 0:
                            wait_tile(T_V + 4 * c + t)
                        for k in range(2):
                            kk = 2 * j + k
                            last = mm3(bank[(T_V + t) % 4][:, :], a_h[:, kk, t * P:(t + 1) * P], a_l[:, kk, t * P:(t + 1) * P],
                                       wh[:, k, :], wl[:, k, :], kk == 0, kk == KT - 1)
                        if j == 3 and t < NT - 1:
                            last.then_inc(v_ps, 1)
                    last.then_inc(slab_done, 1)

            def turn_keys(h):
                pe.wait_ge(g_prep, h + 1)
                if h == 0:
                    pe.wait_ge(z_abs, GH)
                    pe.wait_ge(spread_sb, 1)
                else:
                    pe.wait_ge(state_sb, (NCH - 1) * h)
                for t in range(NT):
                    last = pe.transpose(bank[KV_BANKS[0]][:, t * P:(t + 1) * P], d_t[:, h, t * P:(t + 1) * P], ident[:, :])
                last.then_inc(kend_ps, 1)
                for t in range(NT):
                    last = mm(bank[KV_BANKS[1]][:, t * P:(t + 1) * P], b_t[:, h, t * P:(t + 1) * P], q_t[:, h, t * P:(t + 1) * P], True, True)
                last.then_inc(att_ps, 1)

            def chunk_states(h, chunks):
                for c in chunks:
                    if c == 0:
                        pe.wait_ge(kend_sb, h + 1)
                        pe.wait_ge(att_sb, h + 1)
                        pe.wait_ge(tile_taken, T_V + 8)
                    if c == 4 or c == 5:
                        pe.wait_ge(state_sb, (NCH - 1) * h + c - 1)
                    half = slice(CHUNK * (c % 2), CHUNK * (c % 2 + 1))
                    col = c // 2 % 2 * HV
                    mm(bank[KV_BANKS[c % 2]][:, col:col + HV], k_end[half, c // 2, :], v_g[half, c // 2, h * HV:(h + 1) * HV], True, True)\
                        .then_inc(chunk_ps, 1)

            def gla_outputs(h):
                at_least(pe, o_gated, h)
                at_least(pe, spread_sb, h + 1)
                for t in range(NT):
                    for e in range(2):
                        cols = slice(h * HV + e * P, h * HV + (e + 1) * P)
                        o = bank[O_BANKS[e]]
                        last = mm(o[:, t * P:(t + 1) * P], v_g[:, t, cols], att[:, t, :], True, False)
                        for c in (2 * t, 2 * t + 1):
                            if c:
                                pe.wait_ge(state_sb, (NCH - 1) * h + c)
                                last = mm(o[:, c * CHUNK:(c + 1) * CHUNK], state[:, c, e * P:(e + 1) * P],
                                          q_t[:, h, c * CHUNK:(c + 1) * CHUNK], False, c == 2 * t + 1)
                last.then_inc(o_ps, 1)

            def head_sums(h):
                if h:
                    pe.wait_ge(o_gated, h)
                    stat_sum(h, h, o_acc, h, O_BANKS[0])

            def states_and_spread(h):
                chunk_states(h, range(0, 4))
                if h:
                    stat_spread(h, O_BANKS[0])

            for h in range(GH):
                column_tile(L_R + 2 * h, T_R + 2 * h, a_h, a_l, between={
                    0: lambda: turn_keys(h), 3: lambda: head_sums(h), KT - 1: lambda: states_and_spread(h)})
                column_tile(L_R + 2 * h + 1, T_R + 2 * h + 1, a_h, a_l, between={
                    2: lambda: chunk_states(h, range(4, NCH - 1)), KT - 2: lambda: gla_outputs(h)})

            def project_out(n, tile, ready, count, between):
                some, early = 3, KT - 2
                parts_of = [slab(n + m, P) for m in range(some)]

                def step(m, k, stop):
                    wh, wl = parts_of[m]
                    if m == 0:
                        pe.wait_ge(ready, count - KT + k + 1)
                    return mm3(bank[(tile + m) % 4][:, :], wh[:, k, :], wl[:, k, :], a_h[:, k, :], a_l[:, k, :], k == 0, stop)

                for m in range(some):
                    wait_slab(n + m)
                    wait_tile(tile + m)
                    for k in range(early):
                        step(m, k, False)
                    if m in between:
                        between[m]()
                for m in range(some):
                    step(m, early, False)
                    step(m, early + 1, True).then_inc(slab_done, 1)
                for m in range(some, KT):
                    column_tile(n + m, tile + m, a_h, a_l)

            project_out(L_WO, T_WO, o_lo, KT, {0: lambda: stat_sum(GH, GH, o_acc, GH), 1: lambda: stat_spread(GH)})

            def ffn_up(n, tile, s, spreads, xs):
                column_tile(n, tile, b_h, b_l, parts=(x_lo, xs - KT))
                stat_sum(s, spreads, x_acc, xs - KT)
                column_tile(n + 1, tile + 1, b_h, b_l)
                stat_spread(spreads)
                for c in (2, 3):
                    column_tile(n + c, tile + c, b_h, b_l)
                with pe.Fori(1, FT // 2) as i:
                    for c in range(4):
                        column_tile(n + c, tile + c, b_h, b_l, 4 * i)

            def ffn_down(n, tile, hidden, last_layer):
                def down_tile(m, i):
                    for c, (k0, kn) in enumerate(DOWN):
                        wait_slab(n + 4 * m + c, 16 * i)
                        wh, wl = slab(n + c, P)
                        if c == 0:
                            wait_tile(tile + m, 4 * i)
                        for k in range(kn):
                            if m == 0:
                                pe.wait_ge(f_lo, hidden - FT + k0 + k + 1)
                            last = mm3(bank[(tile + m) % 4][:, :], wh[:, k, :], wl[:, k, :], hid_h[:, k0 + k, :], hid_l[:, k0 + k, :],
                                       k0 + k == 0, k0 + k == FT - 1)
                        last.then_inc(slab_done, 1)

                def turn_back(m, i, first):
                    pe.wait_ge(tile_taken, tile + m + 4 * i + 1)
                    if not first:
                        pe.wait_ge(y_sb, m + 4 * i - 1)
                    for t in range(NT):
                        last = pe.transpose(bank[Y_BANKS[m % 2]][:, t * P:(t + 1) * P], t2[:, m % 2, t * P:(t + 1) * P], ident[:, :])
                    last.then_inc(y_ps, 1)

                if not last_layer:
                    with pe.Fori(0, KT // 4) as i:
                        for m in range(4):
                            down_tile(m, i)
                else:
                    for m in range(KT):
                        down_tile(m, 0)
                        if m:
                            turn_back(m - 1, 0, m - 1 < 2)
                    turn_back(KT - 1, 0, False)

            ffn_up(L_UP1, T_UP1, 5, 5, 2 * KT)
            ffn_down(L_DN1, T_DN1, FT, False)

            column_tile(L_CQ, T_CQ, b_h, b_l, parts=(x_lo, 2 * KT))
            stat_sum(6, 6, x_acc, 2 * KT)
            column_tile(L_CQ + 1, T_CQ + 1, b_h, b_l)
            stat_spread(6)
            column_tile(L_CQ + 2, T_CQ + 2, b_h, b_l)
            column_tile(L_C, T_C, a_h, a_l, parts=(xb_lo, 0), between={KT - 2: lambda: stat_sum(7, 7, c_acc, QT)})

            def piece(u, gi, dst, waiting, slabs=L_GRP):
                kind, t = PIECES[u]
                at_least(pe, piece_taken, 16 * gi + u - waiting + 1)
                if kind == "kv" or kind == "q":
                    split, kts = ((c_h, c_l), CT) if kind == "kv" else ((cq_h, cq_l), QT)
                    for c in (2, 3) if kind == "kv" else (0, 1):
                        if t == 0:
                            wait_slab(slabs + c, 4 * gi)
                        k0, kn, width = GROUP_SLABS[c]
                        wh, wl = slab(slabs + c, width)
                        for k in range(k0, k0 + kn):
                            last = mm3(dst[:, 0:width], split[0][:, k, t * P:(t + 1) * P], split[1][:, k, t * P:(t + 1) * P],
                                       wh[:, k - k0, :], wl[:, k - k0, :], k == 0, k == kts - 1)
                        if t == NT - 1:
                            last.then_inc(slab_done, 1)
                    if t < NT - 1:
                        last.then_inc(piece_ps, 1)
                else:
                    src = k_n if kind == "kt" else q_n
                    pe.wait_ge(k_rows if kind == "kt" else q_rows, HG * gi + t + 1)
                    for j in range(NT):
                        last = pe.transpose(dst[0:QK, j * P:(j + 1) * P], src[:, HG * j + t, :], ident[:, :])
                    last.then_inc(piece_ps, 1)

            for u in range(UNITS):
                if PIECES[u] == ("q", 0):
                    pe.wait_ge(c_lo, QT)
                if PIECES[u] == ("kv", 0):
                    column_tile(L_C1, T_C + 1, a_h, a_l)
                    column_tile(L_KR, T_KR, a_h, a_l, between={KT - 2: lambda: stat_sum(8, 7, c_acc, QT + CT)})
                    pe.wait_ge(c_lo, QT + CT)
                if PIECES[u] == ("kv", 2):
                    pe.wait_ge(tile_taken, T_KR + 1)
                    for t in range(NT):
                        last = pe.transpose(bank[T_KRT % 4][:, t * ROPE:(t + 1) * ROPE], t1[P - ROPE:P, 1, t * P:(t + 1) * P],
                                            ident[P - ROPE:P, P - ROPE:P])
                    last.then_inc(kr_ps, 1)
                piece(u, 0, bank[FIRST_PIECES[u % 3]], 3, L_Q0 if PIECES[u][0] == "q" else L_GRP)

            def scores(v, gi):
                h, t = v // NT % HG, v % NT
                n = 16 * gi + v
                at_least(pe, p_exp, n - NT + 1)
                if t == 0:
                    gk = 16 * (gi + v // UNITS)
                    pe.wait_ge(piece_taken, gk + 1 + max(PIECES.index(("kt", h)), PIECES.index(("qt", h))))
                mm(bank[t][:, 0:(t + 1) * P], q_tt[0:QK + NT, h, t * P:(t + 1) * P], k_tt[0:QK + NT, h, 0:(t + 1) * P], True, True)\
                    .then_inc(s_ps, 1)

            def turn(u, gi):
                h, t = divmod(u, NT)
                n = 16 * gi + u
                pe.wait_ge(p_exp, n + 1)
                at_least(pe, pt_sb[1 - u % 2], 8 * gi + (u + 1) // 2)
                for j in range(t + 1):
                    last = pe.transpose(bank[PT_BANK][:, j * P:(j + 1) * P], prob[:, t, j * P:(j + 1) * P], ident[:, :])
                last.then_inc(pt_ps, 1)

            def values(u, gi):
                h, t = divmod(u, NT)
                pe.wait_ge(pt_sb[u % 2], 8 * gi + u // 2 + 1)
                if t == 0:
                    pe.wait_ge(v_ready, HG * gi + h + 1)
                    at_least(pe, o_nat, HG * gi + h - 1)
                    if h % 2:
                        at_least(pe, ot_lo, 2 * gi + h // 2)
                for j in range(t + 1):
                    last = mm(bank[PV_BANKS[h % 2]][:, t * MV:(t + 1) * MV], prob_t[:, u % 2, j * P:(j + 1) * P], v_cur[:, j, h, :],
                              j == 0, j == t)
                last.then_inc(pv_ps, 1)

            def outputs(pair, gi):
                pe.wait_ge(o_nat, HG * gi + 2 * pair + 2)
                for t in range(NT):
                    last = pe.transpose(bank[PV_BANKS[1]][:, t * P:(t + 1) * P], o_n[:, t, :], ident[:, :])
                last.then_inc(ot_ps, 1)

            def group(gi, first, more):
                for u in range(UNITS):
                    turn(u, gi)
                    if u + AHEAD < UNITS or more:
                        scores(u + AHEAD, gi)
                    if u == 2 and not first:
                        outputs(1, gi - 1)
                    if u == 10:
                        outputs(0, gi)
                    if more:
                        piece(u, gi + 1, bank[PIECE], 1)
                    if u:
                        values(u - 1, gi)
                    elif not first:
                        values(UNITS - 1, gi - 1)

            pe.wait_ge(tile_taken, T_KRT + 1)
            pe.wait_ge(mask_rows, 2)
            for v in range(AHEAD):
                scores(v, 0)
            pe.wait_ge(stat_read, 9)
            pe.wait_ge(piece_taken, UNITS)
            group(0, True, True)
            with pe.Fori(1, GROUPS - 1) as g:
                group(g, False, True)
            group(GROUPS - 1, False, False)
            project_out(L_WOB, T_WOB, ot_lo, KT, {0: lambda: values(UNITS - 1, GROUPS - 1), 1: lambda: outputs(1, GROUPS - 1)})
            ffn_up(L_UP2, T_UP2, 9, 7, 4 * KT)
            ffn_down(L_DN2, T_DN2, 2 * FT, True)

        @block.scalar
        def _(act):
            link = Links(act, act_step)

            def copy(o, i, **kw):
                return act.activation(o, i, ACT.Copy, **kw)

            def hi(n, off, size):
                s = n % RING
                act.wait_ge(w_in[s], 16 * (n // RING + 1) + 4 * off)
                if not (isinstance(off, int) and n + off < RING):
                    act.wait_ge(slab_done, n + off - RING + 1)
                copy(w_h[:, s, 0:size], w_raw[:, s, 0:size]).then_inc(w_hi, 1)

            def size_of(n):
                if L_DN1 <= n < L_CQ:
                    return DOWN[(n - L_DN1) % 4][1] * P
                if n >= L_DN2:
                    return DOWN[(n - L_DN2) % 4][1] * P
                if L_Q0 <= n < L_C1:
                    return group_slab(n - L_Q0)
                if L_KR < n < L_WOB:
                    return group_slab((n - L_GRP) % 4)
                return SLAB

            def hi_next(n, off=0):
                if n + RING < L_END:
                    hi(n + RING, off, size_of(n + RING))

            act.wait_ge(rows_one, 1)
            act.dma_start(rows[V_A:V_A + KT, :], a_norm.rearrange("a (k p) -> (a k) p", p=P)).then_inc(gain_in, 16)

            def x_tile(m, n_x, tile, gain, dst):
                act.wait_ge(tile_taken, tile + m + 1)
                copy(dst[:, m, :], x_t[:, m, :], scale=vecs[:, gain + m:gain + m + 1]).then_inc(x_hi, 1)
                at_least(act, x_acc, n_x - KT + m - 1)
                act.activation(sq[:, m % 2, :], x_t[:, m, :], ACT.Square).then_inc(x_sq, 1)

            def spread(b, dst, where=STAT):
                act.wait_ge(spread_ps, b + 1)
                copy(dst[:, :], bank[where][:, :]).then_inc(spread_sb, 1)

            def some_tiles(w, n):
                t, i = divmod(n, 2)
                return w[:, 4 * i:4 * i + 4, t * P:(t + 1) * P]

            def x_hi_part(n):
                act.wait_ge(x_gain, n + 1)
                copy(some_tiles(a_h, n), t1[:, n % 2, :].rearrange("p (m n) -> p m n", n=P)).then_inc(x_hi, 1)

            def take_x(n):
                act.wait_ge(x_ps, n + 1)
                copy(some_tiles(x_t, n), bank[n][:, :].rearrange("p (m n) -> p m n", n=P)).then_inc(x_taken, 1)

            def token_squares(t):
                act.wait_ge(x_in[t], 16)
                at_least(act, x_nat, t)
                act.activation(sq[:, :, :].rearrange("p a n -> p (a n)"), v_g[:, t, :], ACT.Square,
                               accum_out=r_nat[:, 3, t:t + 1]).then_inc(x_nat, 1)

            for n in range(KT):
                x_hi_part(n)
                if n == 1:
                    hi(L_GL, 0, SLAB)
                if n == 3:
                    take_x(0)
            hi(L_Q, 0, SLAB)
            for n in range(1, 5):
                take_x(n)
            hi(L_Q + 1, 0, SLAB)
            for t in range(NT):
                token_squares(t)
            for n in range(5, KT):
                take_x(n)
            hi(L_Q + 2, 0, SLAB)

            hi_next(L_GL)
            hi_next(L_Q)
            spread(0, rinv_b)
            for h in range(GH):
                act.wait_ge(z_abs, h + 1)
                link(act.activation(gt[:, h % 2, :], gt[:, h % 2, :], ACT.Exp))
                act.activation(gt[:, h % 2, :], gt[:, h % 2, :], ACT.Ln, bias=1.0).then_inc(g_soft, 1)
                if h < 3:
                    hi_next(L_Q + 1 + h)
            for h in range(GH):
                hi_next(L_K + h)
                act.wait_ge(g_cum, h + 1)
                at_least(act, g_prep, h - 1)
                act.activation(e_ring[:, h % 2, :], b_t[:, h, :], ACT.Exp, scale=1.0 / TAU).then_inc(g_up, 1)
                ends = b_t[:, h, :].rearrange("p (c n) -> p c n", n=CHUNK)[:, :, CHUNK - 1]
                link(act.activation(dec[:, h, :], ends, ACT.Exp, scale=1.0 / TAU))
                act.wait_ge(g_diff, h + 1)
                act.activation(b_t[:, h, :], b_t[:, h, :], ACT.Exp, scale=-1.0 / TAU).then_inc(g_down, 1)
                act.activation(d_t[:, h, :], d_t[:, h, :], ACT.Exp, scale=1.0 / TAU).then_inc(g_end, 1)
            for n in range(4):
                hi_next(L_V + n)
            act.wait_ge(turns, 1)
            act.activation(trig[:, :, :, :], t1[:, 0, 0:2 * NT * HALF].rearrange("p (a t j) -> p a t j", a=2, t=NT), ACT.Sin,
                           scale=float(2.0 * np.pi)).then_inc(trig_done, 1)
            for n in range(4, 8):
                hi_next(L_V + n)

            def o_split(h):
                for e in range(2):
                    act.wait_ge(o_fin, 2 * h + e + 1)
                    copy(a_h[:, 2 * h + e, :], sr[:, 2 * h + e, :]).then_inc(o_hi, 1)

            def gate(m):
                act.wait_ge(tile_taken, T_R + m + 1)
                act.activation(sr[:, m, :], t1[:, m % 2, :], ACT.Silu).then_inc(r_silu, 1)

            for h in range(GH):
                act.wait_ge(kend_ps, h + 1)
                at_least(act, chunk_ps, (NCH - 1) * h)
                copy(k_end[:, :, :], bank[KV_BANKS[0]][:, :].rearrange("p (t n) -> p t n", n=HK)).then_inc(kend_sb, 1)
                if h:
                    spread(h, rinvo_b, O_BANKS[0])
                hi_next(L_R + 2 * h)
                gate(2 * h)
                act.wait_ge(o_ps, h + 1)
                at_least(act, o_acc, h)
                for e in range(2):
                    act.activation(sq[:, e, :], bank[O_BANKS[e]][:, :], ACT.Square).then_inc(o_sq, 1)
                if h < GH - 1:
                    hi_next(L_R + 2 * h + 1)
                    gate(2 * h + 1)
            act.wait_ge(slab_done, L_WO)
            for h in range(GH - 1):
                o_split(h)
            hi_next(L_WO - 1)
            gate(KT - 1)
            spread(GH, rinvo_b)
            o_split(GH - 1)

            def project_out(n, tile, n_x, gain):
                for m in range(KT):
                    hi_next(n + m)
                    x_tile(m, n_x, tile, gain, b_h)

            project_out(L_WO, T_WO, KT, V_F)

            def ffn_up(n, tile, hidden, b):
                def pair(i, c, off, last):
                    m = hidden + 2 * i + c
                    hi_next(n + 2 * c + (2 * FT - 4 if last else 0), 0 if last else off)
                    if b is not None and c == 0 and isinstance(i, int) and i == 0:
                        spread(b, rinv_b)
                    act.wait_ge(tile_taken, tile + 4 * i + 2 * c + 1)
                    act.activation(t1[:, c, :], t1[:, c, :], ACT.Silu).then_inc(f_silu, 1)
                    hi_next(n + 2 * c + 1 + (2 * FT - 4 if last else 0), 0 if last else off)
                    act.wait_ge(f_prod, m + 1)
                    copy(hid_h[:, bass.ts(2 * i + c, 1), :] if not isinstance(i, int) else hid_h[:, 2 * i + c:2 * i + c + 1, :],
                         t2[:, c:c + 1, :]).then_inc(f_hi, 1)

                for c in range(2):
                    pair(0, c, 0, False)
                with act.Fori(1, FT // 2 - 1) as i:
                    for c in range(2):
                        pair(i, c, 4 * i, False)
                for c in range(2):
                    pair(FT // 2 - 1, c, 0, True)

            def ffn_down(n, tile, n_x, gain):
                for m in range(KT):
                    for c in range(4):
                        hi_next(n + 4 * m + c)
                    if gain is not None:
                        x_tile(m, n_x, tile, gain, b_h)
                    elif m:
                        turn_back(m - 1)

            def turn_back(m):
                act.wait_ge(y_ps, m + 1)
                if m >= 2:
                    act.wait_ge(y_out[m % 2], 16 * (m // 2))
                copy(t1[:, m % 2, :], bank[Y_BANKS[m % 2]][:, :]).then_inc(y_sb, 1)
                act.wait_ge(y_sb, m + 1)
                y_cols = out.rearrange("b (t p) n -> p (b t) n", p=P)
                act.dma_start(y_cols[:, :, m * P:(m + 1) * P], t1[:, m % 2, :].rearrange("p (t n) -> p t n", n=P))\
                    .then_inc(y_out[m % 2], 16)

            ffn_up(L_UP1, T_UP1, 0, 5)
            ffn_down(L_DN1, T_DN1, 2 * KT, V_B)

            def latent(j, gain, dst, m):
                act.wait_ge(tile_taken, T_CQ + j + 1)
                copy(dst[:, m, :], t1[:, j % 2, :], scale=vecs[:, gain + m:gain + m + 1]).then_inc(c_hi, 1)
                act.wait_ge(x_acc, 2 * KT)
                at_least(act, c_acc, j - 1)
                act.activation(sq[:, j % 2, :], t1[:, j % 2, :], ACT.Square).then_inc(c_sq, 1)

            act.wait_ge(slab_done, L_CQ)
            for m in range(KT):
                copy(a_h[:, m, :], x_t[:, m, :], scale=vecs[:, V_KV + m:V_KV + m + 1]).then_inc(xb_hi, 1)
            hi_next(L_CQ)
            spread(6, rinv_b)
            hi_next(L_CQ + 1)
            for j in range(QT):
                if j == 2:
                    hi_next(L_CQ + 2)
                latent(j, V_QL, cq_h, j)
            hi_next(L_C)
            latent(QT, V_CL, c_h, 0)

            def piece(u, gi, src, first=False):
                kind, t = PIECES[u]
                if kind in ("kv", "q") and t == NT - 1:
                    act.wait_ge(slab_done, L_C1 if first and kind == "q" else L_GRP + 4 * gi + (4 if kind == "kv" else 2))
                else:
                    act.wait_ge(piece_ps, NCOUNTED * gi + COUNTED[u] + 1)
                if kind == "kv":
                    if t == 0:
                        at_least(act, v_ready, HG * gi)
                    copy(kv_n[:, t, :], src[:, :], scale=r_nat[:, 1, t:t + 1]).then_inc(piece_taken, 1)
                elif kind == "q":
                    copy(q_n[:, HG * t:HG * (t + 1), :], src[:, 0:HG * QK].rearrange("p (h n) -> p h n", n=QK),
                         scale=r_nat[:, 2, t:t + 1]).then_inc(piece_taken, 1)
                else:
                    dst, gain = (k_tt, V_KN) if kind == "kt" else (q_tt, V_QN)
                    copy(dst[0:QK, t, :], src[0:QK, :], scale=vecs[0:QK, gain:gain + 1]).then_inc(piece_taken, 1)
                if kind == "q":
                    act.wait_ge(piece_taken, 16 * gi + u + 1)
                    at_least(act, k_sum, NT * gi + t + 1 - NT)
                    act.activation(sq_g[:, HG * t:HG * (t + 1), :], q_n[:, HG * t:HG * (t + 1), :], ACT.Square).then_inc(qsq, 1)
                if kind == "kv":
                    act.wait_ge(piece_taken, 16 * gi + u + 1)
                    act.wait_ge(q_sum, NT * gi + t + 1)
                    act.activation(sq_g[:, HG * t:HG * (t + 1), 0:NOPE],
                                   kv_n[:, t, :].rearrange("p (h n) -> p h n", n=P)[:, :, 0:NOPE], ACT.Square).then_inc(ksq, 1)

            def exps(v, gi):
                t = v % NT
                n = 16 * gi + v
                act.wait_ge(s_bias, n + 1)
                at_least(act, pt_ps, n - NT + 1)
                w = (t + 1) * P
                col = v % UNITS
                act.activation(prob[:, t, 0:w], bank[t][:, 0:w], ACT.Exp,
                               bias=stat[:, 0, col:col + 1], accum_out=stat[:, 1, col:col + 1]).then_inc(p_exp, 1)

            def turned(u, gi):
                if u % 2 == 0:
                    act.wait_ge(pt_ps, 16 * gi + u + 1)
                    at_least(act, pv_ps, 16 * gi + u - 1)
                    w = (u % NT + 1) * P
                    copy(prob_t[:, 0, 0:w], bank[PT_BANK][:, 0:w]).then_inc(pt_sb[0], 1)

            def outputs(pair, gi):
                act.wait_ge(ot_ps, 2 * gi + pair + 1)
                dst = a_h[:, 2 * gi + pair:2 * gi + pair + 1, :] if isinstance(gi, int) else a_h[:, bass.ts(2 * gi + pair, 1), :]
                copy(dst, bank[PV_BANKS[1]][:, :].rearrange("p (a n) -> p a n", a=1)).then_inc(ot_hi, 1)

            NEXT_SLAB = (5, 6, 9, 10)

            def group(gi, first, more, last=False):
                for u in range(UNITS):
                    turned(u, gi)
                    if u + AHEAD - 1 < UNITS or more:
                        exps(u + AHEAD - 1, gi)
                    if u == 2 and not first:
                        outputs(1, gi - 1)
                    if u == 10:
                        outputs(0, gi)
                    if more:
                        piece(u, gi + 1, bank[PIECE])
                    if more and u in NEXT_SLAB:
                        n = L_GRP + NEXT_SLAB.index(u)
                        if last:
                            hi_next(n + 4 * (GROUPS - 1))
                        else:
                            hi_next(n, 4 * gi + 4)

            for u in range(UNITS):
                if PIECES[u] == ("q", 0):
                    act.wait_ge(stat_nat, 1)
                if PIECES[u] == ("kv", 0):
                    latent(QT + 1, V_CL, c_h, 1)
                    hi_next(L_C1)
                    hi_next(L_KR)
                    act.wait_ge(stat_nat, 2)
                piece(u, 0, bank[FIRST_PIECES[u % 3]], True)
                if PIECES[u] in (("q", NT - 1), ("kv", NT - 1)):
                    for c in range(2):
                        hi_next((L_Q0 if PIECES[u][0] == "q" else L_GRP + 2) + c)
            for v in range(AHEAD - 1):
                exps(v, 0)
            group(0, True, True)
            with act.Fori(1, GROUPS - 2) as g:
                group(g, False, True)
            group(GROUPS - 2, False, True, True)
            group(GROUPS - 1, False, False)
            outputs(1, GROUPS - 1)

            project_out(L_WOB, T_WOB, 3 * KT, V_F + KT)
            ffn_up(L_UP2, T_UP2, FT, 7)
            ffn_down(L_DN2, T_DN2, 0, None)
            turn_back(KT - 1)
            for s in y_out:
                act.wait_ge(s, 16 * KT // 2)

        @block.vector
        def _(dve):
            link = Links(dve, dve_step)

            def tt(o, a, b, op):
                return dve.tensor_tensor(o, a, b, op)

            def stt(o, a, scalar, b, op0, op1):
                return dve.scalar_tensor_tensor(out=o, in0=a, scalar=scalar, in1=b, op0=op0, op1=op1)

            def ts(o, a, s1, s2, op0, op1=None):
                if op1 is None:
                    return dve.tensor_scalar(o, a, s1, None, op0)
                return dve.tensor_scalar(o, a, s1, s2, op0, op1)

            def guess(sums, width, eps, count, signal=None):
                m, y = (nw[:, j, 0:count] for j in range(2))
                first = ts(m, sums, 1.0 / width, eps, ALU.mult, ALU.add)
                if signal is not None:
                    first.then_inc(signal[0], 1)
                    dve.wait_ge(signal[0], signal[1])
                else:
                    link(first)
                link(ts(y.bitcast(I32), m.bitcast(I32), -0.5, float(0x5f3759df), ALU.mult, ALU.add))

            def newton(count, dst=None):
                m, y, a = (nw[:, j, 0:count] for j in range(3))
                link(tt(a, y, y, ALU.mult))
                link(stt(a, a, -0.5, m, ALU.mult, ALU.mult))
                last = stt(y if dst is None else dst, a, 1.5, y, ALU.add, ALU.mult)
                if dst is None:
                    link(last)
                return last

            def x_tile(m, n_x, gain, dst_h, dst_l):
                n = n_x + m
                dve.wait_ge(x_hi, n + 1)
                stt(dst_l[:, m, :], x_t[:, m, :], vecs[:, gain + m:gain + m + 1], dst_h[:, m, :].bitcast(F32),
                    ALU.mult, ALU.subtract).then_inc(x_lo, 1)
                n -= KT
                dve.wait_ge(x_sq, n + 1)
                if m == 0:
                    dve.tensor_copy(acc[:, :], sq[:, 0, :]).then_inc(x_acc, 1)
                else:
                    dve.wait_ge(x_acc, n)
                    tt(acc[:, :], acc[:, :], sq[:, m % 2, :], ALU.add).then_inc(x_acc, 1)

            def norm(s, row, spreads=None, width=D, where=STAT):
                if s:
                    dve.wait_ge(stat_ps, s)
                guess(bank[where][:, 0:NT] if s else r_nat[:, 3, :], width, EPS, NT, (stat_read, s + 1))
                newton(NT)
                newton(NT)
                last = newton(NT, r_nat[:, row, :])
                if spreads is None:
                    last.then_inc(stat_nat, 1)
                    return
                link(last)
                at_least(dve, spread_ps, spreads)
                for t in range(NT):
                    last = ts(diag[:, t, :], ident[:, :], r_nat[:, row, t:t + 1], None, ALU.mult)
                last.then_inc(diag_done, 1)

            dve.memset(rows[:, :], 1.0).then_inc(rows_one, 1)
            dve.wait_ge(gain_ps, 1)
            dve.tensor_copy(vecs[:, 0:KT], bank[GAIN][:, 0:KT]).then_inc(gain_sb, 1)
            dve.wait_ge(gain_sb, 1)

            for n in range(KT + 1):
                if n < KT:
                    dve.wait_ge(x_ps, n + 1)
                    at_least(dve, x_lo, n - 1)
                    gains = vecs[:, 4 * (n % 2):4 * (n % 2) + 4].rearrange("p (m a) -> p m a", a=1).to_broadcast([P, 4, P])
                    tt(t1[:, n % 2, :].rearrange("p (m n) -> p m n", n=P), bank[n][:, :].rearrange("p (m n) -> p m n", n=P), gains,
                       ALU.mult).then_inc(x_gain, 1)
                if n:
                    t, i = divmod(n - 1, 2)
                    cut = (slice(None), slice(4 * i, 4 * i + 4), slice(t * P, (t + 1) * P))
                    dve.wait_ge(x_hi, n)
                    tt(a_l[cut], t1[:, i, :].rearrange("p (m n) -> p m n", n=P), a_h[cut].bitcast(F32), ALU.subtract).then_inc(x_lo, 1)

            dve.wait_ge(gate_in, 32)
            dve.tensor_copy(pos_f[0:NT, :], pos_i[0:NT, :].bitcast(I32)).then_inc(rows_pos, 1)
            dve.wait_ge(vec_ps, 1)
            dve.tensor_copy(vecs[:, KT:NVEC + NT], bank[STAT][:, KT:NVEC + NT]).then_inc(vec_sb, 1)
            dve.wait_ge(vec_sb, 1)
            dve.wait_ge(x_nat, NT)

            norm(0, 0, 0)
            dve.wait_ge(spread_sb, 1)
            dve.wait_ge(slab_done, L_GL + 1)
            tt(gl_t[:, :], bank[T_GL % 4][:, :], rinv_b[:, :], ALU.mult).then_inc(tile_taken, 1)
            for h in range(GH):
                dve.wait_ge(z_ps, h + 1)
                if h >= 2:
                    dve.wait_ge(g_soft, h - 1)
                    link(stt(gt[:, h % 2, :], b_t[:, h - 2, :], 0.0, gt[:, h % 2, :], ALU.min, ALU.subtract))
                    dve.tensor_tensor_scan(b_t[:, h - 2, :], t2[:, 1, :], gt[:, h % 2, :], 0.0, ALU.mult, ALU.add).then_inc(g_cum, 1)
                    dve.wait_ge(g_cum, h - 1)
                link(ts(b_t[:, h, :], bank[GATE_BANKS[h]][:, :], vecs[:, V_BG + h:V_BG + h + 1], None, ALU.add))
                stt(gt[:, h % 2, :], b_t[:, h, :], -1.0, b_t[:, h, :], ALU.mult, ALU.min).then_inc(z_abs, 1)
                dve.wait_ge(slab_done, L_Q + h + 1)
                tt(q_t[:, h, :], bank[(T_Q + h) % 4][:, :], rinv_b[:, :], ALU.mult).then_inc(tile_taken, 1)
            for h in (2, 3):
                dve.wait_ge(g_soft, h + 1)
                link(stt(gt[:, h % 2, :], b_t[:, h, :], 0.0, gt[:, h % 2, :], ALU.min, ALU.subtract))
                dve.tensor_tensor_scan(b_t[:, h, :], t2[:, 1, :], gt[:, h % 2, :], 0.0, ALU.mult, ALU.add).then_inc(g_cum, 1)
            dve.wait_ge(g_cum, GH)
            for h in range(GH):
                chunks = b_t[:, h, :].rearrange("p (c n) -> p c n", n=CHUNK)
                tt(d_t[:, h, :].rearrange("p (c n) -> p c n", n=CHUNK), chunks[:, :, CHUNK - 1:CHUNK].to_broadcast([P, NCH, CHUNK]),
                   chunks, ALU.subtract).then_inc(g_diff, 1)
            for h in range(GH):
                dve.wait_ge(slab_done, L_K + h + 1)
                tt(k_ring[:, h % 2, :], bank[(T_K + h) % 4][:, :], rinv_b[:, :], ALU.mult).then_inc(tile_taken, 1)
                dve.wait_ge(g_up, h + 1)
                stt(q_t[:, h, :], q_t[:, h, :], HK ** -0.5, e_ring[:, h % 2, :], ALU.mult, ALU.mult)
                dve.wait_ge(tile_taken, T_K + h + 1)
                dve.wait_ge(g_down, h + 1)
                tt(b_t[:, h, :], b_t[:, h, :], k_ring[:, h % 2, :], ALU.mult)
                dve.wait_ge(g_end, h + 1)
                tt(d_t[:, h, :], d_t[:, h, :], k_ring[:, h % 2, :], ALU.mult).then_inc(g_prep, 1)

            n_ang = NT * HALF
            ang, high, low = t2[:, 0, 0:n_ang], t2[:, 0, n_ang:2 * n_ang], t2[:, 0, 2 * n_ang:3 * n_ang]
            prods = t1[:, :, :].rearrange("p a n -> p (a n)")[:, 0:10 * n_ang]
            whole = sq[:, :, :].rearrange("p a n -> p (a n)")[:, 0:10 * n_ang]
            for t in range(NT):
                last = ts(t2[:, 0, t * HALF:(t + 1) * HALF], inv_freq[:, :], vecs[:, NVEC + t:NVEC + t + 1], None, ALU.mult)
            link(last)
            link(dve.tensor_single_scalar(high.bitcast(I32), ang.bitcast(I32), -4096, op=ALU.bitwise_and))
            link(tt(low, ang, high, ALU.subtract))
            for j, part in enumerate(TURN):
                ts(prods[:, 2 * j * n_ang:(2 * j + 1) * n_ang], high, part, None, ALU.mult)
                last = ts(prods[:, (2 * j + 1) * n_ang:(2 * j + 2) * n_ang], low, part, None, ALU.mult)
            link(last)

            def drop_whole(numbers, space):
                link(ts(space, numbers, MAGIC, MAGIC, ALU.add, ALU.subtract))
                link(tt(numbers, numbers, space, ALU.subtract))

            for _ in range(2):
                drop_whole(prods, whole)
            link(dve.tensor_reduce(ang, prods.rearrange("p (j n) -> p n j", j=10), AX_X, ALU.add))
            both = t1[:, 0, 0:2 * n_ang]
            link(ts(both[:, 0:n_ang], ang, 0.25, None, ALU.add))
            link(dve.tensor_copy(both[:, n_ang:2 * n_ang], ang))
            drop_whole(both, whole[:, 0:2 * n_ang])
            ts(both, both, 0.4999999, -0.4999999, ALU.min, ALU.max).then_inc(turns, 1)

            for c in range(2):
                for t in range(NT):
                    if t < NT - 1:
                        dve.wait_ge(v_ps, (NT - 1) * c + t + 1)
                    else:
                        dve.wait_ge(slab_done, L_V + 4 * c + 4)
                    ts(v_g[:, t, c * S:(c + 1) * S], bank[(T_V + t) % 4][:, :], r_nat[:, 0, t:t + 1], None, ALU.mult)\
                        .then_inc(tile_taken, 1)

            def o_final(h):
                dve.wait_ge(o_gated, h + 1)
                for e in range(2):
                    m = 2 * h + e
                    stt(sr[:, m, :], sr[:, m, :], vecs[:, V_AO + e:V_AO + e + 1], rinvo_b[:, :], ALU.mult, ALU.mult).then_inc(o_fin, 1)

            def o_split(h):
                for e in range(2):
                    m = 2 * h + e
                    dve.wait_ge(o_hi, m + 1)
                    tt(a_l[:, m, :], sr[:, m, :], a_h[:, m, :].bitcast(F32), ALU.subtract).then_inc(o_lo, 1)

            def scale_r(m):
                dve.wait_ge(slab_done, L_R + m + 1)
                at_least(dve, r_silu, m - 1)
                tt(t1[:, m % 2, :], bank[(T_R + m) % 4][:, :], rinv_b[:, :], ALU.mult).then_inc(tile_taken, 1)

            def states(h, chunks):
                dve.wait_ge(chunk_ps, (NCH - 1) * h + chunks[-1] + 1)
                for c in chunks:
                    kv = bank[KV_BANKS[c % 2]][:, c // 2 % 2 * HV:(c // 2 % 2 + 1) * HV]
                    if c == 0:
                        dve.tensor_copy(state[:, 1, :], kv).then_inc(state_sb, 1)
                    else:
                        dve.wait_ge(state_sb, (NCH - 1) * h + c)
                        stt(state[:, c + 1, :], state[:, c, :], dec[:, h, c:c + 1], kv, ALU.mult, ALU.add).then_inc(state_sb, 1)

            def sum_squares(h):
                dve.wait_ge(o_sq, 2 * h + 2)
                at_least(dve, stat_ps, h)
                tt(acc[:, :], sq[:, 0, :], sq[:, 1, :], ALU.add).then_inc(o_acc, 1)

            def gated(h):
                dve.wait_ge(o_sq, 2 * h + 2)
                dve.wait_ge(r_silu, 2 * h + 2)
                for e in range(2):
                    m = 2 * h + e
                    last = tt(sr[:, m, :], sr[:, m, :], bank[O_BANKS[e]][:, :], ALU.mult)
                last.then_inc(o_gated, 1)

            for h in range(GH):
                if h:
                    sum_squares(h - 1)
                    gated(h - 1)
                dve.wait_ge(att_ps, h + 1)
                at_least(dve, o_ps, h)
                dve.copy_predicated(att[:, :, :], mask[:, :].bitcast(I32).rearrange("p (a n) -> p a n", a=1).to_broadcast([P, NT, P]),
                                    bank[KV_BANKS[1]][:, :].rearrange("p (t n) -> p t n", n=P)).then_inc(att_sb, 1)
                if h:
                    norm(h, 3, h, HV, O_BANKS[0])
                else:
                    dve.wait_ge(trig_done, 1)
                states(h, range(0, 4))
                scale_r(2 * h)
                if h:
                    dve.wait_ge(spread_sb, h + 1)
                    o_final(h - 1)
                states(h, range(4, NCH - 1))
                if h < GH - 1:
                    scale_r(2 * h + 1)
            o_split(0)
            o_split(1)
            sum_squares(GH - 1)
            o_split(2)
            scale_r(KT - 1)
            norm(GH, 3, GH, HV)
            gated(GH - 1)
            dve.wait_ge(spread_sb, GH + 1)
            o_final(GH - 1)
            o_split(GH - 1)

            def project_out(n, tile, n_x, gain):
                for m in range(KT):
                    dve.wait_ge(slab_done, n + m + 1)
                    tt(x_t[:, m, :], x_t[:, m, :], bank[(tile + m) % 4][:, :], ALU.add).then_inc(tile_taken, 1)
                    x_tile(m, n_x, gain, b_h, b_l)

            project_out(L_WO, T_WO, KT, V_F)

            def ffn_up(n, tile, hidden):
                with dve.Fori(0, FT // 2) as i:
                    for c in range(2):
                        m = hidden + 2 * i + c
                        dve.wait_ge(slab_done, n + 4 * i + 2 * c + 1)
                        tt(t1[:, c, :], bank[(tile + 2 * c) % 4][:, :], rinv_b[:, :], ALU.mult).then_inc(tile_taken, 1)
                        dve.wait_ge(slab_done, n + 4 * i + 2 * c + 2)
                        tt(t2[:, c, :], bank[(tile + 2 * c + 1) % 4][:, :], rinv_b[:, :], ALU.mult).then_inc(tile_taken, 1)
                        dve.wait_ge(tile_taken, tile + 4 * i + 2 * c + 2)
                        dve.wait_ge(f_silu, m + 1)
                        tt(t2[:, c, :], t2[:, c, :], t1[:, c, :], ALU.mult).then_inc(f_prod, 1)
                        dve.wait_ge(f_hi, m + 1)
                        tt(hid_l[:, bass.ts(2 * i + c, 1), :], t2[:, c:c + 1, :], hid_h[:, bass.ts(2 * i + c, 1), :].bitcast(F32),
                           ALU.subtract).then_inc(f_lo, 1)

            def ffn_down(n, tile, n_x, gain):
                for m in range(KT):
                    dve.wait_ge(slab_done, n + 4 * m + 4)
                    ps = bank[(tile + m) % 4][:, :]
                    if gain is not None:
                        tt(x_t[:, m, :], x_t[:, m, :], ps, ALU.add).then_inc(tile_taken, 1)
                        x_tile(m, n_x, gain, b_h, b_l)
                    else:
                        if m == 0:
                            dve.wait_ge(f_hi, 2 * FT)
                        at_least(dve, y_ps, m - 1)
                        tt(t2[:, m % 2, :], x_t[:, m, :], ps, ALU.add).then_inc(tile_taken, 1)

            dve.wait_ge(x_acc, KT)
            norm(5, 0, 5)
            dve.wait_ge(spread_sb, 6)
            ffn_up(L_UP1, T_UP1, 0)
            ffn_down(L_DN1, T_DN1, 2 * KT, V_B)

            for m in range(KT):
                dve.wait_ge(xb_hi, m + 1)
                stt(a_l[:, m, :], x_t[:, m, :], vecs[:, V_KV + m:V_KV + m + 1], a_h[:, m, :].bitcast(F32),
                    ALU.mult, ALU.subtract).then_inc(xb_lo, 1)
            norm(6, 0, 6)
            for j, (kind, g_half, f) in enumerate([(kind, a, f) for kind in range(2) for a, f in ((0, 0), (1, 1), (0, 1), (1, 0))]):
                gains = rope_g[:, kind:kind + 1, g_half * HALF:(g_half + 1) * HALF].to_broadcast([P, NT, HALF])
                last = tt(rope_c[:, j, :, :], trig[:, f, :, :], gains, ALU.mult)
            link(last)
            dve.wait_ge(spread_sb, 7)

            def latent(j, gain, split_h, split_l, m):
                tile = T_CQ + j
                dve.wait_ge(slab_done, (L_C1 if j == QT + 1 else L_CQ + j) + 1)
                at_least(dve, c_sq, j - 1)
                tt(t1[:, j % 2, :], bank[tile % 4][:, :], rinv_b[:, :], ALU.mult).then_inc(tile_taken, 1)
                dve.wait_ge(tile_taken, tile + 1)
                dve.wait_ge(c_hi, j + 1)
                stt(split_l[:, m, :], t1[:, j % 2, :], vecs[:, gain + m:gain + m + 1], split_h[:, m, :].bitcast(F32),
                    ALU.mult, ALU.subtract).then_inc(c_lo, 1)
                dve.wait_ge(c_sq, j + 1)
                if m == 0:
                    if j:
                        dve.wait_ge(stat_ps, 7)
                    dve.tensor_copy(acc[:, :], sq[:, j % 2, :]).then_inc(c_acc, 1)
                else:
                    dve.wait_ge(c_acc, j)
                    tt(acc[:, :], acc[:, :], sq[:, j % 2, :], ALU.add).then_inc(c_acc, 1)

            for j in range(QT):
                latent(j, V_QL, cq_h, cq_l, j)
            def query_sums(t, gi):
                dve.wait_ge(qsq, NT * gi + t + 1)
                dve.tensor_reduce(q_scale[:, HG * t:HG * (t + 1)], sq_g[:, HG * t:HG * (t + 1), :], AX_X, ALU.add).then_inc(q_sum, 1)

            def query_factors(part, gi):
                if part == 0:
                    dve.wait_ge(q_sum, NT * gi + NT)
                    if isinstance(gi, int) and gi == 0:
                        dve.wait_ge(stat_nat, 1)
                    else:
                        dve.wait_ge(k_fac, gi)
                    guess(q_scale[:, :], 1.0, QK * EPS, UNITS)
                    newton(UNITS)
                else:
                    newton(UNITS)
                    newton(UNITS, q_scale[:, :]).then_inc(q_fac, 1)

            norm(7, 2, None, QRANK)
            latent(QT, V_CL, c_h, c_l, 0)
            dve.wait_ge(mask_rows, 1)
            by_tile = ident[QK:QK + NT, QK:QK + NT].rearrange("p (t a) -> p t a", a=1).to_broadcast([NT, NT, CHUNK])
            for h in range(HG):
                queries, keys = (w[QK:QK + NT, h, :].rearrange("p (t c n) -> p t c n", c=2, n=CHUNK) for w in (q_tt, k_tt))
                dve.tensor_copy(queries[:, :, 0, :], by_tile)
                last = ts(keys[:, :, 1, :], by_tile, NEG, None, ALU.mult)
            last.then_inc(mask_rows, 1)
            for t in range(NT):
                query_sums(t, 0)
            query_factors(0, 0)
            latent(QT + 1, V_CL, c_h, c_l, 1)
            query_factors(1, 0)
            dve.wait_ge(slab_done, L_KR + 1)
            tt(t1[P - ROPE:P, 1, :], bank[T_KR % 4][P - ROPE:P, :], rinv_b[P - ROPE:P, :], ALU.mult).then_inc(tile_taken, 1)
            dve.wait_ge(q_fac, 1)
            norm(8, 1, None, KVRANK)
            dve.wait_ge(kr_ps, 1)
            dve.tensor_copy(kr[:, 0, :, :], bank[T_KRT % 4][:, 0:NT * ROPE].rearrange("p (t n) -> p t n", n=ROPE)).then_inc(tile_taken, 1)
            dve.wait_ge(tile_taken, T_KRT + 1)
            link(tt(kr[:, 1, :, :], kr[:, 0, :, :], kr[:, 0, :, :], ALU.mult))
            link(dve.tensor_reduce(kr_ss[:, :], kr[:, 1, :, :], AX_X, ALU.add))
            space = [kr[:, 2 + j // 2, :, (j % 2) * HALF:(j % 2 + 1) * HALF] for j in range(4)]
            x1, x2 = kr[:, 0, :, 0:HALF], kr[:, 0, :, HALF:ROPE]
            for j, x_half in enumerate((x1, x2, x1, x2)):
                last = tt(space[j], x_half, rope_c[:, 4 + j, :, :], ALU.mult)
            link(last)
            tt(kr[:, 1, :, 0:HALF], space[0], space[1], ALU.subtract)
            link(tt(kr[:, 1, :, HALF:ROPE], space[2], space[3], ALU.add))


            def key_sums(t, gi):
                dve.wait_ge(ksq, NT * gi + t + 1)
                dve.tensor_reduce(k_scale[:, HG * t:HG * (t + 1)], sq_g[:, HG * t:HG * (t + 1), 0:NOPE], AX_X, ALU.add).then_inc(k_sum, 1)

            def key_factors(part, gi):
                if part == 0:
                    dve.wait_ge(k_sum, NT * gi + NT)
                    by_token = k_scale[:, :].rearrange("p (t h) -> p t h", h=HG)
                    link(tt(by_token, by_token, kr_ss[:, :].rearrange("p (t a) -> p t a", a=1).to_broadcast([P, NT, HG]), ALU.add))
                    if isinstance(gi, int) and gi == 0:
                        dve.wait_ge(stat_nat, 2)
                    else:
                        dve.wait_ge(q_fac, gi + 1)
                    guess(k_scale[:, :], QK, EPS, UNITS)
                elif part < 3:
                    newton(UNITS)
                else:
                    newton(UNITS, k_scale[:, :]).then_inc(k_fac, 1)

            def bias(v, gi):
                t = v % NT
                col = v % UNITS
                dve.wait_ge(s_ps, 16 * gi + v + 1)
                dve.tensor_reduce(stat[:, 0, col:col + 1], bank[t][:, 0:(t + 1) * P], AX_X, ALU.max, negate=True).then_inc(s_bias, 1)

            def turned(u, gi):
                if u % 2:
                    dve.wait_ge(pt_ps, 16 * gi + u + 1)
                    at_least(dve, pv_ps, 16 * gi + u - 1)
                    w = (u % NT + 1) * P
                    dve.tensor_copy(prob_t[:, 1, 0:w], bank[PT_BANK][:, 0:w]).then_inc(pt_sb[1], 1)

            def head_out(h, gi):
                dve.wait_ge(pv_ps, 16 * gi + NT * (h + 1))
                cols = slice(NT * h, NT * (h + 1))
                link(dve.reciprocal(stat[:, 2, cols], stat[:, 1, cols]))
                if h % 2 == 0:
                    at_least(dve, ot_ps, 2 * gi + h // 2)
                tt(o_n[:, :, (h % 2) * MV:(h % 2 + 1) * MV], bank[PV_BANKS[h % 2]][:, 0:NT * MV].rearrange("p (t n) -> p t n", n=MV),
                   stat[:, 2, cols].rearrange("p (t a) -> p t a", a=1).to_broadcast([P, NT, MV]), ALU.mult).then_inc(o_nat, 1)

            def outputs(pair, gi):
                dve.wait_ge(ot_hi, 2 * gi + pair + 1)
                m = 2 * gi + pair
                cut = slice(m, m + 1) if isinstance(gi, int) else bass.ts(m, 1)
                tt(a_l[:, cut, :], bank[PV_BANKS[1]][:, :].rearrange("p (a n) -> p a n", a=1), a_h[:, cut, :].bitcast(F32),
                   ALU.subtract).then_inc(ot_lo, 1)

            def take_values(h, gi):
                at_least(dve, pv_ps, 16 * (gi - 1) + NT * (h + 1))
                dve.wait_ge(piece_taken, 16 * gi + 2 * NT)
                dve.tensor_copy(v_cur[:, :, h, :], kv_n[:, :, h * P + NOPE:(h + 1) * P]).then_inc(v_ready, 1)

            def beside(u, gi):
                if 1 <= u <= NT:
                    query_sums(u - 1, gi + 1)
                if u in (5, 6):
                    query_factors(u - 5, gi + 1)
                if NT < u <= 2 * NT:
                    key_sums(u - NT - 1, gi + 1)
                for part in {8: (0,), 9: (1, 2), 10: (3,)}.get(u, ()):
                    key_factors(part, gi + 1)

            BESIDE_LINKS = (2 + 8) + (1 + 2 + 8)

            def group(gi, first, more):
                for u in range(UNITS):
                    turned(u, gi)
                    if u + AHEAD < UNITS or more:
                        bias(u + AHEAD, gi)
                    if u % NT == 1 and not (first and u == 1):
                        head_out((u // NT - 1) % HG, gi if u > 1 else gi - 1)
                    if u == 1 and not first:
                        take_values(3, gi)
                    if u == 3 and not first:
                        outputs(1, gi - 1)
                    if u == 11:
                        outputs(0, gi)
                    if more:
                        beside(u, gi)
                        for h in {12: (0,), 14: (1, 2)}.get(u, ()):
                            take_values(h, gi + 1)

            for t in range(NT):
                key_sums(t, 0)
            for part in range(4):
                key_factors(part, 0)
            for v in range(AHEAD):
                bias(v, 0)
            for h in range(HG):
                take_values(h, 0)
            group(0, True, True)
            with dve.Fori(1, GROUPS - 1) as g:
                link.enter(g, HG + BESIDE_LINKS, 1)
                group(g, False, True)
            link.leave(GROUPS - 2)
            group(GROUPS - 1, False, False)
            head_out(HG - 1, GROUPS - 1)
            outputs(1, GROUPS - 1)

            project_out(L_WOB, T_WOB, 3 * KT, V_F + KT)
            norm(9, 0, 7)
            dve.wait_ge(spread_sb, 8)
            ffn_up(L_UP2, T_UP2, FT)
            ffn_down(L_DN2, T_DN2, 0, None)


_INS = ['x', 'positions', 'a_norm', 'a_w_in', 'a_w_gate_up', 'a_b_gate', 'a_out_norm', 'a_w_out',
        'b_norm', 'b_w_dq', 'b_q_latent_norm', 'b_w_uq', 'b_q_norm', 'b_w_out',
        'kv_norm', 'kv_w_down', 'kv_latent_norm', 'kv_w_up', 'k_norm', 'f_norm', 'f_w_in', 'f_w_out']
_OUTS = [((1, S, D), 'float32')]


def kernel(**inputs):
    import numpy as _np
    import concourse.bacc as _bacc
    from concourse import mybir as _mybir
    from concourse.bass_utils import run_bass_kernel_spmd as _run

    nc = _bacc.Bacc("TRN2", target_bir_lowering=False, num_devices=1)
    arrays, args = {}, []
    for name in _INS:
        a = _np.ascontiguousarray(inputs[name])
        arrays[f"in_{name}_dram"] = a
        args.append(nc.dram_tensor(f"in_{name}_dram", a.shape, _mybir.dt.from_np(a.dtype), kind="ExternalInput").ap())
    for i, (shape, dtype) in enumerate(_OUTS):
        dt = _mybir.dt.from_np(_np.dtype(dtype))
        args.append(nc.dram_tensor(f"out_{i}_dram", shape, dt, kind="ExternalOutput").ap())
    trunk(nc, *args)
    r = _run(nc, [arrays], core_ids=[0])
    return r.results[0]["out_0_dram"]
```
